# Optimizing a Trainium2 kernel written in Bass

```python
import jax, jax.numpy as jnp
from jax import lax
import numpy as np

D_MODEL = 1024
BATCH = 1
SEQ = 256
DEPTH = 2

CTX_LEN = 256
GRID_W = 64

F_GROUPS = 4
F_GROUP_DIM = D_MODEL // 16
F_WIDTH = F_GROUPS * F_GROUP_DIM
G_HEADS = 4
G_HEAD_DIM = D_MODEL // 16
G_WIDTH = G_HEADS * G_HEAD_DIM
CHUNK = 128
A_HEADS = 8
A_NOPE = D_MODEL // 16
A_ROPE = D_MODEL // 32
A_V = D_MODEL // 16
A_QK = A_NOPE + A_ROPE
A_WIDTH = A_HEADS * A_V
Q_LORA = D_MODEL // 4
KV_LORA = D_MODEL // 8

MIX_WIDTH = F_WIDTH + G_WIDTH + A_WIDTH
IN_WIDTH = 2 * F_WIDTH + 3 * G_WIDTH + Q_LORA + KV_LORA + A_ROPE + A_WIDTH
ROPE_BASE = 10000.0
EPS = 1e-6
Q_BLOCK = 128


def _rmsnorm(t, g):
    tf = t.astype(jnp.float32)
    tf = tf * lax.rsqrt(jnp.mean(tf * tf, axis=-1, keepdims=True) + EPS)
    return (tf * g.astype(jnp.float32)).astype(t.dtype)

def _layernorm(t, g):
    tf = t.astype(jnp.float32)
    tf = tf - jnp.mean(tf, axis=-1, keepdims=True)
    tf = tf * lax.rsqrt(jnp.mean(tf * tf, axis=-1, keepdims=True) + EPS)
    return (tf * g.astype(jnp.float32)).astype(t.dtype)

def _split_in(p):
    sizes = (F_WIDTH, F_WIDTH, G_WIDTH, G_WIDTH, G_WIDTH, Q_LORA, KV_LORA, A_ROPE, A_WIDTH)
    parts = []
    start = 0
    for s in sizes:
        parts.append(p[..., start:start + s])
        start += s
    return parts

def _axial_rope(n):
    rows = n // GRID_W
    row = jnp.repeat(jnp.arange(rows, dtype=jnp.float32), GRID_W)
    col = jnp.tile(jnp.arange(GRID_W, dtype=jnp.float32), rows)
    half = A_ROPE // 2
    inv = ROPE_BASE ** (-jnp.arange(0, half, 2, dtype=jnp.float32) / half)
    ang_r = row[:, None] * inv[None, :]
    ang_c = col[:, None] * inv[None, :]
    ang = jnp.concatenate([ang_r, ang_r, ang_c, ang_c], axis=-1)
    return jnp.cos(ang), jnp.sin(ang)

def _apply_rope(t, rope):
    cos, sin = rope
    q = A_ROPE // 4
    x1, x2, x3, x4 = t[..., :q], t[..., q:2 * q], t[..., 2 * q:3 * q], t[..., 3 * q:]
    rot = jnp.concatenate([-x2, x1, -x4, x3], axis=-1)
    cos = cos[:, None, :].astype(t.dtype)
    sin = sin[:, None, :].astype(t.dtype)
    return t * cos + rot * sin

def _fourier(u):
    b, n, _ = u.shape
    ug = u.astype(jnp.float32).reshape(b, n, F_GROUPS, F_GROUP_DIM).transpose(0, 2, 1, 3)
    f = jnp.fft.fft2(ug, norm="ortho").real
    return f.transpose(0, 2, 1, 3).reshape(b, n, F_WIDTH).astype(u.dtype)

def _spatial_gate(u, v, ln_g, ws, bs):
    b, n, _ = v.shape
    vh = v.reshape(b, n // CHUNK, CHUNK, G_HEADS, G_HEAD_DIM)
    vh = _layernorm(vh, ln_g)
    mixed = jnp.einsum('hpq,bcqhd->bcphd', ws, vh) + bs.T[None, None, :, :, None]
    return u * mixed.reshape(b, n, G_WIDTH)

def _mla_qkv(c_q, c_kv, k_rope, q_a_g, w_uq, kv_a_g, w_ukv, q_norm_g, k_norm_g, rope):
    b, n, _ = c_q.shape
    q = (_rmsnorm(c_q, q_a_g) @ w_uq).reshape(b, n, A_HEADS, A_QK)
    kv = (_rmsnorm(c_kv, kv_a_g) @ w_ukv).reshape(b, n, A_HEADS, A_NOPE + A_V)
    k_nope, v = kv[..., :A_NOPE], kv[..., A_NOPE:]
    k_r = jnp.broadcast_to(k_rope[:, :, None, :], (b, n, A_HEADS, A_ROPE))
    k = jnp.concatenate([k_nope, k_r], axis=-1)
    q = _rmsnorm(q, q_norm_g)
    k = _rmsnorm(k, k_norm_g)
    if rope is not None:
        q = jnp.concatenate([q[..., :A_NOPE], _apply_rope(q[..., A_NOPE:], rope)], axis=-1)
        k = jnp.concatenate([k[..., :A_NOPE], _apply_rope(k[..., A_NOPE:], rope)], axis=-1)
    return q, k, v

def _branches(h, w_in, w_fmix, g_ln_g, g_ws, g_bs, q_a_g, w_uq, kv_a_g, w_ukv, q_norm_g, k_norm_g, rope):
    f_in, f_gate, g_u, g_v, g_gate, c_q, c_kv, k_rope, a_gate = _split_in(h @ w_in)
    f_out = (_fourier(f_in) @ w_fmix) * jax.nn.silu(f_gate)
    g_out = _spatial_gate(g_u, g_v, g_ln_g, g_ws, g_bs) * jax.nn.silu(g_gate)
    q, k, v = _mla_qkv(c_q, c_kv, k_rope, q_a_g, w_uq, kv_a_g, w_ukv, q_norm_g, k_norm_g, rope)
    return f_out, g_out, q, k, v, a_gate

def _attend(q, k, v):
    s = jnp.einsum('bqhd,bkhd->bhqk', q, k).astype(jnp.float32) * (A_QK ** -0.5)
    p = jax.nn.softmax(s, axis=-1).astype(v.dtype)
    return jnp.einsum('bhqk,bkhd->bqhd', p, v)

def _blocked_attention(q, k, v):
    b, n, h, d = q.shape
    nb = n // Q_BLOCK
    qb = q.reshape(b, nb, Q_BLOCK, h, d).transpose(1, 0, 2, 3, 4)
    o = lax.map(lambda blk: _attend(blk, k, v), qb)
    return o.transpose(1, 0, 2, 3, 4).reshape(b, n, h * A_V)

def first_inputs(seed: int = 0) -> dict:
    key = jax.random.key(seed)
    ks = jax.random.split(key, 24)
    f32 = jnp.float32
    nrm = lambda k, shape, s: jax.random.normal(k, shape, f32) * s
    gain = lambda k, shape: 1.0 + 0.02 * jax.random.normal(k, shape, f32)
    return {
        "x": nrm(ks[0], (BATCH, SEQ, D_MODEL), 1.0),
        "c": nrm(ks[1], (BATCH, D_MODEL), 1.0),
        "ctx": nrm(ks[2], (BATCH, CTX_LEN, D_MODEL), 1.0),
        "c_ctx": nrm(ks[3], (D_MODEL,), 1.0),
        "w_mod": nrm(ks[4], (DEPTH, D_MODEL, 3 * D_MODEL), 0.5 * D_MODEL ** -0.5),
        "b_mod": nrm(ks[5], (DEPTH, 3 * D_MODEL), 0.01),
        "norm_g": gain(ks[6], (DEPTH, D_MODEL)),
        "w_in": nrm(ks[7], (DEPTH, D_MODEL, IN_WIDTH), D_MODEL ** -0.5),
        "w_fmix": nrm(ks[8], (DEPTH, F_WIDTH, F_WIDTH), F_WIDTH ** -0.5),
        "g_ln_g": gain(ks[9], (DEPTH, G_HEAD_DIM)),
        "g_ws": nrm(ks[10], (DEPTH, G_HEADS, CHUNK, CHUNK), CHUNK ** -0.5),
        "g_bs": 1.0 + nrm(ks[11], (DEPTH, G_HEADS, CHUNK), 0.01),
        "q_a_g": gain(ks[12], (DEPTH, Q_LORA)),
        "w_uq": nrm(ks[13], (DEPTH, Q_LORA, A_HEADS * A_QK), Q_LORA ** -0.5),
        "kv_a_g": gain(ks[14], (DEPTH, KV_LORA)),
        "w_ukv": nrm(ks[15], (DEPTH, KV_LORA, A_HEADS * (A_NOPE + A_V)), KV_LORA ** -0.5),
        "q_norm_g": gain(ks[16], (DEPTH, A_QK)),
        "k_norm_g": gain(ks[17], (DEPTH, A_QK)),
        "w_out": nrm(ks[18], (DEPTH, MIX_WIDTH, D_MODEL), MIX_WIDTH ** -0.5),
    }

def first_block(x, c, ctx, c_ctx, w_mod, b_mod, norm_g, w_in, w_fmix, g_ln_g, g_ws, g_bs,
              q_a_g, w_uq, kv_a_g, w_ukv, q_norm_g, k_norm_g, w_out):
    n = x.shape[1]
    rope = _axial_rope(n)
    y = ctx
    silu_c = jax.nn.silu(c)
    silu_cc = jax.nn.silu(c_ctx)
    for l in range(DEPTH):
        shift, scale, gate = jnp.split(silu_c @ w_mod[l] + b_mod[l], 3, axis=-1)
        shift_c, scale_c, gate_c = jnp.split(silu_cc @ w_mod[l] + b_mod[l], 3, axis=-1)
        hx = _rmsnorm(x, norm_g[l]) * (1.0 + scale[:, None, :]) + shift[:, None, :]
        hy = _rmsnorm(y, norm_g[l]) * (1.0 + scale_c) + shift_c
        params = (w_in[l], w_fmix[l], g_ln_g[l], g_ws[l], g_bs[l], q_a_g[l], w_uq[l],
                  kv_a_g[l], w_ukv[l], q_norm_g[l], k_norm_g[l])
        fy, gy, qy, ky, vy, ay = _branches(hy, *params, None)
        fx, gx, qx, kx, vx, ax = _branches(hx, *params, rope)
        k_all = jnp.concatenate([ky, kx], axis=1)
        v_all = jnp.concatenate([vy, vx], axis=1)
        ox = _blocked_attention(qx, k_all, v_all) * jax.nn.silu(ax)
        x = x + gate[:, None, :] * (jnp.concatenate([fx, gx, ox], axis=-1) @ w_out[l])
        if l < DEPTH - 1:
            b = y.shape[0]
            oy = _attend(qy, ky, vy).reshape(b, y.shape[1], A_WIDTH) * jax.nn.silu(ay)
            y = y + gate_c * (jnp.concatenate([fy, gy, oy], axis=-1) @ w_out[l])
    return x


DEPTH_2 = 1

HEAD_DIM = 64
N_HEADS = 8
DILATED_GROUPS = ((128, 1), (512, 4), (2048, 16))
N_GROUPS = len(DILATED_GROUPS)
ATTN_WIDTH = N_HEADS * HEAD_DIM
CONV_CHANNELS = 512
CONV_WIDTH = 31
D_FF = -(-8 * D_MODEL // (3 * 256)) * 256
ROPE_THETA = 10000.0
BLOCK = 128
LN_EPS = 1e-5
QKV_COLS = N_GROUPS * 3 * ATTN_WIDTH
IN_COLS = QKV_COLS + 2 * CONV_CHANNELS + 2 * D_MODEL


def layer_norm(x, g, b):
    xf = x.astype(jnp.float32)
    mu = jnp.mean(xf, axis=-1, keepdims=True)
    var = jnp.mean(jnp.square(xf - mu), axis=-1, keepdims=True)
    y = (xf - mu) * lax.rsqrt(var + LN_EPS)
    return (y * g.astype(jnp.float32) + b.astype(jnp.float32)).astype(x.dtype)

def rotary_tables(seq_len):
    inv_freq = 1.0 / (ROPE_THETA ** (jnp.arange(0, HEAD_DIM, 2, dtype=jnp.float32) / HEAD_DIM))
    ang = jnp.arange(seq_len, dtype=jnp.float32)[:, None] * inv_freq[None, :]
    return jnp.cos(ang)[:, None, :], jnp.sin(ang)[:, None, :]

def apply_rotary(x, cos, sin):
    xf = x.astype(jnp.float32)
    x1, x2 = jnp.split(xf, 2, axis=-1)
    return jnp.concatenate([x1 * cos - x2 * sin, x2 * cos + x1 * sin], axis=-1).astype(x.dtype)

def dilated_window_attention(q, k, v, window, dilation):
    B, S, H, Dh = q.shape
    n_keys = window // dilation
    L = S // dilation
    n_blk = -(-L // BLOCK)
    Lp = n_blk * BLOCK

    def by_residue(a):
        return a.reshape(B, L, dilation, H, Dh).transpose(0, 2, 1, 3, 4)

    qb = jnp.pad(by_residue(q), ((0, 0), (0, 0), (0, Lp - L), (0, 0), (0, 0)))
    qb = qb.reshape(B, dilation, n_blk, BLOCK, H, Dh)
    pad_k = ((0, 0), (0, 0), (BLOCK, Lp - L), (0, 0), (0, 0))
    kp = jnp.pad(by_residue(k), pad_k)
    vp = jnp.pad(by_residue(v), pad_k)

    def band(a):
        prev = a[:, :, :Lp].reshape(B, dilation, n_blk, BLOCK, H, Dh)
        cur = a[:, :, BLOCK:].reshape(B, dilation, n_blk, BLOCK, H, Dh)
        return jnp.concatenate([prev, cur], axis=3)

    kb, vb = band(kp), band(vp)
    s = jnp.einsum('brnqhd,brnkhd->brnhqk', qb, kb,
                   preferred_element_type=jnp.float32) * (Dh ** -0.5)
    iq = jnp.arange(BLOCK)[:, None]
    ik = jnp.arange(2 * BLOCK)[None, :]
    dist = iq + BLOCK - ik
    k_pos = jnp.arange(n_blk)[:, None, None] * BLOCK - BLOCK + ik[None]
    mask = (dist >= 0) & (dist <= n_keys) & (k_pos >= 0)
    s = jnp.where(mask[None, None, :, None], s, -jnp.inf)
    m = jnp.max(s, axis=-1, keepdims=True)
    p = jnp.exp(s - m)
    den = jnp.sum(p, axis=-1, keepdims=True)
    o = jnp.einsum('brnhqk,brnkhd->brnqhd', p, vb.astype(jnp.float32))
    o = o / den.transpose(0, 1, 2, 4, 3, 5)
    lse = (m + jnp.log(den))[..., 0].transpose(0, 1, 2, 4, 3)
    o = o.reshape(B, dilation, Lp, H, Dh)[:, :, :L].transpose(0, 2, 1, 3, 4).reshape(B, S, H, Dh)
    lse = lse.reshape(B, dilation, Lp, H)[:, :, :L].transpose(0, 2, 1, 3).reshape(B, S, H)
    return o, lse

def hybrid_mixer(x, w_in, conv_w, conv_b, conv_ln_g, conv_ln_b, w_attn_out, w_conv_out, w_o):
    B, S, _ = x.shape
    h = x @ w_in
    qkv = h[..., :QKV_COLS].reshape(B, S, N_GROUPS, 3, N_HEADS, HEAD_DIM)
    conv_in = h[..., QKV_COLS:QKV_COLS + 2 * CONV_CHANNELS]
    gates = jax.nn.sigmoid(h[..., QKV_COLS + 2 * CONV_CHANNELS:].astype(jnp.float32)).astype(x.dtype)
    g_attn, g_conv = jnp.split(gates, 2, axis=-1)

    cos, sin = rotary_tables(S)
    outs, lses = [], []
    for g, (window, dilation) in enumerate(DILATED_GROUPS):
        q = apply_rotary(qkv[:, :, g, 0], cos, sin)
        k = apply_rotary(qkv[:, :, g, 1], cos, sin)
        o, lse = dilated_window_attention(q, k, qkv[:, :, g, 2], window, dilation)
        outs.append(o)
        lses.append(lse)
    wts = jax.nn.softmax(jnp.stack(lses, axis=0), axis=0)
    o = jnp.sum(wts[..., None] * jnp.stack(outs, axis=0), axis=0).astype(x.dtype)
    y_attn = o.reshape(B, S, ATTN_WIDTH) @ w_attn_out

    a, b = jnp.split(conv_in, 2, axis=-1)
    u = a * jax.nn.sigmoid(b)
    u = lax.conv_general_dilated(u, conv_w[:, None, :].astype(u.dtype), window_strides=(1,),
                                 padding=[(CONV_WIDTH - 1, 0)],
                                 dimension_numbers=('NWC', 'WIO', 'NWC'),
                                 feature_group_count=CONV_CHANNELS) + conv_b
    u = jax.nn.silu(layer_norm(u, conv_ln_g, conv_ln_b))
    y_conv = u @ w_conv_out

    merged = g_attn * y_attn + g_conv * y_conv
    return merged @ w_o

def swiglu_ffn(x, w_gate, w_up, w_down):
    return (jax.nn.silu(x @ w_gate) * (x @ w_up)) @ w_down

def second_inputs(seed: int = 0) -> dict:
    key = jax.random.key(seed)
    ks = jax.random.split(key, 17)
    f32 = jnp.float32
    beta = (8 * DEPTH_2) ** -0.25
    nrm = lambda k, shape, scale: jax.random.normal(k, shape, f32) * scale
    return {
        "x": jax.random.normal(ks[0], (BATCH, SEQ, D_MODEL), f32),
        "w_in": nrm(ks[1], (DEPTH_2, D_MODEL, IN_COLS), D_MODEL ** -0.5),
        "conv_w": nrm(ks[2], (DEPTH_2, CONV_WIDTH, CONV_CHANNELS), CONV_WIDTH ** -0.5),
        "conv_b": nrm(ks[3], (DEPTH_2, CONV_CHANNELS), 0.02),
        "conv_ln_g": 1.0 + nrm(ks[4], (DEPTH_2, CONV_CHANNELS), 0.05),
        "conv_ln_b": nrm(ks[5], (DEPTH_2, CONV_CHANNELS), 0.02),
        "w_attn_out": nrm(ks[6], (DEPTH_2, ATTN_WIDTH, D_MODEL), ATTN_WIDTH ** -0.5),
        "w_conv_out": nrm(ks[7], (DEPTH_2, CONV_CHANNELS, D_MODEL), CONV_CHANNELS ** -0.5),
        "w_o": nrm(ks[8], (DEPTH_2, D_MODEL, D_MODEL), beta * D_MODEL ** -0.5),
        "ln1_g": 1.0 + nrm(ks[9], (DEPTH_2, D_MODEL), 0.05),
        "ln1_b": nrm(ks[10], (DEPTH_2, D_MODEL), 0.02),
        "w_ffn_gate": nrm(ks[11], (DEPTH_2, D_MODEL, D_FF), D_MODEL ** -0.5),
        "w_ffn_up": nrm(ks[12], (DEPTH_2, D_MODEL, D_FF), D_MODEL ** -0.5),
        "w_ffn_down": nrm(ks[13], (DEPTH_2, D_FF, D_MODEL), beta * D_FF ** -0.5),
        "ln2_g": 1.0 + nrm(ks[14], (DEPTH_2, D_MODEL), 0.05),
        "ln2_b": nrm(ks[15], (DEPTH_2, D_MODEL), 0.02),
    }

def second_block(x, w_in, conv_w, conv_b, conv_ln_g, conv_ln_b, w_attn_out, w_conv_out, w_o,
              ln1_g, ln1_b, w_ffn_gate, w_ffn_up, w_ffn_down, ln2_g, ln2_b):
    alpha = (2 * DEPTH_2) ** 0.25
    for l in range(DEPTH_2):
        mix = hybrid_mixer(x, w_in[l], conv_w[l], conv_b[l], conv_ln_g[l], conv_ln_b[l],
                           w_attn_out[l], w_conv_out[l], w_o[l])
        x = layer_norm(alpha * x + mix, ln1_g[l], ln1_b[l])
        ff = swiglu_ffn(x, w_ffn_gate[l], w_ffn_up[l], w_ffn_down[l])
        x = layer_norm(alpha * x + ff, ln2_g[l], ln2_b[l])
    return x


def setup_inputs(seed=0):
    out = dict(first_inputs(seed))
    for name, value in second_inputs(seed + 1).items():
        if name != "x":
            out[name + "_2"] = value
    return out


def reference(
    x, c, ctx, c_ctx, w_mod, b_mod, norm_g, w_in, w_fmix, g_ln_g, g_ws, g_bs, q_a_g, w_uq,
    kv_a_g, w_ukv, q_norm_g, k_norm_g, w_out, w_in_2, conv_w_2, conv_b_2, conv_ln_g_2,
    conv_ln_b_2, w_attn_out_2, w_conv_out_2, w_o_2, ln1_g_2, ln1_b_2, w_ffn_gate_2, w_ffn_up_2,
    w_ffn_down_2, ln2_g_2, ln2_b_2,
):
    x = first_block(
        x, c, ctx, c_ctx, w_mod, b_mod, norm_g, w_in, w_fmix, g_ln_g, g_ws, g_bs, q_a_g, w_uq,
        kv_a_g, w_ukv, q_norm_g, k_norm_g, w_out,
    )
    return second_block(
        x, w_in_2, conv_w_2, conv_b_2, conv_ln_g_2, conv_ln_b_2, w_attn_out_2, w_conv_out_2,
        w_o_2, ln1_g_2, ln1_b_2, w_ffn_gate_2, w_ffn_up_2, w_ffn_down_2, ln2_g_2, ln2_b_2,
    )


_drawn_inputs = setup_inputs


def setup_inputs(seed=0):
    import zlib

    import numpy as np

    out = dict(_drawn_inputs(seed))
    spreads = {}
    factors = {'ctx': 5.461,
     'b_mod': 5.493,
     'norm_g': 7.166,
     'g_ln_g': 8.0,
     'g_bs': 8.0,
     'q_a_g': 8.0,
     'w_uq': 2.822,
     'kv_a_g': 8.0,
     'q_norm_g': 8.0,
     'k_norm_g': 8.0,
     'conv_b_2': 200.0,
     'conv_ln_g_2': 130.523,
     'conv_ln_b_2': 200.0,
     'ln1_b_2': 2.76,
     'ln2_b_2': 2.884,
     'conv_w_2': 4.691,
     'w_conv_out_2': 3.876}
    for name, (base, spread) in spreads.items():
        noise = np.random.default_rng([zlib.crc32(name.encode()), seed]).standard_normal(out[name].shape)
        drawn = base * np.exp(spread * noise) if base else spread * noise
        out[name] = __import__('jax').numpy.asarray(drawn.astype(out[name].dtype))
    for name, factor in factors.items():
        out[name] = (out[name] * factor).astype(out[name].dtype)
    return out
```

```python
import math
from contextlib import ExitStack

import numpy as np
import concourse.bass as bass
from concourse import mybir

F32 = mybir.dt.float32
F32R = mybir.dt.float32r
ALU = mybir.AluOpType
ACT = mybir.ActivationFunctionType
AX = mybir.AxisListType

P = 128
D = 1024
T = 256
TT = 512
KD = D // P
FF = 2816
KF = FF // P
EPS = 1e-6
LN_EPS = 1e-5
ALPHA = 2.0 ** 0.25
NRAW = 5
NHL = 4
CH = 1024
NEG = -1.0e30
WTOTAL = 128 * 250368


def const_layout():
    items = [
        ("cvec", 8 * 2), ("bmod", 2 * 24), ("ng", 2 * 8), ("eps", 4), ("sel", 2),
        ("ones", 128), ("ident", 128),
        ("c64", 128), ("s64", 128), ("c256", 512), ("s256", 512),
        ("qag", 2 * 2), ("kvag", 2), ("gq", 2), ("gk", 2), ("gqr", 2 * 32), ("gkr", 2 * 32),
        ("cos1", 2 * 32), ("sin1", 2 * 32), ("lng", 2 * 64), ("bs", 2 * 2 * 128),
        ("cos2", 2 * 32), ("sin2", 2 * 32), ("nsin2", 2 * 32), ("convw", 4 * 31), ("convb", 4), ("cg", 4), ("cb", 4),
        ("l1g", 8), ("l1b", 8), ("l2g", 8), ("l2b", 8),
        ("mask1", 3 * 256),
    ]
    at, off = {}, 0
    for name, n in items:
        at[name] = (off, n)
        off += n
    return at, off


C_AT, C_N = const_layout()
C_EARLY = C_AT["c64"][0]


class Lane:

    def __init__(self, sem):
        self.sem, self.n, self.q, self.seen = sem, 0, [], {}

    def wait(self, toks):
        for t in toks:
            if t is None:
                continue
            sem, v = t
            if self.seen.get(sem.name, 0) < v:
                self.seen[sem.name] = v
                self.q.append(("w", sem, v))

    def quiet(self, fn, after=()):
        self.wait(after)
        self.q.append(("i", fn, None, 0))

    def __call__(self, fn, after=()):
        self.wait(after)
        self.n += 1
        self.q.append(("i", fn, self.sem, 1))
        return (self.sem, self.n)

    def dma(self, fn, tok, after=()):
        self.wait(after)
        self.q.append(("i", fn, tok[0], 16))
        return tok

    def last(self):
        return (self.sem, self.n)

    def run(self, e):
        for x in self.q:
            if x[0] == "w":
                e.wait_ge(x[1], x[2])
            else:
                i = x[1](e)
                if x[2] is not None:
                    i.then_inc(x[2], x[3])


class Banks:

    def __init__(self, ps):
        self.ps, self.free, self.held, self.i = ps, [()] * 8, [False] * 8, 0

    def take(self, n=1):
        for _ in range(16):
            i = self.i % 8
            if i + n <= 8 and not any(self.held[i:i + n]):
                self.i = i + n
                for j in range(i, i + n):
                    self.held[j] = True
                return i, [t for j in range(i, i + n) for t in self.free[j]]
            self.i += 1
        raise RuntimeError("no PSUM bank is free")

    def give(self, i, toks, n=1):
        for j in range(i, i + n):
            self.held[j] = False
            self.free[j] = tuple(toks)

    def ap(self, i, n=512):
        return self.ps[:, i * 512:i * 512 + n]


class Stream:

    def __init__(self, S, plan):
        self.S, self.plan, self.seq = S, plan, []
        self.loaded = self.prepped = self.split = 0
        self.rel = {}
        self.relsplit = {}
        self.ready = {}
        self.off = 0

    def advance(self):
        S = self.S
        while self.loaded < len(self.plan):
            i = self.loaded
            if i >= NRAW and (i - NRAW) not in self.rel:
                break
            _, n, _ = self.plan[i]
            slot, off = i % NRAW, self.off
            dst, src = S.raw[:, slot * CH:slot * CH + n], S.wpack[off:off + P * n].rearrange("(p n) -> p n", n=n)
            tok = (S.s_raw[slot], 16 * (i // NRAW + 1))
            S.SP.dma(lambda e, d=dst, s=src: e.dma_start(d, s), tok, [self.rel.get(i - NRAW)])
            self.off += P * n
            self.loaded += 1
        while self.prepped < self.loaded:
            i = self.prepped
            _, n, sp = self.plan[i]
            slot = i % NRAW
            tok = (S.s_raw[slot], 16 * (i // NRAW + 1))
            if not sp:
                self.ready[i] = ([tok], None)
            else:
                j = self.split
                if j >= NHL and (j - NHL) not in self.relsplit:
                    break
                h = j % NHL
                raw = S.raw[:, slot * CH:slot * CH + n]
                hi, lo = S.whi[:, h * CH:h * CH + n], S.wlo[:, h * CH:h * CH + n]
                used = self.relsplit.get(j - NHL)
                t1 = S.ACT(lambda e, o=hi, x=raw: e.activation(o, x, ACT.Copy), [tok, used])
                t2 = S.DVE(lambda e, o=lo, x=raw, y=hi: e.tensor_tensor(o, x, y, ALU.subtract), [tok, t1])
                self.rel[i] = t2
                self.ready[i] = ([t1, t2], j)
                self.split += 1
            self.prepped += 1

    def get(self, desc, n, split=True):
        i = len(self.seq)
        self.seq.append((desc, n, split))
        if self.plan is None:
            z = self.S.raw[:, 0:n]
            return (z, z if split else None), [], i
        self.advance()
        toks, j = self.ready[i]
        if j is None:
            s = i % NRAW
            return (self.S.raw[:, s * CH:s * CH + n], None), toks, i
        h = j % NHL
        return (self.S.whi[:, h * CH:h * CH + n], self.S.wlo[:, h * CH:h * CH + n]), toks, i

    def done(self, i, tok):
        if self.plan is None:
            return
        j = self.ready[i][1]
        if j is None:
            self.rel[i] = tok
        else:
            self.relsplit[j] = tok


class State:
    pass


def emit(S, plan):
    PE, AC, DV, SP, GP = Lane(S.s_pe), Lane(S.s_act), Lane(S.s_dve), Lane(S.s_c0), Lane(S.s_uq)
    S.GP = GP
    S.PE, S.ACT, S.DVE, S.SP = PE, AC, DV, SP
    W = Stream(S, plan)
    B = Banks(S.ps)
    XT, hh, hl = S.XT, S.hh, S.hl
    AF = S.AF

    def C(name, a=0, n=None, parts=P):
        off, m = C_AT[name]
        return S.cst[0:parts, off + a:off + a + (m - a if n is None else n)]

    def mm(out, lhsT, rhs, start, stop, after=(), inc=False):
        f = lambda e: e.matmul(out, lhsT, rhs, start=start, stop=stop, skip_group_check=True)
        if inc:
            return PE(f, after)
        PE.quiet(f, after)

    def act(out, in_, func=ACT.Copy, after=(), **kw):
        return AC(lambda e: e.activation(out, in_, func, **kw), after)

    def tt(out, a, b, op, after=()):
        return DV(lambda e: e.tensor_tensor(out, a, b, op), after)

    def stt(out, a, s, b, op0, op1, after=()):
        return DV(lambda e: e.scalar_tensor_tensor(out=out, in0=a, scalar=s, in1=b, op0=op0, op1=op1), after)

    def ts(out, a, s1, s2, op0, op1, after=()):
        return DV(lambda e: e.tensor_scalar(out, a, s1, s2, op0, op1), after)

    def rsum(out, in_, after=()):
        return DV(lambda e: e.tensor_reduce(out, in_, AX.X, ALU.add), after)

    def dcopy(out, in_, after=()):
        return DV(lambda e: e.tensor_copy(out, in_), after)

    def transpose(out, in_, after=()):
        return PE(lambda e: e.transpose(out, in_, C("ident")), after)

    def split_to(hi, lo, src, after=()):
        t = act(hi, src, after=after)
        u = tt(lo, src, hi, ALU.subtract, [*after, t])
        return [t, u]

    def barrier():
        return [PE.last(), AC.last(), DV.last()]

    t_c0 = SP.dma(lambda e: e.dma_start(S.cst[:, 0:C_EARLY], S.cpack[:, 0:C_EARLY]), (S.s_c0, 16))
    if plan is not None:
        W.advance()
    t_x = AC.dma(lambda e: e.dma_start(XT[:, :, :], S.xin.rearrange("p (k n) -> p k n", k=KD)), (S.s_x, 16))
    t_c1 = AC.dma(lambda e: e.dma_start(S.cst[:, C_EARLY:C_N], S.cpack[:, C_EARLY:C_N]), (S.s_c1, 16))

    def lin_fm(wname, l, cols, K, xh, xl, N, xtoks, ps=None, kk=None, start=True, stop=True, free=()):
        if ps is None:
            b, free = B.take()
            ps = B.ap(b, N)
        else:
            b = None
        kk = list(range(K)) if kk is None else kk
        tok = None
        groups = [kk[i:i + 8] for i in range(0, len(kk), 8)]
        for g in groups:
            (whi, wlo), toks, ci = W.get((wname, l, tuple(g), tuple(cols)), len(g) * P)
            for j, k in enumerate(g):
                wh, wl = whi[:, j * P:(j + 1) * P], wlo[:, j * P:(j + 1) * P]
                xt = list(xtoks(k)) if callable(xtoks) else list(xtoks)
                first, last = start and k == kk[0], stop and k == kk[-1]
                mm(ps, wh, xh(k), first, False, [*toks, *free, *xt])
                mm(ps, wh, xl(k), False, False)
                if k == g[-1]:
                    tok = mm(ps, wl, xh(k), False, last, inc=True)
                else:
                    mm(ps, wl, xh(k), False, last)
            W.done(ci, tok)
        return b, ps, tok

    def lin_tm(wname, l, c0, ncols, xh, xl, toks_of, tiles, per, xtoks, cut=None):
        bs = {t: B.take() for t in tiles}
        k = 0
        while k < KD:
            g = list(range(k, min(k + per, KD)))
            (whi, wlo), toks, ci = W.get((wname, l, tuple(g), (c0, ncols)), len(g) * ncols)
            for j, kk in enumerate(g):
                xt = list(xtoks(kk)) if callable(xtoks) else list(xtoks)
                for t in tiles:
                    lo_c = cut(t) if cut else 0
                    wh, wl = (w[:, j * ncols + lo_c:(j + 1) * ncols] for w in (whi, wlo))
                    o = B.ps[:, bs[t][0] * 512 + lo_c:bs[t][0] * 512 + ncols]
                    ts_ = toks_of(t)
                    mm(o, xh(kk)[:, ts_], wh, kk == 0, False, [*toks, *bs[t][1], *xt])
                    mm(o, xh(kk)[:, ts_], wl, False, False)
                    tok = mm(o, xl(kk)[:, ts_], wh, False, kk == KD - 1, inc=True)
            W.done(ci, tok)
            k += per
        return {t: bs[t][0] for t in tiles}, tok

    t = act(S.c32[:, 0:16], C("cvec"), ACT.Silu, [t_c0])
    c32 = S.c32[:, 0:16].rearrange("p (k s) -> p k s", s=2)
    c4 = S.c4[:, :].rearrange("p (k s) -> p k s", s=4)
    t1 = act(c4[:, :, 0:2], c32, after=[t])
    t_c4 = [t1, tt(c4[:, :, 2:4], c32, c4[:, :, 0:2], ALU.subtract, [t, t1])]
    modt = {}
    mod_rd = [None, None]
    modc = [0]

    def modulation(l, n):
        b, free = B.take()
        ps = B.ps[0:4, b * 512:b * 512 + 512]
        for g in range(4):
            (whi, wlo), toks, ci = W.get(("w_mod", l, (2 * g, 2 * g + 1), (512 * n, 512)), 1024)
            for j in range(2):
                k = 2 * g + j
                mm(ps, c4[:, k, :], whi[:, j * 512:(j + 1) * 512], k == 0, False, [*toks, *free, *t_c4])
                tok = mm(ps, c4[:, k, :], wlo[:, j * 512:(j + 1) * 512], False, k == 7, inc=(j == 1))
            W.done(ci, tok)
        z = 0
        row = S.modrow[0:4, :]
        t = act(row, ps, after=[tok, mod_rd[z]])
        B.give(b, [t])
        b, free = B.take()
        for j in range(4):
            tok = mm(B.ps[:, b * 512 + 2 * j:b * 512 + 2 * j + 2], row[:, j * P:(j + 1) * P],
                     C("sel", parts=4), True, True, [t, *free], inc=(j == 3))
        mod_rd[z] = tok
        o = S.mod[:, l * 48 + 8 * n:l * 48 + 8 * n + 8].rearrange("p (j s) -> p j s", s=2)
        bm = C("bmod", 24 * l + 4 * n, 4).unsqueeze(2).broadcast_to([P, 4, 2])
        t = tt(o, B.ap(b, 8).rearrange("p (j s) -> p j s", s=2), bm, ALU.add, [tok])
        B.give(b, [t])
        if n in (2, 3):
            ng = C("ng", 8 * l + 4 * (n - 2), 4).unsqueeze(2).broadcast_to([P, 4, 2])
            t = stt(o, o, 1.0, ng, ALU.add, ALU.mult, [t])
        modt[(l, n)] = t

    def modv(l, what, k, s):
        n = what * 2 + k // 4
        c = l * 48 + 8 * n + 2 * (k % 4) + s
        return S.mod[:, c:c + 1], modt[(l, n)]

    def rms_add(k, n0, n1, after, rd=None):
        z = k % 2
        sq = S.sq[:, z * 512 + n0:z * 512 + n1]
        t = act(sq, XT[:, k, n0:n1], ACT.Square, [*after, S.sq_rd[z]])
        if k == 0:
            u = DV(lambda e: e.tensor_copy(S.acc[:, n0:n1], sq), [t, *S.acc_rd])
        else:
            u = tt(S.acc[:, n0:n1], S.acc[:, n0:n1], sq, ALU.add, [t, S.acc_t])
        S.sq_rd[z] = u
        S.acc_t = u

    def rms_rstd():
        b, free = B.take()
        tok = mm(B.ap(b), C("ones"), S.acc[:, 0:512], True, True, [S.acc_t, t_c0, *free], inc=True)
        S.acc_rd = [tok]
        t = act(S.rs[:, 0:512], B.ap(b), ACT.Ln, [tok, *S.rs_rd], scale=1.0 / D, bias=C("eps", 0, 1))
        B.give(b, [t])
        return act(S.rs[:, 0:512], S.rs[:, 0:512], ACT.Exp, [t], scale=-0.5)

    def make_h(l, tr):
        toks = []
        bar = barrier()
        for k in range(KD):
            out = []
            for s in range(2):
                c = slice(256 * s, 256 * s + 256)
                A, ta = modv(l, 1, k, s)
                sh, tb = modv(l, 0, k, s)
                z = (2 * k + s) % 4
                tmp = S.sq[:, z * 256:(z + 1) * 256]
                t = stt(tmp, XT[:, k, c], A, S.rs[:, c], ALU.mult, ALU.mult, [tr, ta, *bar, S.tmp_rd[z]])
                u = act(hh[:, k, c], tmp, ACT.Identity, [t, tb], bias=sh)
                v = stt(hl[:, k, c], tmp, sh, hh[:, k, c], ALU.add, ALU.subtract, [u])
                S.tmp_rd[z] = v
                S.rs_rd = [v]
                out += [u, v]
            toks.append(out)
        S.sq_rd = [DV.last(), DV.last()]
        return toks

    S.sq_rd, S.acc_rd, S.rs_rd, S.tmp_rd, S.acc_t = [None, None], [], [], [None] * 4, None

    S.x2 = [None] * KD
    for k in range(KD):
        rms_add(k, 0, 512, [t_x])
    for n in (2, 3, 0, 1):
        modulation(0, n)

    for l in range(2):
        ns = 2 if l == 0 else 1
        x0 = 0 if l == 0 else 256
        N = TT - x0
        cs = slice(x0, TT)
        tiles = list(range(x0 // P, 4))
        qtiles = tiles
        tr = rms_rstd()
        t_h = make_h(l, tr)
        bar = barrier()

        o = 0

        def area(n):
            nonlocal o
            a = AF[:, o:o + n]
            o += n
            return a

        fg = area(2 * TT).rearrange("p (k n) -> p k n", k=2)
        ug = area(2 * TT).rearrange("p (k n) -> p k n", k=2)
        ag = area(4 * TT).rearrange("p (k n) -> p k n", k=4)
        gv = area(4 * 256)
        kr = area(4 * 32)
        cq = area(2 * TT).rearrange("p (k n) -> p k n", k=2)
        ckv = area(TT)
        tq = area(2 * 768)
        stat = area(128)
        V = area(4 * 512).rearrange("p (t n) -> p t n", t=4)
        Q = area(2 * 1024)
        Pb = area(3 * 512)
        PT = area(2 * 512)
        ko = o
        K = area(8 * TT).rearrange("p (h n) -> p h n", h=8)
        end = o
        o = ko
        fi = area(2 * TT).rearrange("p (k n) -> p k n", k=2)
        W12 = area(1024).rearrange("p (c k n) -> p c k n", c=2, k=2)
        Vf = area(4 * 512).rearrange("p (t n) -> p t n", t=4)
        assert max(o, end) <= S.NAF, max(o, end)
        gv2 = Pb[:, 0:1024]
        xh, xl = (lambda k: hh[:, k, cs]), (lambda k: hl[:, k, cs])
        XH, XL = (lambda k: hh[:, k, :]), (lambda k: hl[:, k, :])
        ht = lambda k: t_h[k]
        off = {}
        c0 = 0
        for nm, w in (("fin", 256), ("fgate", 256), ("gu", 256), ("gv", 256), ("ggate", 256), ("cq", 256), ("ckv", 128), ("kr", 32), ("agate", 512)):
            off[nm] = c0
            c0 += w

        def inp(nm, m, full=False):
            return lin_fm("w_in", l, (off[nm] + P * m, P), KD, XH if full else xh, XL if full else xl,
                          TT if full else N, ht)

        t_fi = []
        for m in range(2):
            b, ps, tok = inp("fin", m)
            t = act(fi[:, m, cs], ps, after=[tok, *bar])
            B.give(b, [t])
            t_fi.append(t)

        sqb = S.sq
        b_st, free_st = B.take()
        t_sq = []
        for m in range(2):
            b, ps, tok = inp("cq", m)
            t = act(cq[:, m, cs], ps, after=[tok, t_c1, *bar], scale=C("qag", 2 * l + m, 1))
            u = act(sqb[:, m * 512:m * 512 + N], ps, ACT.Square, [tok, *bar])
            B.give(b, [u])
            t_sq.append(u)
        t_cq = [t]
        for t in qtiles:
            for m in range(2):
                j = (t - tiles[0]) * P
                tok = mm(B.ps[:, b_st * 512 + t:b_st * 512 + t + 1], sqb[:, m * 512 + j:m * 512 + j + P],
                         C("ones", 0, 1), m == 0, m == 1, [*t_sq, *free_st], inc=(m == 1))
        b, ps, tokc = inp("ckv", 0, True)
        t_ck = act(ckv, ps, after=[tokc, *bar], scale=C("kvag", l, 1))
        u = act(sqb[:, 0:512], ps, ACT.Square, [tokc, tok])
        B.give(b, [u])
        for t in range(4):
            tok = mm(B.ps[:, b_st * 512 + 4 + t:b_st * 512 + 5 + t], sqb[:, t * P:(t + 1) * P],
                     C("ones", 0, 1), True, True, [u], inc=True)
        S.sq_rd = [tok, tok]
        S.tmp_rd = [tok] * 4
        t = act(stat[:, 0:4][:, tiles[0]:4], B.ps[:, b_st * 512 + tiles[0]:b_st * 512 + 4], ACT.Ln, [tok, *bar],
                scale=1.0 / 256, bias=C("eps", 0, 1))
        t = act(stat[:, 4:8], B.ps[:, b_st * 512 + 4:b_st * 512 + 8], ACT.Ln, [t], scale=1.0 / 128, bias=C("eps", 0, 1))
        B.give(b_st, [t])
        t_stat = act(stat[:, tiles[0]:8], stat[:, tiles[0]:8], ACT.Exp, [t], scale=-0.5)

        gb, tok = lin_tm("w_in", l, ("gvkr",), 288, XH, XL, lambda t: slice(t * P, (t + 1) * P), list(range(4)), 3, ht,
                         cut=lambda t: 0 if t in tiles else 256)
        t_gv = []
        for t in range(4):
            pb = B.ap(gb[t])
            u = act(kr[:, t * 32:(t + 1) * 32], pb[:, 256:288], after=[tok, *bar])
            if t in tiles:
                u = act(gv[:, t * 256:(t + 1) * 256], pb[:, 0:256], after=[tok])
            B.give(gb[t], [u])
        t_gv = [u]

        (wf, _), toks, ci = W.get(("w_fmix", l, (0, 1), (0, 256)), 512, split=False)
        for c, nm in enumerate(("c64", "s64")):
            b, free = B.take()
            tok = mm(B.ap(b), C(nm), wf, True, True, [*toks, *free, t_c1], inc=True)
            t = act(W12[:, c, :, :], B.ap(b).rearrange("p (k n) -> p k n", k=2), after=[tok, *bar])
            B.give(b, [t])
        W.done(ci, tok)
        t_w12 = t
        t_vf = {}
        for t in tiles:
            b, free = B.take()
            for m in range(2):
                tok = mm(B.ap(b).rearrange("p (c n) -> p c n", c=2), fi[:, m, t * P:(t + 1) * P], W12[:, :, m, :],
                         m == 0, m == 1, [t_w12, *t_fi, *free], inc=(m == 1))
            t_vf[t] = DV(lambda e, o=Vf[:, t, :], i=B.ap(b): e.tensor_copy(o, i), [tok, *bar])
            B.give(b, [t_vf[t]])

        t_mix = {}
        mixt = {}

        def to_mix(k, c, src, after):
            mixt.setdefault(k, [])
            mixt[k] += split_to(hh[:, k, c], hl[:, k, c], src, after)

        def f_gate(m):
            b, ps, tok = inp("fgate", m)
            t = act(fg[:, m, cs], ps, ACT.Silu, [tok, *bar])
            B.give(b, [t])
            t_fg[m] = t

        def g_gate(m):
            b, ps, tok = inp("ggate", m)
            t = act(ug[:, m, cs], ps, ACT.Silu, [tok, *bar])
            B.give(b, [t])
            b, ps, tok = inp("gu", m)
            u = tt(ug[:, m, cs], ug[:, m, cs], ps, ALU.mult, [tok, t])
            B.give(b, [u])
            t_ug[m] = u

        def a_gate(m):
            b, ps, tok = inp("agate", m)
            t = act(ag[:, m, cs], ps, ACT.Silu, [tok, *bar])
            B.give(b, [t])
            t_ag[m] = t

        t_fg, t_ug, t_ag = {}, {}, {}
        for m in range(2):
            f_gate(m)
        for m in range(2):
            g_gate(m)

        G = gv[:, tiles[0] * 256:1024].rearrange("p (g d) -> p g d", d=64)
        G2 = gv2[:, tiles[0] * 256:1024].rearrange("p (g d) -> p g d", d=64)
        ng_ = 4 * len(tiles)
        mu, va = stat[:, 16:16 + ng_], stat[:, 32:32 + ng_]
        t = rsum(mu, G, [*t_gv, *bar])
        t = ts(mu, mu, -1.0 / 64, None, ALU.mult, ALU.bypass, [t])
        t = tt(G, G, mu.unsqueeze(2).broadcast_to([P, ng_, 64]), ALU.add, [t])
        u = tt(G2, G, G, ALU.mult, [t])
        u = rsum(va, G2, [u])
        u = act(va, va, ACT.Ln, [u], scale=1.0 / 64, bias=C("eps", 0, 1))
        u = act(va, va, ACT.Exp, [u], scale=-0.5)
        t = tt(G, G, va.unsqueeze(2).broadcast_to([P, ng_, 64]), ALU.mult, [t, u])
        t_ln = tt(G, G, C("lng", 64 * l, 64).unsqueeze(1).broadcast_to([P, ng_, 64]), ALU.mult, [t, t_c1])

        for m in range(4):
            a_gate(m)

        hfree = [PE.last()]
        for m in range(2):
            b, free = B.take()
            for s in range(2 if l == 0 else 1):
                q = s if l == 0 else 1
                for t in range(2):
                    tk = 2 * q + t
                    o_ = B.ps[:, b * 512 + 256 * s:b * 512 + 256 * s + 256]
                    mm(o_, Vf[:, tk, m * P:(m + 1) * P], C("c256", 256 * t, 256), t == 0, False, [t_vf[tk], *free])
                    tok = mm(o_, Vf[:, tk, 256 + m * P:256 + (m + 1) * P], C("s256", 256 * t, 256), False, t == 1, inc=True)
            fo = S.sq[:, 0:N]
            t = tt(fo, B.ap(b, N), fg[:, m, cs], ALU.mult, [tok, t_fg[m], *S.sq_rd, *S.tmp_rd, *hfree])
            B.give(b, [t])
            to_mix(m, cs, fo, [t])
            S.sq_rd = [DV.last(), AC.last()]

        (ws, _), toks, ci = W.get(("g_ws", l, (0, 1, 2, 3), (0, 128)), 512, split=False)
        for m in range(2):
            b, free = B.take()
            for t in tiles:
                j = t - tiles[0]
                for h2 in range(2):
                    h = 2 * m + h2
                    tok = mm(B.ps[64 * h2:64 * h2 + 64, b * 512 + j * P:b * 512 + (j + 1) * P],
                             gv[:, t * 256 + h * 64:t * 256 + h * 64 + 64], ws[:, h * P:(h + 1) * P],
                             True, True, [t_ln, *toks, *free], inc=True)
            go = S.sq[:, 512:512 + N]
            bs = C("bs", (2 * l + m) * P, P).unsqueeze(1).broadcast_to([P, len(tiles), P])
            t = tt(go.rearrange("p (t n) -> p t n", n=P), B.ap(b, N).rearrange("p (t n) -> p t n", n=P), bs, ALU.add,
                   [tok, *S.sq_rd])
            B.give(b, [t])
            t = tt(go, go, ug[:, m, cs], ALU.mult, [t, t_ug[m]])
            to_mix(2 + m, cs, go, [t, *hfree])
            S.sq_rd = [DV.last(), AC.last()]
        W.done(ci, tok)

        uq = AF[:, 0:1536]
        t_uq = GP.dma(lambda e, l=l: e.dma_start(uq, S.wuq[l]), (S.s_uq, 16 * (l + 1)), barrier())

        rt = {}
        for i, nm in enumerate(("gqr", "gkr")):
            g32 = C(nm, 32 * l, 32)
            tab = S.rtab[:, i * 128:(i + 1) * 128]
            gc = tab[:, 0:64].rearrange("p (t n) -> p t n", t=2)
            gs = tab[:, 64:128].rearrange("p (t a b n) -> p t a b n", t=2, a=2, b=2)
            gr = g32.rearrange("p (a b n) -> p a b n", a=2, b=2)
            sn = C("sin1").rearrange("p (t a b n) -> p t a b n", t=2, a=2, b=2)
            a = tt(gc, C("cos1").rearrange("p (t n) -> p t n", t=2), g32.unsqueeze(1).broadcast_to([P, 2, 32]),
                   ALU.mult, [t_c1, *bar])
            for hf in range(2):
                for tt_ in range(2):
                    a = tt(gs[:, tt_, :, hf, :], sn[:, tt_, :, hf, :], gr[:, :, 1 - hf, :], ALU.mult, [a])
            rt[i] = (tab, g32, a)

        st_i = [0]
        tq_free = [(), (), [DV.last()]]

        def norm_rope(i, t, X, ready, lnscale, parity):
            X3 = X.rearrange("p (h d) -> p h d", h=8)
            sqq = gv[:, 0:768]
            ss = stat[:, 48 + 8 * parity:56 + 8 * parity]
            a = act(sqq, X, ACT.Square, [*ready, *tq_free[2]])
            a = rsum(ss, sqq.rearrange("p (h d) -> p h d", h=8), [a, *st_free[parity]])
            a = act(ss, ss, ACT.Ln, [a], scale=1.0 / 96, bias=C("eps", 0, 1))
            a = act(ss, ss, ACT.Exp, [a], scale=-0.5, bias=C("eps", 2 if lnscale else 3, 1))
            a = tt(X3, X3, ss.unsqueeze(2).broadcast_to([P, 8, 96]), ALU.mult, [a])
            st_free[parity] = [a]
            tab, g32, tk = rt[i]
            R = X3[:, :, 64:96]
            if t >= 2:
                R1 = sqq[:, 0:256].rearrange("p (h n) -> p h n", h=8)
                R2 = sqq[:, 256:512].rearrange("p (h n) -> p h n", h=8)
                gc = tab[:, 32 * (t - 2):32 * (t - 1)].unsqueeze(1).broadcast_to([P, 8, 32])
                gs = tab[:, 64 + 32 * (t - 2):64 + 32 * (t - 1)].rearrange("p (a b n) -> p a b n", a=2, b=2)
                u = tt(R1, R, gc, ALU.mult, [a, tk])
                for ax in range(2):
                    for hf in range(2):
                        v = tt(R2[:, :, 16 * ax + 8 * hf:16 * ax + 8 * hf + 8],
                               R[:, :, 16 * ax + 8 * (1 - hf):16 * ax + 8 * (1 - hf) + 8],
                               gs[:, ax, hf, :].unsqueeze(1).broadcast_to([P, 8, 8]), ALU.mult, [a, tk])
                a = tt(R, R1, R2, ALU.add, [u, v])
            else:
                a = tt(R, R, g32.unsqueeze(1).broadcast_to([P, 8, 32]), ALU.mult, [a])
            tq_free[2] = [a]
            return a

        def heads_T(X, dst, gcol, ready, after):
            for h0 in (0, 4):
                b, free = B.take()
                for j in range(4):
                    tok = PE(lambda e, o=B.ps[0:96, b * 512 + j * P:b * 512 + (j + 1) * P],
                             i=X[:, (h0 + j) * 96:(h0 + j + 1) * 96]: e.transpose(o, i, C("ident")), [*ready, *free])
                a = act(dst(h0), B.ps[0:96, b * 512:b * 512 + 512].rearrange("p (h n) -> p h n", h=4),
                        after=[tok, *after], scale=gcol)
                B.give(b, [a])
            return tok, a

        st_free = [[], []]
        kbar = barrier()
        (wkv, _), toks, ci = W.get(("w_ukv", l, (0,), (0, 1024)), 1024, split=False)
        t_K = {}
        t_V = {}
        xp = [0]
        for t in range(4):
            b0, f0 = B.take()
            b1, f1 = B.take()
            tk0 = mm(B.ap(b0), ckv[:, t * P:(t + 1) * P], wkv[:, 0:512], True, True, [*toks, *f0, t_ck], inc=True)
            tk1 = mm(B.ap(b1), ckv[:, t * P:(t + 1) * P], wkv[:, 512:1024], True, True, [*f1], inc=True)
            z = xp[0] % 2
            xp[0] += 1
            X = tq[:, z * 768:(z + 1) * 768]
            X3 = X.rearrange("p (h d) -> p h d", h=8)
            a = act(X3[:, :, 0:64], B.ap(b0).rearrange("p (h d) -> p h d", h=8), after=[tk0, t_stat, *tq_free[z]],
                    scale=stat[:, 4 + t:5 + t])
            B.give(b0, [a])
            c = DV(lambda e, o=X3[:, :, 64:96], i=kr[:, t * 32:(t + 1) * 32].unsqueeze(1).broadcast_to([P, 8, 32]):
                   e.tensor_copy(o, i), [*t_gv, *tq_free[z]])
            v = act(V[:, t, :], B.ap(b1), after=[tk1, *bar], scale=stat[:, 4 + t:5 + t])
            B.give(b1, [v])
            t_V[t] = v
            r = norm_rope(1, t, X, [a, c], False, z)
            tkx, a = heads_T(X, lambda h0: K[0:96, h0:h0 + 4, t * P:(t + 1) * P], C("gk", l, 1, 96), [r], kbar)
            tq_free[z] = [tkx]
            t_K[t] = a
        W.done(ci, tk1)
        if l == 0:
            modulation(0, 4)
            modulation(0, 5)

        t_mo = {}
        it = [0]
        P_free = [[], [], []]
        PT_free = [[], []]
        Q_free = [[], []]
        wq0, wq1, toks0, toks1 = uq[:, 0:768], uq[:, 768:1536], [t_uq], [t_uq]
        qq = {}

        def make_q(t):
            b0, f0 = B.take(2)
            for c, w in ((0, 512), (512, 256)):
                for m, (wq, tks) in enumerate(((wq0, toks0), (wq1, toks1))):
                    tok = mm(B.ps[:, b0 * 512 + c:b0 * 512 + c + w], cq[:, m, t * P:(t + 1) * P], wq[:, c:c + w],
                             m == 0, m == 1, [*f0, *tks, *t_cq], inc=(m == 1))
            qq["tok"] = tok
            z = xp[0] % 2
            xp[0] += 1
            X = tq[:, z * 768:(z + 1) * 768]
            a = act(X, B.ap(b0, 768), after=[tok, t_stat, *tq_free[z]], scale=stat[:, t:t + 1])
            B.give(b0, [a], 2)
            r = norm_rope(0, t, X, [a], True, z)
            y = t % 2
            Qt = Q[:, y * 1024:(y + 1) * 1024].rearrange("p (h n) -> p h n", h=8)
            tkx, a = heads_T(X, lambda h0: Qt[0:96, h0:h0 + 4, :], C("gq", l, 1, 96), [r], Q_free[y])
            tq_free[z] = [tkx]
            qq[t] = (Qt, a)

        items = []
        for t in qtiles:
            for h in range(8):
                items.append((t, h))
        ob = {}
        info = {}

        def partA(i):
            t, h = items[i]
            Qt, tQ = qq[t]
            nk = 2 if t < 2 else 4
            b, free = B.take()
            n = nk * P
            tok = mm(B.ap(b, n), Qt[0:96, h, :], K[0:96, h, 0:n], True, True, [tQ, *(t_K[j] for j in range(nk)), *free], inc=True)
            Q_free[t % 2] = [tok]
            z = i % 3
            mx, sm = stat[:, 64 + z:65 + z], stat[:, 68 + z:69 + z]
            a = DV(lambda e: e.tensor_reduce(mx, B.ap(b, n), AX.X, ALU.max, negate=True), [tok, *P_free[z]])
            pb = Pb[:, z * 512:z * 512 + n]
            c = AC(lambda e: e.activation(pb, B.ap(b, n), ACT.Exp, bias=mx, accum_out=sm), [a, *P_free[z]])
            B.give(b, [c])
            info[i] = [nk, z, pb, c, sm]

        def partA2(i):
            nk, z, pb, c, sm = info[i]
            a = DV(lambda e: e.reciprocal(sm, sm), [c])
            a = ts(pb, pb, sm, None, ALU.mult, ALU.bypass, [a])
            info[i].append(a)

        def partB(i):
            nk, z, pb, c, sm, a = info[i]
            b, free = B.take()
            for j in range(nk):
                tok = PE(lambda e, o=B.ps[:, b * 512 + j * P:b * 512 + (j + 1) * P], x=pb[:, j * P:(j + 1) * P]:
                         e.transpose(o, x, C("ident")), [a, *free])
            P_free[z] = [tok]
            y = i % 2
            pt = PT[:, y * 512:y * 512 + nk * P]
            u = act(pt, B.ap(b, nk * P), after=[tok, *PT_free[y], *bar])
            B.give(b, [u])
            info[i] += [pt, u]

        def partC(i):
            t, h = items[i]
            nk, z, pt, u = info[i][0], info[i][1], info[i][6], info[i][7]
            if h == 0:
                ob[t] = B.take()
            b, free = ob[t]
            o_ = B.ps[64 * (h % 2):64 * (h % 2) + 64, b * 512 + (h // 2) * P:b * 512 + (h // 2 + 1) * P]
            for j in range(nk):
                tok = mm(o_, V[:, j, h * 64:(h + 1) * 64], pt[:, j * P:(j + 1) * P], j == 0, j == nk - 1,
                         [u, t_V[j], *free], inc=(j == nk - 1))
            PT_free[i % 2] = [tok]
            if h == 7:
                oo = S.sq[:, (t % 2) * 512:(t % 2) * 512 + 512]
                o3 = oo.rearrange("p (k n) -> p k n", k=4)
                c = slice(t * P, (t + 1) * P)
                a = tt(o3, B.ap(b).rearrange("p (k n) -> p k n", k=4), ag[:, :, c], ALU.mult,
                       [tok, *(t_ag[m] for m in range(4)), *S.sq_rd])
                B.give(b, [a])
                r = split_to(hh[:, 4:8, c], hl[:, 4:8, c], o3, [a, *hfree])
                for k in range(4, 8):
                    mixt.setdefault(k, [])
                    mixt[k] += r
                S.sq_rd = [DV.last(), AC.last()]

        make_q(qtiles[0])
        ni = len(items)
        fill = [(1, n) for n in (2, 3, 0, 1)] if l == 0 else []
        for i in range(ni + 3):
            if i < ni:
                partA(i)
                if i % 8 == 3 and i // 8 + 1 < len(qtiles):
                    make_q(qtiles[i // 8 + 1])
            if 0 <= i - 1 < ni:
                partA2(i - 1)
            if 0 <= i - 2 < ni:
                partB(i - 2)
            if 0 <= i - 3 < ni:
                partC(i - 3)
        for f in fill:
            modulation(*f)

        mt = lambda k: mixt[k]
        S.acc_ready = None
        for m in range(KD):
            b, ps, tok = lin_fm("w_out", l, (P * m, P), KD, xh, xl, N, mt)
            for s in range(2):
                if s == 0 and l == 1:
                    continue
                c = slice(256 * s, 256 * s + 256)
                gt, tg = modv(l, 2, m, s)
                pc = slice(256 * s - x0, 256 * s - x0 + 256)
                t = stt(XT[:, m, c], ps[:, pc], gt, XT[:, m, c], ALU.mult, ALU.add, [tok, tg])
            B.give(b, [t])
            if l == 0:
                rms_add(m, 0, 512, [t, *S.sq_rd])
            else:
                S.x2[m] = t
        if l == 0:
            for n in (4, 5):
                modulation(1, n)

    xc = slice(256, 512)
    bar = barrier()
    t_x2 = [split_to(hh[:, k, 0:256], hl[:, k, 0:256], XT[:, k, xc], [S.x2[k], *bar]) for k in range(KD)]
    X2h, X2l = (lambda k: hh[:, k, 0:256]), (lambda k: hl[:, k, 0:256])
    xt2 = lambda k: t_x2[k]
    o = 0

    def area(n):
        nonlocal o
        a = AF[:, o:o + n]
        o += n
        return a

    Q2 = area(3 * 1024).rearrange("p (g j n) -> p g j n", g=3, j=4)
    K2 = area(3 * 1024).rearrange("p (g j n) -> p g j n", g=3, j=4)
    V2 = area(2 * 1536).rearrange("p (t g n) -> p t g n", t=2, g=3)
    U = area(4 * 286).rearrange("p (m n) -> p m n", m=4)
    CV = area(4 * 256).rearrange("p (m n) -> p m n", m=4)
    Gt = area(16 * 256).rearrange("p (m n) -> p m n", m=16)
    P2 = area(2 * 768)
    rot = P2
    P2T = area(2 * 768)
    st2 = area(16)
    c2 = area(512)
    assert o <= S.NAF, o

    rfree = [[], [], []]
    t_q2, t_v2 = [], []
    sgt = {}
    t_u = [None] * 4
    bsz = {}
    tz = DV(lambda e: e.memset(U[:, :, 0:30], 0.0), bar)
    cur = {"m": 0}

    def conv_in():
        m = cur["m"]
        cur["m"] += 1
        b, ps, tok = lin_fm("w_in_2", 0, (4608 + 512 + P * m, P), KD, X2h, X2l, 256, xt2)
        sg = Gt[:, m, :]
        a = act(sg, ps, ACT.Sigmoid, [tok, *bar])
        B.give(b, [a])
        b, ps, tok = lin_fm("w_in_2", 0, (4608 + P * m, P), KD, X2h, X2l, 256, xt2)
        u = tt(U[:, m, 30:286], ps, sg, ALU.mult, [tok, a, tz])
        B.give(b, [u])
        t_u[m] = u

    for m in range(4):
        conv_in()
    t_cv = [None] * 4
    taps = []
    for j in range(31):
        for m in range(4):
            taps.append((j, m))

    def conv_taps(n):
        for _ in range(min(n, len(taps))):
            j, m = taps.pop(0)
            w = C("convw", 31 * m + j, 1)
            if j == 0:
                t_cv[m] = ts(CV[:, m, :], U[:, m, 0:256], w, C("convb", m, 1), ALU.mult, ALU.add, [t_u[m], tz, t_c1, *bar])
            else:
                t_cv[m] = stt(CV[:, m, :], U[:, m, j:j + 256], w, CV[:, m, :], ALU.mult, ALU.add, [t_cv[m]])

    for g in range(3):
        for w in range(3):
            bb, tok = lin_tm("w_in_2", 0, g * 1536 + w * 512, 512, X2h, X2l, lambda t: slice(t * P, (t + 1) * P), [0, 1], 2, xt2)
            for t in range(2):
                ps = B.ap(bb[t])
                if w == 2:
                    a = act(V2[:, t, g, :], ps, after=[tok, *bar])
                    B.give(bb[t], [a])
                    t_v2 = [a]
                    continue
                r1, r2 = rot[:, 0:512], rot[:, 512:1024]
                p4 = ps.rearrange("p (h a n) -> p h a n", h=8, a=2)
                q4 = r2.rearrange("p (h a n) -> p h a n", h=8, a=2)
                a = tt(r1.rearrange("p (h n) -> p h n", n=32), ps.rearrange("p (h n) -> p h n", n=32),
                       C("cos2", 32 * t, 32).unsqueeze(1).broadcast_to([P, 16, 32]), ALU.mult, [tok, t_c1, *rfree[0], *bar])
                tt(q4[:, :, 0, :], p4[:, :, 1, :], C("nsin2", 32 * t, 32).unsqueeze(1).broadcast_to([P, 8, 32]), ALU.mult, [*rfree[0]])
                u = tt(q4[:, :, 1, :], p4[:, :, 0, :], C("sin2", 32 * t, 32).unsqueeze(1).broadcast_to([P, 8, 32]), ALU.mult, [])
                B.give(bb[t], [u])
                a = tt(r1, r1, r2, ALU.add, [a, u])
                b, free = B.take()
                for j in range(4):
                    tk = PE(lambda e, o=B.ps[:, b * 512 + j * P:b * 512 + (j + 1) * P], x=r1[:, j * P:(j + 1) * P]:
                            e.transpose(o, x, C("ident")), [a, *free])
                rfree[0] = [tk]
                dst = (Q2, K2)[w][:, g, :, t * P:(t + 1) * P]
                a = act(dst, B.ap(b).rearrange("p (j n) -> p j n", j=4), after=[tk, *bar])
                B.give(b, [a])
                t_q2 = [a]
            conv_taps(8)

    t_g = {}
    gl = list(range(16))

    def gate(m):
        b, ps, tok = lin_fm("w_in_2", 0, (4608 + 1024 + P * m, P), KD, X2h, X2l, 256, xt2)
        a = act(Gt[:, m, :], ps, ACT.Sigmoid, [tok, *(x for x in t_u if x)])
        B.give(b, [a])
        t_g[m] = a
        conv_taps(4)

    for m in gl:
        gate(m)
    conv_taps(200)

    ch, cl = S.ch, S.cl

    def ln_stats(src, nt, nfeat, toks, eps_i):
        for k in range(nt):
            if k == 0:
                a = DV(lambda e: e.tensor_copy(S.acc[:, 0:256], src(0)), [*toks(0), *S.acc_rd])
            else:
                a = tt(S.acc[:, 0:256], S.acc[:, 0:256], src(k), ALU.add, [a, *toks(k)])
        b, free = B.take()
        tok = mm(B.ap(b, 256), C("ones"), S.acc[:, 0:256], True, True, [a, *free], inc=True)
        a = act(S.rs[:, 256:512], B.ap(b, 256), after=[tok, *S.rs_rd], scale=1.0 / nfeat)
        B.give(b, [a])
        for k in range(nt):
            u = tt(src(k), src(k), S.rs[:, 256:512], ALU.subtract, [a, *toks(k)])
            z = k % 2
            v = act(S.sq[:, z * 512:z * 512 + 256], src(k), ACT.Square, [u, *S.sq_rd])
            if k == 0:
                w = DV(lambda e: e.tensor_copy(S.acc[:, 0:256], S.sq[:, 0:256]), [v, tok])
            else:
                w = tt(S.acc[:, 0:256], S.acc[:, 0:256], S.sq[:, z * 512:z * 512 + 256], ALU.add, [v, w])
            S.sq_rd = [S.sq_rd[1], w]
        b, free = B.take()
        tok = mm(B.ap(b, 256), C("ones"), S.acc[:, 0:256], True, True, [w, *free], inc=True)
        S.acc_rd = [tok]
        a = act(S.rs[:, 0:256], B.ap(b, 256), ACT.Ln, [tok, *S.rs_rd], scale=1.0 / nfeat, bias=C("eps", eps_i, 1))
        B.give(b, [a])
        a = act(S.rs[:, 0:256], S.rs[:, 0:256], ACT.Exp, [a], scale=-0.5)
        return [a, u]

    S.sq_rd = [DV.last(), AC.last()]
    tl = ln_stats(lambda k: CV[:, k, :], 4, 512, lambda k: [t_cv[k]], 1)
    t_ch = []
    for m in range(4):
        a = stt(CV[:, m, :], CV[:, m, :], C("cg", m, 1), S.rs[:, 0:256], ALU.mult, ALU.mult, tl)
        S.rs_rd = [a]
        a = act(CV[:, m, :], CV[:, m, :], ACT.Silu, [a], bias=C("cb", m, 1))
        t_ch.append(split_to(ch[:, m, :], cl[:, m, :], CV[:, m, :], [a]))

    oh, ol = S.oh, S.ol
    t_o = []
    items = [(qb, h) for qb in range(2) for h in range(8)]
    info = {}
    Pf, PTf = [list(rfree[0]), list(rfree[0])], [[], []]
    ob = {}

    def A(i):
        qb, h = items[i]
        nb = qb + 1
        r = slice(64 * (h % 2), 64 * (h % 2) + 64)
        w = nb * P
        b, free = B.take(2)
        ps = B.ap(b, 3 * w)
        for g in range(3):
            tok = mm(ps[:, g * w:(g + 1) * w], Q2[r, g, h // 2, qb * P:(qb + 1) * P], K2[r, g, h // 2, 0:w],
                     True, True, [*t_q2, *free], inc=(g == 2))
        z = i % 2
        mx, sm = st2[:, z:z + 1], st2[:, 4 + z:5 + z]
        pb = P2[:, z * 768:z * 768 + 3 * w]
        mk = C("mask1").rearrange("p (g n) -> p g n", g=3)[:, :, (0 if qb else 128):256]
        a = DV(lambda e: e.tensor_tensor_reduce(pb.rearrange("p (g n) -> p g n", g=3), ps.rearrange("p (g n) -> p g n", g=3), mk, 1.0, -3.0e38, ALU.add, ALU.max, mx), [tok, *Pf[z], *bar])
        B.give(b, [a], 2)
        a = ts(mx, mx, -0.125, None, ALU.mult, ALU.bypass, [a])
        c = AC(lambda e: e.activation(pb, pb, ACT.Exp, bias=mx, scale=0.125, accum_out=sm), [a])
        info[i] = [nb, z, pb, sm, c]

    def A2(i):
        nb, z, pb, sm, c = info[i]
        a = DV(lambda e: e.reciprocal(sm, sm), [c])
        info[i].append(ts(pb, pb, sm, None, ALU.mult, ALU.bypass, [a]))

    def Bp(i):
        nb, z, pb, sm, c, a = info[i]
        n = 3 * nb
        b, free = B.take(2)
        for j in range(n):
            tok = PE(lambda e, o=B.ps[:, b * 512 + j * P:b * 512 + (j + 1) * P], x=pb[:, j * P:(j + 1) * P]:
                     e.transpose(o, x, C("ident")), [a, *free])
        Pf[z] = [tok]
        pt = P2T[:, z * 768:z * 768 + n * P]
        u = act(pt, B.ap(b, n * P), after=[tok, *PTf[z], *bar])
        B.give(b, [u], 2)
        info[i] += [pt, u]

    def Cp(i):
        qb, h = items[i]
        nb, z, pt, u = info[i][0], info[i][1], info[i][6], info[i][7]
        if h == 0:
            ob[qb] = B.take()
        b, free = ob[qb]
        o_ = B.ps[64 * (h % 2):64 * (h % 2) + 64, b * 512 + (h // 2) * P:b * 512 + (h // 2 + 1) * P]
        n = 3 * nb
        for j in range(n):
            tok = mm(o_, V2[:, j % nb, j // nb, h * 64:(h + 1) * 64], pt[:, j * P:(j + 1) * P], j == 0, j == n - 1,
                     [u, *t_v2, *free], inc=(j == n - 1))
        PTf[z] = [tok]
        if h == 7:
            oo = c2[:, 0:512]
            a = act(oo, B.ap(b), after=[tok, *t_o, *bar])
            B.give(b, [a])
            o3 = oo.rearrange("p (k n) -> p k n", k=4)
            c = slice(qb * P, (qb + 1) * P)
            t_o.extend(split_to(oh[:, :, c], ol[:, :, c], o3, [a]))

    for i in range(16 + 2):
        if i < 16:
            A(i)
        if 0 <= i - 1 < 16:
            A2(i - 1)
            Bp(i - 1)
        if 0 <= i - 2 < 16:
            Cp(i - 2)

    bar2 = barrier()
    t_m = []
    for m in range(KD):
        b, ps, tok = lin_fm("w_conv_out_2", 0, (P * m, P), 4, lambda k: ch[:, k, :], lambda k: cl[:, k, :], 256, lambda k: t_ch[k])
        a = tt(Gt[:, 8 + m, :], Gt[:, 8 + m, :], ps, ALU.mult, [tok, t_g[8 + m]])
        B.give(b, [a])
        t_m.append(a)
    t_h2 = []
    for m in range(KD):
        b, ps, tok = lin_fm("w_attn_out_2", 0, (P * m, P), 4, lambda k: oh[:, k, :], lambda k: ol[:, k, :], 256, t_o)
        a = tt(Gt[:, m, :], Gt[:, m, :], ps, ALU.mult, [tok, t_g[m]])
        B.give(b, [a])
        a = tt(Gt[:, m, :], Gt[:, m, :], Gt[:, 8 + m, :], ALU.add, [a, t_m[m]])
        t_h2.append(split_to(hh[:, m, 0:256], hl[:, m, 0:256], Gt[:, m, :], [a, *bar2]))

    def resid_tile(m, ps, tok):
        return stt(XT[:, m, xc], XT[:, m, xc], ALPHA, ps, ALU.mult, ALU.add, [tok])

    t_r = []
    for m in range(KD):
        b, ps, tok = lin_fm("w_o_2", 0, (P * m, P), KD, X2h, X2l, 256, lambda k: t_h2[k])
        t_r.append(resid_tile(m, ps, tok))
        B.give(b, [t_r[-1]])
    tl = ln_stats(lambda k: XT[:, k, xc], KD, D, lambda k: [t_r[k]], 1)
    bar3 = barrier()
    t_x3 = []
    for k in range(KD):
        a = stt(XT[:, k, xc], XT[:, k, xc], C("l1g", k, 1), S.rs[:, 0:256], ALU.mult, ALU.mult, tl)
        a = act(XT[:, k, xc], XT[:, k, xc], ACT.Identity, [a], bias=C("l1b", k, 1))
        t_x3.append(split_to(hh[:, k, 0:256], hl[:, k, 0:256], XT[:, k, xc], [a, *bar3]))
    S.rs_rd = [DV.last()]

    HK = KF // 2
    fh, fl = S.fh, S.fl
    acc_b = [B.take(1) for _ in range(4)]
    rd_h = [None] * HK
    toks_d = None
    sgs = [AF[:, 0:256], AF[:, 256:512]]
    hs = [AF[:, 512:768], AF[:, 768:1024]]
    s_rd = [list(bar3), list(bar3)]
    h_rd = [list(bar3), list(bar3)]
    tz_b = []
    t_d = [None] * KD
    for half in range(2):
        t_f = {}
        for f in range(HK):
            m = half * HK + f
            z = f % 2
            b, ps, tok = lin_fm("w_ffn_gate_2", 0, (P * m, P), KD, X2h, X2l, 256, lambda k: t_x3[k])
            a = act(sgs[z], ps, ACT.Silu, [tok, *s_rd[z]])
            B.give(b, [a])
            b, ps, tok = lin_fm("w_ffn_up_2", 0, (P * m, P), KD, X2h, X2l, 256, lambda k: t_x3[k])
            u = tt(hs[z], sgs[z], ps, ALU.mult, [tok, a, *h_rd[z]])
            B.give(b, [u])
            s_rd[z] = [u]
            t_f[f] = split_to(fh[:, f, :], fl[:, f, :], hs[z], [u, toks_d])
            h_rd[z] = t_f[f]
        for m in range(KD):
            bk, free = acc_b[m // 2]
            ps = B.ps[:, bk * 512 + 256 * (m % 2):bk * 512 + 256 * (m % 2) + 256]
            kk = list(range(half * HK, (half + 1) * HK))
            _, _, t_d[m] = lin_fm("w_ffn_down_2", 0, (P * m, P), None, lambda k: fh[:, k - half * HK, :],
                                  lambda k: fl[:, k - half * HK, :], 256, lambda k: t_f[k - half * HK],
                                  ps=ps, kk=kk, free=free)
        toks_d = t_d[KD - 1]
        if half == 0:
            acc_b2 = []
            t_r = []
            for m in range(KD):
                bk, _ = acc_b[m // 2]
                ps = B.ps[:, bk * 512 + 256 * (m % 2):bk * 512 + 256 * (m % 2) + 256]
                t_r.append(resid_tile(m, ps, t_d[m | 1]))
            for j in range(4):
                B.give(acc_b[j][0], [t_r[2 * j], t_r[2 * j + 1]])
            acc_b = [B.take(1) for _ in range(4)]
        else:
            t_r = []
            for m in range(KD):
                bk, _ = acc_b[m // 2]
                ps = B.ps[:, bk * 512 + 256 * (m % 2):bk * 512 + 256 * (m % 2) + 256]
                t_r.append(tt(XT[:, m, xc], XT[:, m, xc], ps, ALU.add, [t_d[m | 1]]))
            for j in range(4):
                B.give(acc_b[j][0], [t_r[2 * j], t_r[2 * j + 1]])
    tl = ln_stats(lambda k: XT[:, k, xc], KD, D, lambda k: [t_r[k]], 1)
    outs = S.out.rearrange("(k p) n -> p k n", p=P)
    for k in range(KD):
        a = stt(XT[:, k, xc], XT[:, k, xc], C("l2g", k, 1), S.rs[:, 0:256], ALU.mult, ALU.mult, tl)
        a = act(XT[:, k, xc], XT[:, k, xc], ACT.Identity, [a], bias=C("l2b", k, 1))
        SP.dma(lambda e, k=k: e.dma_start(outs[:, k, :], XT[:, k, xc]), (S.s_out, 16 * (k + 1)), [a])
    SP.wait([(S.s_out, 16 * KD)])
    return W.seq


def build(nc, cpack, xin, wpack, wuq, out):
    with ExitStack() as ctx:
        S = State()

        def sb(name, shape, dt=F32):
            return ctx.enter_context(nc.sbuf_tensor(name, shape, dt))

        def sem(name):
            return ctx.enter_context(nc.semaphore(name))

        S.cpack, S.xin, S.wpack, S.wuq, S.out = cpack, xin, wpack, wuq, out
        S.NAF = 19200
        S.cst = sb("cst", [P, C_N])
        S.XT = sb("XT", [P, KD, TT])
        S.hh = sb("hh", [P, KD, TT], F32R)
        S.hl = sb("hl", [P, KD, TT], F32R)
        S.raw = sb("raw", [P, NRAW * CH])
        S.whi = sb("whi", [P, NHL * CH], F32R)
        S.wlo = sb("wlo", [P, NHL * CH], F32R)
        HB = KF // 2
        S.fh = S.hh[:, :, 256:512]
        S.xr = sb("xr", [P, 2 * 3 * 256], F32R)
        S.AF = sb("AF", [P, S.NAF])
        S.sq = sb("sq", [P, 1024])
        S.acc = sb("acc", [P, 512])
        S.rs = sb("rs", [P, 512])
        S.mod = sb("mod", [P, 96])
        S.modrow = sb("modrow", [4, 512])
        S.c32 = sb("c32", [P, 16])
        S.c4 = sb("c4", [P, 32], F32R)
        S.rtab = sb("rtab", [P, 256])
        S.ps = ctx.enter_context(nc.psum_tensor("ps", [P, 8 * 512], F32))

        class Hidden:

            def __init__(self, h, off):
                self.h, self.off = h, off

            def __getitem__(self, key):
                _, k, _ = key
                if k < 8:
                    return self.h[:, k, 256:512]
                o = self.off + (k - 8) * 256
                return S.xr[:, o:o + 256]

        S.fh, S.fl = Hidden(S.hh, 0), Hidden(S.hl, 768)
        S.ch, S.cl = S.hh[:, 0:4, 256:512], S.hl[:, 0:4, 256:512]
        S.oh, S.ol = S.hh[:, 4:8, 256:512], S.hl[:, 4:8, 256:512]

        S.s_pe, S.s_act, S.s_dve = sem("s_pe"), sem("s_act"), sem("s_dve")
        S.s_raw = [sem(f"s_raw{i}") for i in range(NRAW)]
        S.s_uq, S.s_c0, S.s_c1, S.s_x, S.s_out = sem("s_uq"), sem("s_c0"), sem("s_c1"), sem("s_x"), sem("s_out")

        plan = emit(S, None)
        assert sum(P * n for _, n, _ in plan) == WTOTAL, sum(n for _, n, _ in plan)
        emit(S, plan)

        block = ctx.enter_context(nc.Block())

        @block.sync
        def _(e):
            S.SP.run(e)

        @block.gpsimd
        def _(e):
            S.GP.run(e)

        @block.scalar
        def _(e):
            e.preload_act_table_set("natural_log_exp_and_others")
            S.ACT.run(e)

        @block.vector
        def _(e):
            S.DVE.run(e)

        @block.tensor
        def _(e):
            S.PE.run(e)
    return plan


def tables():
    f32 = np.float32
    c = {}
    i = np.arange(256)
    a = 2 * np.pi * np.outer(i, i) / 256
    c["c256"] = (np.cos(a) / 128).astype(f32).reshape(2, 128, 256).transpose(1, 0, 2)
    c["s256"] = (-np.sin(a) / 128).astype(f32).reshape(2, 128, 256).transpose(1, 0, 2)
    j = np.arange(64)
    b = 2 * np.pi * np.outer(j, j) / 64
    for nm, m in (("c64", np.cos(b)), ("s64", np.sin(b))):
        z = np.zeros((128, 128), f32)
        z[:64, :64] = m
        z[64:, 64:] = m
        c[nm] = z
    c["ones"] = np.ones((128, 128), f32)
    c["ident"] = np.eye(128, dtype=f32)
    half = 16
    inv = (f32(10000.0) ** (-np.arange(0, half, 2, dtype=f32) / f32(half))).astype(f32)
    row = np.repeat(np.arange(4, dtype=f32), 64)
    col = np.tile(np.arange(64, dtype=f32), 4)
    ar, ac = (row[:, None] * inv[None]).astype(f32), (col[:, None] * inv[None]).astype(f32)
    ang = np.concatenate([ar, ar, ac, ac], -1)
    sgn = np.tile(np.repeat(np.array([-1, 1], f32), 8), 2)
    c["cos1"] = np.cos(ang).astype(f32).reshape(2, 128, 32).transpose(1, 0, 2)
    c["sin1"] = (np.sin(ang).astype(f32) * sgn).reshape(2, 128, 32).transpose(1, 0, 2)
    inv2 = (1.0 / (f32(10000.0) ** (np.arange(0, 64, 2, dtype=f32) / f32(64)))).astype(f32)
    ang2 = (np.arange(256, dtype=f32)[:, None] * inv2[None]).astype(f32)
    c["cos2"] = np.cos(ang2).astype(f32).reshape(2, 128, 32).transpose(1, 0, 2)
    c["sin2"] = np.sin(ang2).astype(f32).reshape(2, 128, 32).transpose(1, 0, 2)
    c["nsin2"] = -c["sin2"]
    t, s = np.arange(256)[:, None], np.arange(256)[None, :]
    m = []
    for win, dil in ((128, 1), (512, 4), (2048, 16)):
        ok = (t >= s) & ((t - s) % dil == 0) & ((t - s) <= win)
        m.append(np.where(ok, 0.0, NEG).astype(f32))
    c["mask1"] = np.stack([x[128:, :] for x in m], 1)
    e = np.zeros((128, 4), f32)
    e[:, 0], e[:, 1], e[:, 2] = EPS, LN_EPS, -0.5 * math.log(96.0)
    c["eps"] = e
    z = np.zeros((128, 2), f32)
    z[0, 0] = z[1, 1] = z[2, 0] = z[3, 1] = 1.0
    c["sel"] = z
    return c


def kernel(**inputs):
    import concourse.bacc as _bacc
    from concourse.bass_utils import run_bass_kernel_spmd as _run

    I = {k: np.asarray(v) for k, v in inputs.items()}
    f32 = np.float32

    nc = _bacc.Bacc("TRN2", target_bir_lowering=False, num_devices=1)
    ci = nc.dram_tensor("cpack", (P, C_N), F32, kind="ExternalInput").ap()
    xi = nc.dram_tensor("xin", (P, KD * TT), F32, kind="ExternalInput").ap()
    wi = nc.dram_tensor("wpack", (WTOTAL,), F32, kind="ExternalInput").ap()
    ui = nc.dram_tensor("wuq", (2, P, 1536), F32, kind="ExternalInput").ap()
    oo = nc.dram_tensor("out", (D, T), F32, kind="ExternalOutput").ap()
    plan = build(nc, ci, xi, wi, ui, oo)

    def cols(v, n):
        return v.reshape(n, P).T

    def rows(v):
        return np.broadcast_to(v.reshape(1, -1), (P, v.size))

    c = tables()
    c["cvec"] = np.stack([cols(I["c_ctx"], 8), cols(I["c"][0], 8)], 2)
    c["bmod"] = np.concatenate([cols(I["b_mod"][l], 24) for l in range(2)], 1)
    c["ng"] = np.concatenate([cols(I["norm_g"][l], 8) for l in range(2)], 1)
    c["qag"] = np.concatenate([cols(I["q_a_g"][l], 2) for l in range(2)], 1)
    c["kvag"] = np.concatenate([cols(I["kv_a_g"][l], 1) for l in range(2)], 1)
    for nm, src in (("gq", "q_norm_g"), ("gk", "k_norm_g")):
        z = np.ones((P, 2), f32)
        z[:64, :] = I[src][:, :64].T
        c[nm] = z
        c[nm + "r"] = np.concatenate([rows(I[src][l, 64:]) for l in range(2)], 1)
    c["lng"] = np.concatenate([rows(I["g_ln_g"][l]) for l in range(2)], 1)
    c["bs"] = np.stack([np.repeat(I["g_bs"][l, 2 * m:2 * m + 2], 64, 0) for l in range(2) for m in range(2)], 1)
    c["convw"] = I["conv_w_2"][0].T.reshape(4, P, 31).transpose(1, 0, 2)
    c["convb"] = cols(I["conv_b_2"][0], 4)
    c["cg"], c["cb"] = cols(I["conv_ln_g_2"][0], 4), cols(I["conv_ln_b_2"][0], 4)
    c["l1g"], c["l1b"] = cols(I["ln1_g_2"][0], 8), cols(I["ln1_b_2"][0], 8)
    c["l2g"], c["l2b"] = cols(I["ln2_g_2"][0], 8), cols(I["ln2_b_2"][0], 8)
    cpack = np.zeros((P, C_N), f32)
    for nm, (off, n) in C_AT.items():
        cpack[:, off:off + n] = np.asarray(c[nm]).reshape(P, n)

    xin = np.concatenate([I["ctx"][0].T, I["x"][0].T], 1).reshape(KD, P, TT).transpose(1, 0, 2).reshape(P, KD * TT)

    kvc = np.concatenate([np.arange(h * 128, h * 128 + 64) for h in range(8)] + [np.arange(h * 128 + 64, h * 128 + 128) for h in range(8)])
    gvkr = np.concatenate([np.arange(768, 1024), np.arange(1664, 1696)])
    wpack = np.empty(WTOTAL, f32)
    at = 0
    for (name, l, ks, cc), n, _ in plan:
        if name == "g_ws":
            blk = I[name][l].transpose(2, 0, 1)
        else:
            w = I[name][l]
            if name == "w_ukv":
                w = w[:, kvc]
            blk = w.reshape(-1, P, w.shape[1])[ks[0]:ks[-1] + 1]
            if cc[0] == ("gvkr",):
                blk = blk[:, :, gvkr]
            else:
                blk = blk[:, :, cc[0]:cc[0] + cc[1]]
            blk = blk.transpose(1, 0, 2)
        wpack[at:at + P * n] = blk.reshape(-1)
        at += P * n
    assert at == WTOTAL

    r = _run(nc, [{"cpack": cpack, "xin": np.ascontiguousarray(xin), "wpack": wpack,
                    "wuq": np.ascontiguousarray(I["w_uq"].reshape(2, 2, P, 768).transpose(0, 2, 1, 3).reshape(2, P, 1536))}], core_ids=[0])
    y = r.results[0]["out"]
    return np.ascontiguousarray(y.T).reshape(1, T, D)
```

```python
import math
from contextlib import ExitStack

import numpy as np
import concourse.bass as bass
from concourse import mybir

F32 = mybir.dt.float32
F32R = mybir.dt.float32r
I32 = mybir.dt.int32
ALU = mybir.AluOpType
ACT = mybir.ActivationFunctionType
AX = mybir.AxisListType

P = 128
D = 1024
T = 256
TT = 512
KD = D // P
FF = 2816
KF = FF // P
EPS = 1e-6
LN_EPS = 1e-5
ALPHA = 2.0 ** 0.25
NRAW = 4
NHL = 4
CH = 1024
NEG = -1.0e30
WTOTAL = 128 * 248320


def const_layout():
    items = [
        ("cvec", 8 * 2), ("bmod", 2 * 24), ("ng", 2 * 8), ("eps", 4), ("sel", 2),
        ("ones", 128), ("ident", 128),
        ("c64", 128), ("s64", 128), ("c256", 512), ("s256", 512),
        ("qag", 2 * 2), ("kvag", 2), ("gq", 2), ("gk", 2), ("gqr", 2 * 32), ("gkr", 2 * 32),
        ("cos1", 2 * 32), ("sin1", 2 * 32), ("lng", 2 * 64), ("bs", 2 * 2 * 128),
        ("cos2", 2 * 32), ("sin2", 2 * 32), ("nsin2", 2 * 32), ("convw", 4 * 31), ("convb", 4), ("cg", 4), ("cb", 4),
        ("l1g", 8), ("l1b", 8), ("l2g", 8), ("l2b", 8),
        ("mask1", 3 * 256),
    ]
    at, off = {}, 0
    for name, n in items:
        at[name] = (off, n)
        off += n
    return at, off


C_AT, C_N = const_layout()
C_EARLY = C_AT["c64"][0]
C2_FROM, C2_TO = C_AT["cos2"][0], C_AT["c64"][0]
C_SB = C_AT["cos2"][0]
assert C_N - C2_FROM <= C_AT["qag"][0] - C2_TO


class Lane:

    def __init__(self, sem):
        self.sem, self.n, self.q, self.seen = sem, 0, [], {}

    def wait(self, toks):
        for t in toks:
            if t is None:
                continue
            sem, v = t
            if self.seen.get(sem.name, 0) < v:
                self.seen[sem.name] = v
                self.q.append(("w", sem, v))

    def quiet(self, fn, after=()):
        self.wait(after)
        self.q.append(("i", fn, None, 0))

    def __call__(self, fn, after=()):
        self.wait(after)
        self.n += 1
        self.q.append(("i", fn, self.sem, 1))
        return (self.sem, self.n)

    def dma(self, fn, tok, after=()):
        self.wait(after)
        self.q.append(("i", fn, tok[0], 16))
        return tok

    def last(self):
        return (self.sem, self.n)

    def run(self, e):
        for x in self.q:
            if x[0] == "w":
                e.wait_ge(x[1], x[2])
            else:
                i = x[1](e)
                if x[2] is not None:
                    i.then_inc(x[2], x[3])


class Banks:

    def __init__(self, ps):
        self.ps, self.free, self.held, self.i = ps, [()] * 8, [False] * 8, 0

    def take(self, n=1):
        for _ in range(16):
            i = self.i % 8
            if i + n <= 8 and not any(self.held[i:i + n]):
                self.i = i + n
                for j in range(i, i + n):
                    self.held[j] = True
                return i, [t for j in range(i, i + n) for t in self.free[j]]
            self.i += 1
        raise RuntimeError("no PSUM bank is free")

    def give(self, i, toks, n=1):
        for j in range(i, i + n):
            self.held[j] = False
            self.free[j] = tuple(toks)

    def ap(self, i, n=512):
        return self.ps[:, i * 512:i * 512 + n]


class Stream:

    def __init__(self, S, plan):
        self.S, self.plan, self.seq = S, plan, []
        self.loaded = self.prepped = self.split = 0
        self.rel = {}
        self.relsplit = {}
        self.ready = {}
        self.off = 0

    def advance(self):
        S = self.S
        while self.loaded < len(self.plan):
            i = self.loaded
            if i >= NRAW and (i - NRAW) not in self.rel:
                break
            _, n, _ = self.plan[i]
            slot, off = i % NRAW, self.off
            dst, src = S.raw[:, slot * CH:slot * CH + n], S.wpack[off:off + P * n].rearrange("(p n) -> p n", n=n)
            tok = (S.s_raw[slot], 16 * (i // NRAW + 1))
            S.SP.dma(lambda e, d=dst, s=src: e.dma_start(d, s), tok, [self.rel.get(i - NRAW)])
            self.off += P * n
            self.loaded += 1
        while self.prepped < self.loaded:
            i = self.prepped
            _, n, sp = self.plan[i]
            slot = i % NRAW
            tok = (S.s_raw[slot], 16 * (i // NRAW + 1))
            if not sp:
                self.ready[i] = ([tok], None)
            else:
                j = self.split
                if j >= NHL and (j - NHL) not in self.relsplit:
                    break
                h = j % NHL
                raw = S.raw[:, slot * CH:slot * CH + n]
                hi, lo = S.whi[:, h * CH:h * CH + n], S.wlo[:, h * CH:h * CH + n]
                used = self.relsplit.get(j - NHL)
                t1 = S.ACT(lambda e, o=hi, x=raw: e.activation(o, x, ACT.Copy), [tok, used])
                t2 = S.DVE(lambda e, o=lo, x=raw, y=hi: e.tensor_tensor(o, x, y, ALU.subtract), [tok, t1])
                self.rel[i] = t2
                self.ready[i] = ([t1, t2], j)
                self.split += 1
            self.prepped += 1

    def get(self, desc, n, split=True):
        i = len(self.seq)
        self.seq.append((desc, n, split))
        if self.plan is None:
            z = self.S.raw[:, 0:n]
            return (z, z if split else None), [], i
        self.advance()
        toks, j = self.ready[i]
        if j is None:
            s = i % NRAW
            return (self.S.raw[:, s * CH:s * CH + n], None), toks, i
        h = j % NHL
        return (self.S.whi[:, h * CH:h * CH + n], self.S.wlo[:, h * CH:h * CH + n]), toks, i

    def done(self, i, tok):
        if self.plan is None:
            return
        j = self.ready[i][1]
        if j is None:
            self.rel[i] = tok
        else:
            self.relsplit[j] = tok




class State:
    pass


def emit(S, plan):
    PE, AC, DV, SP, GP = Lane(S.s_pe), Lane(S.s_act), Lane(S.s_dve), Lane(S.s_c0), Lane(S.s_uq)
    S.GP = GP
    S.PE, S.ACT, S.DVE, S.SP = PE, AC, DV, SP
    W = Stream(S, plan)
    B = Banks(S.ps)
    XT, hh, hl = S.XT, S.hh, S.hl
    AF = S.AF

    def C(name, a=0, n=None, parts=P):
        off, m = C_AT[name]
        if off >= C2_FROM:
            off += C2_TO - C2_FROM
        return S.cst[0:parts, off + a:off + a + (m - a if n is None else n)]

    def mm(out, lhsT, rhs, start, stop, after=(), inc=False):
        f = lambda e: e.matmul(out, lhsT, rhs, start=start, stop=stop, skip_group_check=True)
        if inc:
            return PE(f, after)
        PE.quiet(f, after)

    def act(out, in_, func=ACT.Copy, after=(), **kw):
        return AC(lambda e: e.activation(out, in_, func, **kw), after)

    def tt(out, a, b, op, after=()):
        return DV(lambda e: e.tensor_tensor(out, a, b, op), after)

    def stt(out, a, s, b, op0, op1, after=()):
        return DV(lambda e: e.scalar_tensor_tensor(out=out, in0=a, scalar=s, in1=b, op0=op0, op1=op1), after)

    def ts(out, a, s1, s2, op0, op1, after=()):
        return DV(lambda e: e.tensor_scalar(out, a, s1, s2, op0, op1), after)

    def rsum(out, in_, after=()):
        return DV(lambda e: e.tensor_reduce(out, in_, AX.X, ALU.add), after)

    def dcopy(out, in_, after=()):
        return DV(lambda e: e.tensor_copy(out, in_), after)

    def transpose(out, in_, after=()):
        return PE(lambda e: e.transpose(out, in_, C("ident")), after)

    def split_to(hi, lo, src, after=()):
        t = act(hi, src, after=after)
        u = tt(lo, src, hi, ALU.subtract, [*after, t])
        return [t, u]

    def barrier():
        return [PE.last(), AC.last(), DV.last()]

    t_c0 = SP.dma(lambda e: e.dma_start(S.cst[:, 0:C_EARLY], S.cpack[:, 0:C_EARLY]), (S.s_c0, 16))
    if plan is not None:
        W.advance()
    t_x = AC.dma(lambda e: e.dma_start(XT[:, :, :], S.xin.rearrange("p (k n) -> p k n", k=KD)), (S.s_x, 16))
    t_c1 = AC.dma(lambda e: e.dma_start(S.cst[:, C_EARLY:C_SB], S.cpack[:, C_EARLY:C_SB]), (S.s_c1, 16))

    def lin_fm(wname, l, cols, K, xh, xl, N, xtoks, ps=None, kk=None, start=True, stop=True, free=()):
        if ps is None:
            b, free = B.take()
            ps = B.ap(b, N)
        else:
            b = None
        kk = list(range(K)) if kk is None else kk
        tok = None
        groups = [kk[i:i + 8] for i in range(0, len(kk), 8)]
        for g in groups:
            (whi, wlo), toks, ci = W.get((wname, l, tuple(g), tuple(cols)), len(g) * P)
            for j, k in enumerate(g):
                wh, wl = whi[:, j * P:(j + 1) * P], wlo[:, j * P:(j + 1) * P]
                xt = list(xtoks(k)) if callable(xtoks) else list(xtoks)
                first, last = start and k == kk[0], stop and k == kk[-1]
                mm(ps, wh, xh(k), first, False, [*toks, *free, *xt])
                mm(ps, wh, xl(k), False, False)
                if k == g[-1]:
                    tok = mm(ps, wl, xh(k), False, last, inc=True)
                else:
                    mm(ps, wl, xh(k), False, last)
            W.done(ci, tok)
        return b, ps, tok

    def lin_tm(wname, l, c0, ncols, xh, xl, toks_of, tiles, per, xtoks, cut=None):
        bs = {t: B.take() for t in tiles}
        k = 0
        while k < KD:
            g = list(range(k, min(k + per, KD)))
            (whi, wlo), toks, ci = W.get((wname, l, tuple(g), (c0, ncols)), len(g) * ncols)
            for j, kk in enumerate(g):
                xt = list(xtoks(kk)) if callable(xtoks) else list(xtoks)
                for t in tiles:
                    lo_c = cut(t) if cut else 0
                    wh, wl = (w[:, j * ncols + lo_c:(j + 1) * ncols] for w in (whi, wlo))
                    o = B.ps[:, bs[t][0] * 512 + lo_c:bs[t][0] * 512 + ncols]
                    ts_ = toks_of(t)
                    mm(o, xh(kk)[:, ts_], wh, kk == 0, False, [*toks, *bs[t][1], *xt])
                    mm(o, xh(kk)[:, ts_], wl, False, False)
                    tok = mm(o, xl(kk)[:, ts_], wh, False, kk == KD - 1, inc=True)
            W.done(ci, tok)
            k += per
        return {t: bs[t][0] for t in tiles}, tok

    t = act(S.c32[:, 0:16], C("cvec"), ACT.Silu, [t_c0])
    c32 = S.c32[:, 0:16].rearrange("p (k s) -> p k s", s=2)
    c4 = S.c4[:, :].rearrange("p (k s) -> p k s", s=4)
    t1 = act(c4[:, :, 0:2], c32, after=[t])
    t_c4 = [t1, tt(c4[:, :, 2:4], c32, c4[:, :, 0:2], ALU.subtract, [t, t1])]
    modt = {}
    mod_rd = [None, None]
    modc = [0]

    def modulation(l, n):
        b, free = B.take()
        ps = B.ps[0:4, b * 512:b * 512 + 512]
        for g in range(4):
            (whi, wlo), toks, ci = W.get(("w_mod", l, (2 * g, 2 * g + 1), (512 * n, 512)), 1024)
            for j in range(2):
                k = 2 * g + j
                mm(ps, c4[:, k, :], whi[:, j * 512:(j + 1) * 512], k == 0, False, [*toks, *free, *t_c4])
                tok = mm(ps, c4[:, k, :], wlo[:, j * 512:(j + 1) * 512], False, k == 7, inc=(j == 1))
            W.done(ci, tok)
        z = 0
        row = S.modrow[0:4, :]
        t = act(row, ps, after=[tok, mod_rd[z]])
        B.give(b, [t])
        b, free = B.take()
        for j in range(4):
            tok = mm(B.ps[:, b * 512 + 2 * j:b * 512 + 2 * j + 2], row[:, j * P:(j + 1) * P],
                     C("sel", parts=4), True, True, [t, *free], inc=(j == 3))
        mod_rd[z] = tok
        o = S.mod[:, l * 48 + 8 * n:l * 48 + 8 * n + 8].rearrange("p (j s) -> p j s", s=2)
        bm = C("bmod", 24 * l + 4 * n, 4).unsqueeze(2).broadcast_to([P, 4, 2])
        t = tt(o, B.ap(b, 8).rearrange("p (j s) -> p j s", s=2), bm, ALU.add, [tok])
        B.give(b, [t])
        if n in (2, 3):
            ng = C("ng", 8 * l + 4 * (n - 2), 4).unsqueeze(2).broadcast_to([P, 4, 2])
            t = stt(o, o, 1.0, ng, ALU.add, ALU.mult, [t])
        modt[(l, n)] = t

    def modv(l, what, k, s):
        n = what * 2 + k // 4
        c = l * 48 + 8 * n + 2 * (k % 4) + s
        return S.mod[:, c:c + 1], modt[(l, n)]

    def rsqrt(v, u, w, after):
        y = u
        t = ts(y.bitcast(I32), v.bitcast(I32), -0.5, 1597463007.0, ALU.mult, ALU.add, after)
        for i in range(3):
            t = tt(w, y, y, ALU.mult, [t])
            t = stt(w, w, -0.5, v, ALU.mult, ALU.mult, [t])
            t = stt(v if i == 2 else y, w, 1.5, y, ALU.add, ALU.mult, [t])
        return t

    def acc_add(src, first, after):
        n = src.free_size()
        a = S.acc[:, 0:n]
        if first:
            S.acc_t = dcopy(a, src, [*after, *S.acc_rd])
        else:
            S.acc_t = tt(a, a, src, ALU.add, [*after, S.acc_t])
        return S.acc_t

    def square_add(src, first, z, after):
        n = src.free_size()
        sq = S.sq[:, z * 512:z * 512 + n]
        t = act(sq, src, ACT.Square, [*after, S.sq_rd[z]])
        S.sq_rd[z] = acc_add(sq, first, [t])

    def rstd_wide(n, nfeat, eps):
        nt = n // P
        b, free = B.take()
        for j in range(nt):
            tok = mm(B.ps[:, b * 512 + j:b * 512 + j + 1], S.acc[:, j * P:(j + 1) * P], C("ones", 0, 1), True, True,
                     [S.acc_t, *free], inc=(j == nt - 1))
        S.acc_rd = [tok]
        v, u, w = (S.nrm[:, 4 * i:4 * i + nt] for i in range(3))
        t = ts(v, B.ap(b, nt), 1.0 / nfeat, eps, ALU.mult, ALU.add, [tok])
        B.give(b, [t])
        t = rsqrt(v, u, w, [t])
        dg = S.rs[:, 0:n].rearrange("p (t n) -> p t n", n=P)
        t = tt(dg, C("ident").unsqueeze(1).broadcast_to([P, nt, P]), v.unsqueeze(2).broadcast_to([P, nt, P]),
               ALU.mult, [t, *S.rs_rd])
        b, free = B.take()
        tok = mm(B.ap(b, n), C("ones"), S.rs[:, 0:n], True, True, [t, *free], inc=True)
        S.rs_rd = [tok]
        return b, tok

    def make_h(l, b, tr):
        toks = []
        bar = barrier()
        for k in range(KD):
            out = []
            for s in range(2):
                c = slice(256 * s, 256 * s + 256)
                A, ta = modv(l, 1, k, s)
                sh, tb = modv(l, 0, k, s)
                z = (2 * k + s) % 4
                tmp = S.sq[:, z * 256:(z + 1) * 256]
                t = stt(tmp, XT[:, k, c], A, B.ap(b)[:, c], ALU.mult, ALU.mult, [tr, ta, *bar, S.tmp_rd[z]])
                u = act(hh[:, k, c], tmp, ACT.Identity, [t, tb], bias=sh)
                out.append((tmp, sh, hh[:, k, c], hl[:, k, c], z, u))
            for tmp, sh, oh_, ol_, z, u in out:
                v = stt(ol_, tmp, sh, oh_, ALU.add, ALU.subtract, [u])
                S.tmp_rd[z] = v
            toks.append([u, v])
        B.give(b, [v])
        S.sq_rd = [v, v]
        return toks

    S.mean_rd = []
    S.sq_rd, S.acc_rd, S.rs_rd, S.tmp_rd, S.acc_t = [None, None], [], [], [None] * 4, None

    S.x2 = [None] * KD
    for k in range(KD):
        square_add(XT[:, k, :], k == 0, k % 2, [t_x])
    for n in (2, 3):
        modulation(0, n)
    br, tr = rstd_wide(TT, D, EPS)
    for n in (0, 1):
        modulation(0, n)

    t_x2 = [None] * KD
    for l in range(2):
        ns = 2 if l == 0 else 1
        x0 = 0 if l == 0 else 256
        N = TT - x0
        cs = slice(x0, TT)
        tiles = list(range(x0 // P, 4))
        t_h = make_h(l, br, tr)
        bar = barrier()
        t_uq = GP.dma(lambda e, l=l: e.dma_start(S.uq[:, :], S.wuq[l]), (S.s_uq, 16 * (2 * l + 1)), bar)
        uq = S.uq

        o = 0

        def area(n):
            nonlocal o
            a = AF[:, o:o + n]
            o += n
            return a

        fg = area(2 * TT).rearrange("p (k n) -> p k n", k=2)
        ug = area(2 * TT).rearrange("p (k n) -> p k n", k=2)
        ag = area(4 * TT).rearrange("p (k n) -> p k n", k=4)
        ckv = area(TT)
        gv = area(1024)
        Pb = area(3 * 512)
        kr = area(4 * 32)
        cq = area(2 * TT).rearrange("p (k n) -> p k n", k=2)
        tq = area(2 * 768)
        stat = area(144)
        V = area(4 * 512).rearrange("p (t n) -> p t n", t=4)
        Q = area(2 * 1024)
        PT = area(2 * 512)
        ko = o
        K = area(8 * TT).rearrange("p (h n) -> p h n", h=8)
        end = o
        o = ko
        fi = area(2 * TT).rearrange("p (k n) -> p k n", k=2)
        W12 = area(1024).rearrange("p (c k n) -> p c k n", c=2, k=2)
        Vf = area(4 * 512).rearrange("p (t n) -> p t n", t=4)
        assert max(o, end) <= S.NAF, max(o, end)
        wkv = Pb[:, 512:1536]
        sqqs = {1: AF[:, 4608:4608 + 1536], 0: AF[:, 4096:4096 + 1536]}
        gsq = V[:, 0:2, :].rearrange("p t n -> p (t n)")
        t_ukv = GP.dma(lambda e, l=l, w=wkv: e.dma_start(w, S.wukv[l]), (S.s_uq, 16 * (2 * l + 2)), bar)
        xh, xl = (lambda k: hh[:, k, cs]), (lambda k: hl[:, k, cs])
        XH, XL = (lambda k: hh[:, k, :]), (lambda k: hl[:, k, :])
        ht = lambda k: t_h[k]
        off = {}
        c0 = 0
        for nm, w in (("fin", 256), ("fgate", 256), ("gu", 256), ("gv", 256), ("ggate", 256), ("cq", 256), ("ckv", 128), ("kr", 32), ("agate", 512)):
            off[nm] = c0
            c0 += w

        def inp(nm, m, full=False):
            return lin_fm("w_in", l, (off[nm] + P * m, P), KD, XH if full else xh, XL if full else xl,
                          TT if full else N, ht)

        t_fi = []
        for m in range(2):
            b, ps, tok = inp("fin", m)
            t = act(fi[:, m, cs], ps, after=[tok, *bar])
            B.give(b, [t])
            t_fi.append(t)
        (wf, _), toks, ci = W.get(("w_fmix", l, (0, 1), (0, 256)), 512, split=False)
        for c, nm in enumerate(("c64", "s64")):
            b, free = B.take()
            tok = mm(B.ap(b), C(nm), wf, True, True, [*toks, *free, t_c1], inc=True)
            t = act(W12[:, c, :, :], B.ap(b).rearrange("p (k n) -> p k n", k=2), after=[tok, *bar])
            B.give(b, [t])
        W.done(ci, tok)
        t_w12 = t
        t_fg, t_ug, t_ag = {}, {}, {}

        def f_gate(m):
            b, ps, tok = inp("fgate", m)
            t = act(fg[:, m, cs], ps, ACT.Silu, [tok, *bar])
            B.give(b, [t])
            t_fg[m] = t

        def g_gate(m):
            b, ps, tok = inp("ggate", m)
            t = act(ug[:, m, cs], ps, ACT.Silu, [tok, *bar])
            B.give(b, [t])
            t_ug[m] = t

        def g_u(m):
            b, ps, tok = inp("gu", m)
            u = tt(ug[:, m, cs], ug[:, m, cs], ps, ALU.mult, [tok, t_ug[m]])
            B.give(b, [u])
            t_ug[m] = u

        def a_gate(m):
            b, ps, tok = inp("agate", m)
            t = act(ag[:, m, cs], ps, ACT.Silu, [tok, *bar])
            B.give(b, [t])
            t_ag[m] = t

        f_gate(0)
        t_vf = {}
        for t in tiles:
            b, free = B.take()
            for m in range(2):
                tok = mm(B.ap(b).rearrange("p (c n) -> p c n", c=2), fi[:, m, t * P:(t + 1) * P], W12[:, :, m, :],
                         m == 0, m == 1, [t_w12, *t_fi, *free], inc=(m == 1))
            t_vf[t] = dcopy(Vf[:, t, :], B.ap(b), [tok, *bar])
            B.give(b, [t_vf[t]])
        f_gate(1)
        for m in range(2):
            b, free = B.take()
            for s in range(2 if l == 0 else 1):
                q = s if l == 0 else 1
                for t in range(2):
                    tk = 2 * q + t
                    o_ = B.ps[:, b * 512 + 256 * s:b * 512 + 256 * s + 256]
                    mm(o_, Vf[:, tk, m * P:(m + 1) * P], C("c256", 256 * t, 256), t == 0, False, [t_vf[tk], *free])
                    tok = mm(o_, Vf[:, tk, 256 + m * P:256 + (m + 1) * P], C("s256", 256 * t, 256), False, t == 1, inc=True)
            t_fg[m] = tt(fg[:, m, cs], B.ap(b, N), fg[:, m, cs], ALU.mult, [tok, t_fg[m]])
            B.give(b, [t_fg[m]])
        kbar = [PE.last(), *t_vf.values()]

        sqb = S.sq
        b_st, free_st = B.take()
        t_sq = []
        for m in range(2):
            b, ps, tok = inp("cq", m)
            t = act(cq[:, m, cs], ps, after=[tok, t_c1, *bar], scale=C("qag", 2 * l + m, 1))
            u = act(sqb[:, m * 512:m * 512 + N], ps, ACT.Square, [tok, *S.sq_rd])
            B.give(b, [u])
            t_sq.append(u)
        t_cq = [t]
        b, ps, tokc = inp("ckv", 0, True)
        t_ck = act(ckv, ps, after=[tokc, *bar], scale=C("kvag", l, 1))
        for t in tiles:
            for m in range(2):
                j = (t - tiles[0]) * P
                tok = mm(B.ps[:, b_st * 512 + t:b_st * 512 + t + 1], sqb[:, m * 512 + j:m * 512 + j + P],
                         C("ones", 0, 1), m == 0, m == 1, [*t_sq, *free_st], inc=(m == 1))
        u = act(sqb[:, 0:512], ps, ACT.Square, [tokc, tok])
        B.give(b, [u])

        gb, tok = lin_tm("w_in", l, ("gvkr",), 288, XH, XL, lambda t: slice(t * P, (t + 1) * P), list(range(4)), 3, ht,
                         cut=lambda t: 0 if t in tiles else 256)
        for t in range(4):
            tk = mm(B.ps[:, b_st * 512 + 4 + t:b_st * 512 + 5 + t], sqb[:, t * P:(t + 1) * P],
                    C("ones", 0, 1), True, True, [u], inc=(t == 3))
        S.sq_rd = [tk, tk]
        S.tmp_rd = [tk] * 4
        st8, s8u, s8w = stat[:, tiles[0]:8], stat[:, 120 + tiles[0]:128], stat[:, 128 + tiles[0]:136]
        t = ts(stat[:, tiles[0]:4], B.ps[:, b_st * 512 + tiles[0]:b_st * 512 + 4], 1.0 / 256, EPS, ALU.mult, ALU.add, [tk, *bar])
        t = ts(stat[:, 4:8], B.ps[:, b_st * 512 + 4:b_st * 512 + 8], 1.0 / 128, EPS, ALU.mult, ALU.add, [tk, *bar])
        B.give(b_st, [t])
        t_stat = rsqrt(st8, s8u, s8w, [t])
        for t in range(4):
            pb = B.ap(gb[t])
            u = act(kr[:, t * 32:(t + 1) * 32], pb[:, 256:288], after=[tok, *bar])
            if t in tiles:
                u = act(gv[:, t * 256:(t + 1) * 256], pb[:, 0:256], after=[tok, *bar])
            B.give(gb[t], [u])
        t_gv = [u]

        rt = {}
        for i, nm in enumerate(("gqr", "gkr")):
            g32 = C(nm, 32 * l, 32)
            tab = S.rtab[:, i * 128:(i + 1) * 128]
            gc = tab[:, 0:64].rearrange("p (t n) -> p t n", t=2)
            gs = tab[:, 64:128].rearrange("p (t a b n) -> p t a b n", t=2, a=2, b=2)
            gr = g32.rearrange("p (a b n) -> p a b n", a=2, b=2)
            sn = C("sin1").rearrange("p (t a b n) -> p t a b n", t=2, a=2, b=2)
            a = tt(gc, C("cos1").rearrange("p (t n) -> p t n", t=2), g32.unsqueeze(1).broadcast_to([P, 2, 32]),
                   ALU.mult, [t_c1, *bar])
            for hf in range(2):
                for t_ in range(2):
                    a = tt(gs[:, t_, :, hf, :], sn[:, t_, :, hf, :], gr[:, :, 1 - hf, :], ALU.mult, [a])
            rt[i] = (tab, g32, a)

        def gv_norm():
            G = gv[:, tiles[0] * 256:1024].rearrange("p (g d) -> p g d", d=64)
            G2 = gsq[:, tiles[0] * 256:1024].rearrange("p (g d) -> p g d", d=64)
            n = 4 * len(tiles)
            mu, va, vu, vw = (stat[:, 16 * i:16 * i + n] for i in (1, 2, 4, 5))
            t = rsum(mu, G, [*t_gv, *bar])
            t = ts(mu, mu, -1.0 / 64, None, ALU.mult, ALU.bypass, [t])
            t = tt(G, G, mu.unsqueeze(2).broadcast_to([P, n, 64]), ALU.add, [t])
            u = act(G2, G, ACT.Square, [t, *bar])
            yield
            u = rsum(va, G2, [u])
            u = ts(va, va, 1.0 / 64, EPS, ALU.mult, ALU.add, [u])
            u = rsqrt(va, vu, vw, [u])
            t = tt(G, G, va.unsqueeze(2).broadcast_to([P, n, 64]), ALU.mult, [t, u])
            S.t_ln = tt(G, G, C("lng", 64 * l, 64).unsqueeze(1).broadcast_to([P, n, 64]), ALU.mult, [t, t_c1])

        def spatial():
            (ws, _), toks, ci = W.get(("g_ws", l, (0, 1, 2, 3), (0, 128)), 512, split=False)
            for m in range(2):
                b, free = B.take()
                for t in tiles:
                    j = t - tiles[0]
                    for h2 in range(2):
                        h = 2 * m + h2
                        tok = mm(B.ps[64 * h2:64 * h2 + 64, b * 512 + j * P:b * 512 + (j + 1) * P],
                                 gv[:, t * 256 + h * 64:t * 256 + h * 64 + 64], ws[:, h * P:(h + 1) * P],
                                 True, True, [S.t_ln, *toks, *free], inc=True)
                go = S.rs[:, 0:N]
                bs = C("bs", (2 * l + m) * P, P).unsqueeze(1).broadcast_to([P, len(tiles), P])
                t = tt(go.rearrange("p (t n) -> p t n", n=P), B.ap(b, N).rearrange("p (t n) -> p t n", n=P), bs, ALU.add,
                       [tok, *S.rs_rd])
                B.give(b, [t])
                t_ug[m] = tt(ug[:, m, cs], go, ug[:, m, cs], ALU.mult, [t, t_ug[m]])
                S.rs_rd = [t_ug[m]]
            W.done(ci, tok)
            sq_free[0] = [tok]

        sq_free = [[]]
        X_free = [[]]
        Q_free = [[], []]
        t_K, t_V, qq = {}, {}, {}

        def norm_rope(i, t0, ready, scaled):
            X, sqq = tq, sqqs[i]
            Xg = X.rearrange("p (g d) -> p g d", d=96)
            ss, su, sw = stat[:, 48:64], stat[:, 96:112], stat[:, 112:128]
            a = act(sqq, X, ACT.Square, [*ready, *sq_free[0]])
            yield
            a = rsum(ss, sqq.rearrange("p (g d) -> p g d", d=96), [a])
            k = 96.0 if scaled else 1.0
            a = ts(ss, ss, k / 96, EPS * k, ALU.mult, ALU.add, [a])
            a = rsqrt(ss, su, sw, [a])
            a = tt(Xg, Xg, ss.unsqueeze(2).broadcast_to([P, 16, 96]), ALU.mult, [a])
            yield
            tab, g32, tk = rt[i]
            R = Xg[:, :, 64:96]
            if t0 >= 2:
                for y in range(2):
                    Ry = R[:, 8 * y:8 * y + 8, :]
                    R1 = sqq[:, 512 * y:512 * y + 256].rearrange("p (h n) -> p h n", h=8)
                    R2 = sqq[:, 512 * y + 256:512 * y + 512].rearrange("p (h n) -> p h n", h=8)
                    gc = tab[:, 32 * y:32 * y + 32].unsqueeze(1).broadcast_to([P, 8, 32])
                    gs = tab[:, 64 + 32 * y:96 + 32 * y].rearrange("p (a b n) -> p a b n", a=2, b=2)
                    u = tt(R1, Ry, gc, ALU.mult, [a, tk])
                    for ax in range(2):
                        for hf in range(2):
                            v = tt(R2[:, :, 16 * ax + 8 * hf:16 * ax + 8 * hf + 8],
                                   Ry[:, :, 16 * ax + 8 * (1 - hf):16 * ax + 8 * (1 - hf) + 8],
                                   gs[:, ax, hf, :].unsqueeze(1).broadcast_to([P, 8, 8]), ALU.mult, [a, tk])
                    r = tt(Ry, R1, R2, ALU.add, [u, v])
                a = r
            else:
                a = tt(R, R, g32.unsqueeze(1).broadcast_to([P, 16, 32]), ALU.mult, [a])
            sq_free[0] = [a]
            qq["r"] = a

        def heads_T(dst, gcol, ready, after):
            for y in range(2):
                for h0 in (0, 4):
                    b, free = B.take()
                    for j in range(4):
                        tok = transpose(B.ps[0:96, b * 512 + j * P:b * 512 + (j + 1) * P],
                                        tq[:, y * 768 + (h0 + j) * 96:y * 768 + (h0 + j + 1) * 96], [*ready, *free])
                    src = B.ps[0:96, b * 512:b * 512 + 512].rearrange("p (h n) -> p h n", h=4)
                    if h0:
                        a = act(dst(y, h0), src, after=[tok, *after], scale=gcol)
                    else:
                        d = ts(dst(y, h0), src, gcol, None, ALU.mult, ALU.bypass, [tok, *after])
                    B.give(b, [a if h0 else d])
                yield
            qq["T"] = [a, d]
            X_free[0] = [tok]

        def kv_pair(p):
            c = []
            for y in range(2):
                t = 2 * p + y
                b0, f0 = B.take()
                b1, f1 = B.take()
                tk0 = mm(B.ap(b0), ckv[:, t * P:(t + 1) * P], wkv[:, 0:512], True, True, [t_ukv, *f0, t_ck], inc=True)
                tk1 = mm(B.ap(b1), ckv[:, t * P:(t + 1) * P], wkv[:, 512:1024], True, True, [*f1], inc=True)
                X3 = tq[:, y * 768:(y + 1) * 768].rearrange("p (h d) -> p h d", h=8)
                a = act(X3[:, :, 0:64], B.ap(b0).rearrange("p (h d) -> p h d", h=8), after=[tk0, t_stat, *X_free[0], *bar],
                        scale=stat[:, 4 + t:5 + t])
                B.give(b0, [a])
                c += [a, dcopy(X3[:, :, 64:96], kr[:, t * 32:(t + 1) * 32].unsqueeze(1).broadcast_to([P, 8, 32]),
                               [*t_gv, *X_free[0]])]
                v = ts(V[:, t, :], B.ap(b1), stat[:, 4 + t:5 + t], None, ALU.mult, ALU.bypass, [tk1, S.t_ln, *bar])
                B.give(b1, [v])
                t_V[t] = v
            yield
            yield from norm_rope(1, 2 * p, c, False)
            yield
            yield from heads_T(lambda y, h0: K[0:96, h0:h0 + 4, (2 * p + y) * P:(2 * p + y + 1) * P], C("gk", l, 1, 96),
                               [qq["r"]], kbar)
            t_K[2 * p] = t_K[2 * p + 1] = qq["T"]

        def q_pair(p):
            c = []
            for y in range(2):
                t = 2 * p + y
                b0, f0 = B.take(2)
                for cc, w in ((0, 512), (512, 256)):
                    for m in range(2):
                        tok = mm(B.ps[:, b0 * 512 + cc:b0 * 512 + cc + w], cq[:, m, t * P:(t + 1) * P],
                                 uq[:, m * 768 + cc:m * 768 + cc + w], m == 0, m == 1, [*f0, t_uq, *t_cq], inc=(m == 1))
                a = act(tq[:, y * 768:(y + 1) * 768], B.ap(b0, 768), after=[tok, t_stat, *X_free[0]], scale=stat[:, t:t + 1])
                B.give(b0, [a], 2)
                c.append(a)
            yield
            yield from norm_rope(0, 2 * p, c, True)
            yield
            Q4 = Q.rearrange("p (y h n) -> p y h n", y=2, h=8)
            yield from heads_T(lambda y, h0: Q4[0:96, y, h0:h0 + 4, :], C("gq", l, 1, 96), [qq["r"]], [*Q_free[0], *Q_free[1]])
            for y in range(2):
                qq[2 * p + y] = (Q4[:, y, :, :], qq["T"])

        def weave(gen, fill, every=1):
            i = 0
            for _ in gen:
                i += 1
                if i % every == 0 and fill:
                    fill.pop(0)()

        fill = [lambda: g_gate(0), lambda: g_u(0), lambda: g_gate(1), lambda: g_u(1)]
        fill += [lambda m=m: a_gate(m) for m in range(4)]
        weave(gv_norm(), fill)
        kv0 = kv_pair(0)
        next(kv0)
        while len(fill) > 4:
            fill.pop(0)()
        spatial()
        weave(kv0, fill, 2)
        weave(kv_pair(1), fill, 2)
        weave(q_pair(tiles[0] // 2), fill, 2)
        while fill:
            fill.pop(0)()

        hfree = [PE.last()]
        mixt = {}
        for m in range(2):
            mixt[m] = split_to(hh[:, m, cs], hl[:, m, cs], fg[:, m, cs], [t_fg[m], *hfree])
            mixt[2 + m] = split_to(hh[:, 2 + m, cs], hl[:, 2 + m, cs], ug[:, m, cs], [t_ug[m], *hfree])
        for k in range(4, 8):
            mixt[k] = []

        P_free = [[DV.last()], [DV.last()], [DV.last()]]
        PT_free = [[], []]
        items = [(t, h) for t in tiles for h in range(8)]
        ob, info = {}, {}

        def partA(i):
            t, h = items[i]
            Qt, tQ = qq[t]
            nk = 2 if t < 2 else 4
            b, free = B.take()
            n = nk * P
            tok = mm(B.ap(b, n), Qt[0:96, h, :], K[0:96, h, 0:n], True, True, [*tQ, *(x for j in range(nk) for x in t_K[j]), *free], inc=True)
            Q_free[t % 2] = [tok]
            z = i % 3
            mx, sm = stat[:, 64 + z:65 + z], stat[:, 68 + z:69 + z]
            a = DV(lambda e: e.tensor_reduce(mx, B.ap(b, n), AX.X, ALU.max, negate=True), [tok, *P_free[z]])
            pb = Pb[:, z * 512:z * 512 + n]
            c = AC(lambda e: e.activation(pb, B.ap(b, n), ACT.Exp, bias=mx, accum_out=sm), [a, *P_free[z]])
            B.give(b, [c])
            info[i] = [nk, z, pb, c, sm]

        def partA2(i):
            nk, z, pb, c, sm = info[i]
            a = DV(lambda e: e.reciprocal(sm, sm), [c])
            a = ts(pb, pb, sm, None, ALU.mult, ALU.bypass, [a])
            info[i].append(a)

        def partB(i):
            nk, z, pb, c, sm, a = info[i]
            b, free = B.take()
            for j in range(nk):
                tok = transpose(B.ps[:, b * 512 + j * P:b * 512 + (j + 1) * P], pb[:, j * P:(j + 1) * P], [a, *free])
            P_free[z] = [tok]
            y = i % 2
            pt = PT[:, y * 512:y * 512 + nk * P]
            u = act(pt, B.ap(b, nk * P), after=[tok, *PT_free[y], *bar])
            B.give(b, [u])
            info[i] += [pt, u]

        def partC(i):
            t, h = items[i]
            nk, z, pt, u = info[i][0], info[i][1], info[i][6], info[i][7]
            if h == 0:
                ob[t] = B.take()
            b, free = ob[t]
            o_ = B.ps[64 * (h % 2):64 * (h % 2) + 64, b * 512 + (h // 2) * P:b * 512 + (h // 2 + 1) * P]
            for j in range(nk):
                tok = mm(o_, V[:, j, h * 64:(h + 1) * 64], pt[:, j * P:(j + 1) * P], j == 0, j == nk - 1,
                         [u, t_V[j], *free], inc=(j == nk - 1))
            PT_free[i % 2] = [tok]
            if h == 7:
                z = t % 2
                oo = S.sq[:, z * 512:z * 512 + 512]
                o3 = oo.rearrange("p (k n) -> p k n", k=4)
                c = slice(t * P, (t + 1) * P)
                a = tt(o3, B.ap(b).rearrange("p (k n) -> p k n", k=4), ag[:, :, c], ALU.mult,
                       [tok, *(t_ag[m] for m in range(4)), *AS(S.sq_rd[z])])
                B.give(b, [a])
                r = split_to(hh[:, 4:8, c], hl[:, 4:8, c], o3, [a, *hfree])
                for k in range(4, 8):
                    mixt[k] += r
                S.sq_rd[z] = r[1]

        def AS(t):
            return [t] if t is not None else []

        ni = len(items)
        fill = [lambda n=n, l_=l_: modulation(l_, n) for l_, n in ((0, 4), (0, 5), (1, 2), (1, 3), (1, 0), (1, 1))] if l == 0 else []
        qx = q_pair(1) if l == 0 else None
        for i in range(ni + 3):
            if i == 16 and qx is not None:
                for _ in qx:
                    pass
                qx = None
            if i < ni:
                partA(i)
            if 0 <= i - 1 < ni:
                partA2(i - 1)
            if qx is not None and i % 2 == 1 and i < 14:
                if i < 11:
                    next(qx, None)
            if fill and i % 5 == 4:
                fill.pop(0)()
            if 0 <= i - 2 < ni:
                partB(i - 2)
            if 0 <= i - 3 < ni:
                partC(i - 3)
        while fill:
            fill.pop(0)()

        mt = lambda k: mixt[k]
        for m in range(KD):
            b, ps, tok = lin_fm("w_out", l, (P * m, P), KD, xh, xl, N, mt)
            for s in range(2):
                if s == 0 and l == 1:
                    continue
                c = slice(256 * s, 256 * s + 256)
                gt, tg = modv(l, 2, m, s)
                pc = slice(256 * s - x0, 256 * s - x0 + 256)
                t = stt(XT[:, m, c], ps[:, pc], gt, XT[:, m, c], ALU.mult, ALU.add, [tok, tg])
            B.give(b, [t])
            if l == 0:
                square_add(XT[:, m, :], m == 0, m % 2, [t])
            else:
                t_x2[m] = split_to(hh[:, m, 0:256], hl[:, m, 0:256], XT[:, m, 256:512], [t, *hfree])
        if l == 0:
            br, tr = rstd_wide(TT, D, EPS)
            for n in (4, 5):
                modulation(1, n)

    xc = slice(256, 512)
    bar = barrier()
    t_c2 = AC.dma(lambda e: e.dma_start(S.cst[:, C2_TO:C2_TO + C_N - C2_FROM], S.cpack[:, C2_FROM:C_N]), (S.s_c2, 16), bar)
    X2h, X2l = (lambda k: hh[:, k, 0:256]), (lambda k: hl[:, k, 0:256])
    xt2 = lambda k: t_x2[k]
    o = 0

    def area(n):
        nonlocal o
        a = AF[:, o:o + n]
        o += n
        return a

    Q2 = area(3 * 1024).rearrange("p (g j n) -> p g j n", g=3, j=4)
    K2 = area(3 * 1024).rearrange("p (g j n) -> p g j n", g=3, j=4)
    V2 = area(2 * 1536).rearrange("p (t g n) -> p t g n", t=2, g=3)
    U = area(4 * 286).rearrange("p (m n) -> p m n", m=4)
    CV = area(4 * 256).rearrange("p (m n) -> p m n", m=4)
    Gt = area(16 * 256).rearrange("p (m n) -> p m n", m=16)
    P2 = area(3 * 768)
    rot = P2
    P2T = area(2 * 768)
    st2 = area(16)
    assert o <= S.NAF, o

    t_q2, t_v2 = [], []
    t_u = [None] * 4
    tz = DV(lambda e: e.memset(U[:, :, 0:30], 0.0), bar)
    t_cw = ts(C("convw"), C("convw"), 0.5, None, ALU.mult, ALU.bypass, [t_c2])
    for m in range(4):
        b, ps, tok = lin_fm("w_in_2", 0, (4608 + 512 + P * m, P), KD, X2h, X2l, 256, xt2)
        sg = Gt[:, m, :]
        a = act(sg, ps, ACT.Tanh, [tok, *bar], scale=0.5)
        B.give(b, [a])
        b, ps, tok = lin_fm("w_in_2", 0, (4608 + P * m, P), KD, X2h, X2l, 256, xt2)
        u = stt(U[:, m, 30:286], sg, 1.0, ps, ALU.add, ALU.mult, [tok, a, tz])
        B.give(b, [u])
        t_u[m] = u
    t_cv = [None] * 4
    taps = [(j, m) for j in range(31) for m in range(4)]

    def conv_taps(n):
        for _ in range(min(n, len(taps))):
            j, m = taps.pop(0)
            w = C("convw", 31 * m + j, 1)
            if j == 0:
                t_cv[m] = ts(CV[:, m, :], U[:, m, 0:256], w, C("convb", m, 1), ALU.mult, ALU.add, [t_u[m], tz, t_cw, *bar])
            else:
                t_cv[m] = stt(CV[:, m, :], U[:, m, j:j + 256], w, CV[:, m, :], ALU.mult, ALU.add, [t_cv[m]])

    rfree = [[], []]
    late = []

    def turn(ps, give, w, g, t, tok):
        z = t
        r1 = rot[:, z * 1024:z * 1024 + 512]
        r2 = rot[:, z * 1024 + 512:z * 1024 + 1024]
        p4 = ps.rearrange("p (h a n) -> p h a n", h=8, a=2)
        q4 = r2.rearrange("p (h a n) -> p h a n", h=8, a=2)
        a = tt(r1.rearrange("p (h n) -> p h n", n=32), ps.rearrange("p (h n) -> p h n", n=32),
               C("cos2", 32 * t, 32).unsqueeze(1).broadcast_to([P, 16, 32]), ALU.mult, [tok, t_c2, *rfree[z], *bar])
        tt(q4[:, :, 0, :], p4[:, :, 1, :], C("nsin2", 32 * t, 32).unsqueeze(1).broadcast_to([P, 8, 32]), ALU.mult, [])
        u = tt(q4[:, :, 1, :], p4[:, :, 0, :], C("sin2", 32 * t, 32).unsqueeze(1).broadcast_to([P, 8, 32]), ALU.mult, [])
        B.give(give, [u])
        a = tt(r1, r1, r2, ALU.add, [a, u])

        def finish():
            b, free = B.take()
            for j in range(4):
                tk = transpose(B.ps[:, b * 512 + j * P:b * 512 + (j + 1) * P], r1[:, j * P:(j + 1) * P], [a, *free])
            rfree[z] = [tk]
            dst = (Q2, K2)[w][:, g, :, t * P:(t + 1) * P]
            c = act(dst, B.ap(b).rearrange("p (j n) -> p j n", j=4), after=[tk, *bar])
            B.give(b, [c])
            t_q2[:] = [c]
        late.append(finish)

    for g in range(3):
        for w in (0, 1, 2):
            bb, tok = lin_tm("w_in_2", 0, g * 1536 + w * 512, 512, X2h, X2l, lambda t: slice(t * P, (t + 1) * P), [0, 1], 2, xt2)
            while late:
                late.pop(0)()
            for t in range(2):
                ps = B.ap(bb[t])
                if w == 2:
                    a = act(V2[:, t, g, :], ps, after=[tok, *bar])
                    B.give(bb[t], [a])
                    t_v2 = [a]
                else:
                    turn(ps, bb[t], w, g, t, tok)
            conv_taps(14)
    while late:
        late.pop(0)()
    conv_taps(200)

    t_g = {}

    def gate(m):
        b, ps, tok = lin_fm("w_in_2", 0, (4608 + 1024 + P * m, P), KD, X2h, X2l, 256, xt2)
        a = act(Gt[:, m, :], ps, ACT.Tanh, [tok, *t_u], scale=0.5)
        B.give(b, [a])
        t_g[m] = a

    ch, cl = S.ch, S.cl

    def ln(src, nt, nfeat, toks, eps):
        b, free = B.take()
        tok = mm(B.ap(b, 256), C("ones"), S.acc[:, 0:256], True, True, [S.acc_t, *free], inc=True)
        S.acc_rd = [tok]
        a = act(S.mean[:, :], B.ap(b, 256), after=[tok, *S.mean_rd], scale=1.0 / nfeat)
        B.give(b, [a])
        yield
        u = []
        for k in range(nt):
            u.append(tt(src(k), src(k), S.mean[:, :], ALU.subtract, [a, *toks(k)]))
            if k >= 1:
                square_add(src(k - 1), k == 1, (k - 1) % 2, [u[k - 1]])
        S.mean_rd = [u[-1]]
        square_add(src(nt - 1), nt == 1, (nt - 1) % 2, [u[-1]])
        yield
        S.ln_out = rstd_wide(256, nfeat, eps)

    t_ch = []

    def conv_norm():
        for k in range(4):
            acc_add(CV[:, k, :], k == 0, [t_cv[k]])
        yield
        yield from ln(lambda k: CV[:, k, :], 4, 512, lambda k: [t_cv[k]], LN_EPS)
        b, tr = S.ln_out
        yield
        th = P2T[:, 1280:1536]
        for m in range(4):
            a = stt(CV[:, m, :], CV[:, m, :], C("cg", m, 1), B.ap(b, 256), ALU.mult, ALU.mult, [tr])
            if m == 3:
                B.give(b, [a])
            a = ts(CV[:, m, :], CV[:, m, :], C("cb", m, 1), None, ALU.add, ALU.bypass, [a])
            th = U[:, m, 0:256]
            c = act(th, CV[:, m, :], ACT.Tanh, [a, t_cv[m]], scale=0.5)
            a = stt(CV[:, m, :], th, 1.0, CV[:, m, :], ALU.add, ALU.mult, [a, c])
            t = act(ch[:, m, :], CV[:, m, :], after=[a, *bar], scale=0.5)
            u = stt(cl[:, m, :], CV[:, m, :], 0.5, ch[:, m, :], ALU.mult, ALU.subtract, [a, t])
            t_ch.append([t, u])
            yield

    oh, ol = S.oh, S.ol
    t_o = []
    items = [(qb, h) for qb in range(2) for h in range(8)]
    info = {}
    Pf, PTf = [[*rfree[0], *rfree[1]] for _ in range(3)], [[], []]
    ob = {}

    def A(i):
        qb, h = items[i]
        nb = qb + 1
        r = slice(64 * (h % 2), 64 * (h % 2) + 64)
        w = nb * P
        b, free = B.take(2)
        ps = B.ap(b, 3 * w)
        for g in range(3):
            tok = mm(ps[:, g * w:(g + 1) * w], Q2[r, g, h // 2, qb * P:(qb + 1) * P], K2[r, g, h // 2, 0:w],
                     True, True, [*t_q2, *free], inc=(g == 2))
        z = i % 3
        mx, sm = st2[:, z:z + 1], st2[:, 4 + z:5 + z]
        pb = P2[:, z * 768:z * 768 + 3 * w]
        mk = C("mask1").rearrange("p (g n) -> p g n", g=3)[:, :, (0 if qb else 128):256]
        p3, s3 = pb.rearrange("p (g n) -> p g n", g=3), ps.rearrange("p (g n) -> p g n", g=3)
        a = DV(lambda e: e.tensor_tensor_reduce(p3, s3, mk, 1.0, -3.0e38, ALU.add, ALU.max, mx), [tok, *Pf[z], *bar])
        B.give(b, [a], 2)
        a = ts(mx, mx, -0.125, None, ALU.mult, ALU.bypass, [a])
        c = AC(lambda e: e.activation(pb, pb, ACT.Exp, bias=mx, scale=0.125, accum_out=sm), [a])
        info[i] = [nb, z, pb, sm, c]

    def A2(i):
        nb, z, pb, sm, c = info[i]
        a = DV(lambda e: e.reciprocal(sm, sm), [c])
        info[i].append(ts(pb, pb, sm, None, ALU.mult, ALU.bypass, [a]))

    def Bp(i):
        nb, z, pb, sm, c, a = info[i]
        n = 3 * nb
        b, free = B.take(2)
        for j in range(n):
            tok = transpose(B.ps[:, b * 512 + j * P:b * 512 + (j + 1) * P], pb[:, j * P:(j + 1) * P], [a, *free])
        Pf[z] = [tok]
        y = i % 2
        pt = P2T[:, y * 768:y * 768 + n * P]
        u = act(pt, B.ap(b, n * P), after=[tok, *PTf[y], *bar])
        B.give(b, [u], 2)
        info[i] += [pt, u]

    def Cp(i):
        qb, h = items[i]
        nb, z, pt, u = info[i][0], info[i][1], info[i][6], info[i][7]
        if h == 0:
            ob[qb] = B.take()
        b, free = ob[qb]
        o_ = B.ps[64 * (h % 2):64 * (h % 2) + 64, b * 512 + (h // 2) * P:b * 512 + (h // 2 + 1) * P]
        n = 3 * nb
        for j in range(n):
            tok = mm(o_, V2[:, j % nb, j // nb, h * 64:(h + 1) * 64], pt[:, j * P:(j + 1) * P], j == 0, j == n - 1,
                     [u, *t_v2, *free], inc=(j == n - 1))
        PTf[i % 2] = [tok]
        if h == 7:
            o3 = B.ap(b).rearrange("p (k n) -> p k n", k=4)
            c = slice(qb * P, (qb + 1) * P)
            r = split_to(oh[:, :, c], ol[:, :, c], o3, [tok, *bar])
            B.give(b, r)
            t_o.extend(r)

    t_m = [None] * KD
    conv_gen = conv_norm()

    def conv_out(m):
        b, ps, tok = lin_fm("w_conv_out_2", 0, (P * m, P), 4, lambda k: ch[:, k, :], lambda k: cl[:, k, :], 256, lambda k: t_ch[k])
        t_m[m] = stt(Gt[:, 8 + m, :], Gt[:, 8 + m, :], 1.0, ps, ALU.add, ALU.mult, [tok, t_g[8 + m]])
        B.give(b, [t_m[m]])

    fill = [lambda m=m: gate(m) for m in (*range(8, 16), *range(8))] + [lambda m=m: conv_out(m) for m in range(8)]
    nf = len(fill)
    for i in range(16 + 3):
        if i < 16:
            A(i)
        if 0 <= i - 1 < 16:
            A2(i - 1)
        next(conv_gen, None)
        for _ in range(1 if i % 3 or i < 3 else 2):
            if fill and not (i > 17):
                fill.pop(0)()
        if 0 <= i - 2 < 16:
            Bp(i - 2)
        if 0 <= i - 3 < 16:
            Cp(i - 3)
    for _ in conv_gen:
        pass
    while fill:
        fill.pop(0)()

    bar2 = barrier()
    t_h2 = []
    for m in range(KD):
        b, ps, tok = lin_fm("w_attn_out_2", 0, (P * m, P), 4, lambda k: oh[:, k, :], lambda k: ol[:, k, :], 256, lambda k: t_o)
        a = stt(Gt[:, m, :], Gt[:, m, :], 1.0, ps, ALU.add, ALU.mult, [tok, t_g[m]])
        B.give(b, [a])
        a = tt(Gt[:, m, :], Gt[:, m, :], Gt[:, 8 + m, :], ALU.add, [a, t_m[m]])
        t = act(hh[:, m, 0:256], Gt[:, m, :], after=[a, *bar2], scale=0.5)
        u = stt(hl[:, m, 0:256], Gt[:, m, :], 0.5, hh[:, m, 0:256], ALU.mult, ALU.subtract, [a, t])
        t_h2.append([t, u])

    t_r = []
    for m in range(KD):
        b, ps, tok = lin_fm("w_o_2", 0, (P * m, P), KD, X2h, X2l, 256, lambda k: t_h2[k])
        t_r.append(stt(XT[:, m, xc], XT[:, m, xc], ALPHA, ps, ALU.mult, ALU.add, [tok]))
        B.give(b, [t_r[-1]])
        acc_add(XT[:, m, xc], m == 0, [t_r[-1]])
    for _ in ln(lambda k: XT[:, k, xc], KD, D, lambda k: [t_r[k]], LN_EPS):
        pass
    b, tr = S.ln_out
    bar3 = barrier()
    t_x3, t_xt = [], []
    for k in range(KD):
        tmp = S.sq[:, (k % 4) * 256:(k % 4) * 256 + 256]
        a = stt(tmp, XT[:, k, xc], C("l1g", k, 1), B.ap(b, 256), ALU.mult, ALU.mult,
                [tr, *bar3, *([t_x3[k - 4][1], t_xt[k - 4]] if k >= 4 else [])])
        t = act(hh[:, k, 0:256], tmp, ACT.Identity, [a], bias=C("l1b", k, 1))
        if k:
            t_x3.append([tp, stt(hl[:, k - 1, 0:256], tmpp, C("l1b", k - 1, 1), hh[:, k - 1, 0:256], ALU.add, ALU.subtract, [tp])])
            t_xt.append(act(XT[:, k - 1, xc], tmpp, ACT.Identity, [ap], bias=C("l1b", k - 1, 1)))
        ap, tp, tmpp = a, t, tmp
    k = KD
    t_x3.append([tp, stt(hl[:, k - 1, 0:256], tmpp, C("l1b", k - 1, 1), hh[:, k - 1, 0:256], ALU.add, ALU.subtract, [tp])])
    t_xt.append(act(XT[:, k - 1, xc], tmpp, ACT.Identity, [ap], bias=C("l1b", k - 1, 1)))
    B.give(b, [ap])
    S.sq_rd = [t_x3[-1][1], t_xt[-1]]

    HK = KF // 2
    fh, fl = S.fh, S.fl
    toks_d = None
    sgs = [AF[:, 0:256], AF[:, 256:512]]
    hs = [AF[:, 512:768], AF[:, 768:1024]]
    s_rd = [list(bar3), list(bar3)]
    h_rd = [list(bar3), list(bar3)]
    t_d = [None] * KD
    t_r = list(t_xt)
    for half in range(2):
        t_f = {}
        for f in range(HK):
            m = half * HK + f
            z = f % 2
            b, ps, tok = lin_fm("w_ffn_gate_2", 0, (P * m, P), KD, X2h, X2l, 256, lambda k: t_x3[k])
            a = act(sgs[z], ps, ACT.Silu, [tok, *s_rd[z]])
            B.give(b, [a])
            b, ps, tok = lin_fm("w_ffn_up_2", 0, (P * m, P), KD, X2h, X2l, 256, lambda k: t_x3[k])
            u = tt(hs[z], sgs[z], ps, ALU.mult, [tok, a, *h_rd[z]])
            B.give(b, [u])
            s_rd[z] = [u]
            t_f[f] = split_to(fh[:, f, :], fl[:, f, :], hs[z], [u, toks_d])
            h_rd[z] = t_f[f]
        kk = list(range(half * HK, (half + 1) * HK))
        for m in range(KD):
            b, ps, t_d = lin_fm("w_ffn_down_2", 0, (P * m, P), None, lambda k: fh[:, k - half * HK, :],
                                lambda k: fl[:, k - half * HK, :], 256, lambda k: t_f[k - half * HK], kk=kk)
            t_r[m] = stt(XT[:, m, xc], XT[:, m, xc], 1.0 if half else ALPHA, ps, ALU.mult, ALU.add, [t_d, t_r[m]])
            B.give(b, [t_r[m]])
            if half:
                acc_add(XT[:, m, xc], m == 0, [t_r[m]])
        toks_d = t_d
    for _ in ln(lambda k: XT[:, k, xc], KD, D, lambda k: [t_r[k]], LN_EPS):
        pass
    b, tr = S.ln_out
    outs = S.out.rearrange("(k p) n -> p k n", p=P)
    for k in range(KD):
        a = stt(XT[:, k, xc], XT[:, k, xc], C("l2g", k, 1), B.ap(b, 256), ALU.mult, ALU.mult, [tr])
        a = act(XT[:, k, xc], XT[:, k, xc], ACT.Identity, [a], bias=C("l2b", k, 1))
        SP.dma(lambda e, k=k: e.dma_start(outs[:, k, :], XT[:, k, xc]), (S.s_out, 16 * (k + 1)), [a])
    SP.wait([(S.s_out, 16 * KD)])
    return W.seq


def build(nc, cpack, xin, wpack, wuq, wukv, out):
    with ExitStack() as ctx:
        S = State()

        def sb(name, shape, dt=F32):
            return ctx.enter_context(nc.sbuf_tensor(name, shape, dt))

        def sem(name):
            return ctx.enter_context(nc.semaphore(name))

        S.cpack, S.xin, S.wpack, S.wuq, S.wukv, S.out = cpack, xin, wpack, wuq, wukv, out
        S.NAF = 19400
        S.cst = sb("cst", [P, C_SB])
        S.XT = sb("XT", [P, KD, TT])
        S.hh = sb("hh", [P, KD, TT], F32R)
        S.hl = sb("hl", [P, KD, TT], F32R)
        S.raw = sb("raw", [P, NRAW * CH])
        S.whi = sb("whi", [P, NHL * CH], F32R)
        S.wlo = sb("wlo", [P, NHL * CH], F32R)
        HB = KF // 2
        S.fh = S.hh[:, :, 256:512]
        S.xr = sb("xr", [P, 2 * 3 * 256], F32R)
        S.AF = sb("AF", [P, S.NAF])
        S.sq = sb("sq", [P, 1024])
        S.acc = sb("acc", [P, 512])
        S.rs = sb("rs", [P, 512])
        S.mod = sb("mod", [P, 96])
        S.modrow = sb("modrow", [4, 512])
        S.nrm = sb("nrm", [P, 12])
        S.mean = sb("mean", [P, 256])
        S.uq = sb("uq", [P, 1536])
        S.c32 = sb("c32", [P, 16])
        S.c4 = sb("c4", [P, 32], F32R)
        S.rtab = sb("rtab", [P, 256])
        S.ps = ctx.enter_context(nc.psum_tensor("ps", [P, 8 * 512], F32))

        class Hidden:

            def __init__(self, h, off):
                self.h, self.off = h, off

            def __getitem__(self, key):
                _, k, _ = key
                if k < 8:
                    return self.h[:, k, 256:512]
                o = self.off + (k - 8) * 256
                return S.xr[:, o:o + 256]

        S.fh, S.fl = Hidden(S.hh, 0), Hidden(S.hl, 768)
        S.ch, S.cl = S.hh[:, 0:4, 256:512], S.hl[:, 0:4, 256:512]
        S.oh, S.ol = S.hh[:, 4:8, 256:512], S.hl[:, 4:8, 256:512]

        S.s_pe, S.s_act, S.s_dve = sem("s_pe"), sem("s_act"), sem("s_dve")
        S.s_raw = [sem(f"s_raw{i}") for i in range(NRAW)]
        S.s_uq, S.s_c0, S.s_c1, S.s_c2, S.s_x, S.s_out = sem("s_uq"), sem("s_c0"), sem("s_c1"), sem("s_c2"), sem("s_x"), sem("s_out")

        plan = emit(S, None)
        assert sum(P * n for _, n, _ in plan) == WTOTAL, sum(n for _, n, _ in plan)
        emit(S, plan)

        block = ctx.enter_context(nc.Block())

        @block.sync
        def _(e):
            S.SP.run(e)

        @block.gpsimd
        def _(e):
            S.GP.run(e)

        @block.scalar
        def _(e):
            S.ACT.run(e)

        @block.vector
        def _(e):
            S.DVE.run(e)

        @block.tensor
        def _(e):
            S.PE.run(e)
    return plan


def tables():
    f32 = np.float32
    c = {}
    i = np.arange(256)
    a = 2 * np.pi * np.outer(i, i) / 256
    c["c256"] = (np.cos(a) / 128).astype(f32).reshape(2, 128, 256).transpose(1, 0, 2)
    c["s256"] = (-np.sin(a) / 128).astype(f32).reshape(2, 128, 256).transpose(1, 0, 2)
    j = np.arange(64)
    b = 2 * np.pi * np.outer(j, j) / 64
    for nm, m in (("c64", np.cos(b)), ("s64", np.sin(b))):
        z = np.zeros((128, 128), f32)
        z[:64, :64] = m
        z[64:, 64:] = m
        c[nm] = z
    c["ones"] = np.ones((128, 128), f32)
    c["ident"] = np.eye(128, dtype=f32)
    half = 16
    inv = (f32(10000.0) ** (-np.arange(0, half, 2, dtype=f32) / f32(half))).astype(f32)
    row = np.repeat(np.arange(4, dtype=f32), 64)
    col = np.tile(np.arange(64, dtype=f32), 4)
    ar, ac = (row[:, None] * inv[None]).astype(f32), (col[:, None] * inv[None]).astype(f32)
    ang = np.concatenate([ar, ar, ac, ac], -1)
    sgn = np.tile(np.repeat(np.array([-1, 1], f32), 8), 2)
    c["cos1"] = np.cos(ang).astype(f32).reshape(2, 128, 32).transpose(1, 0, 2)
    c["sin1"] = (np.sin(ang).astype(f32) * sgn).reshape(2, 128, 32).transpose(1, 0, 2)
    inv2 = (1.0 / (f32(10000.0) ** (np.arange(0, 64, 2, dtype=f32) / f32(64)))).astype(f32)
    ang2 = (np.arange(256, dtype=f32)[:, None] * inv2[None]).astype(f32)
    c["cos2"] = np.cos(ang2).astype(f32).reshape(2, 128, 32).transpose(1, 0, 2)
    c["sin2"] = np.sin(ang2).astype(f32).reshape(2, 128, 32).transpose(1, 0, 2)
    c["nsin2"] = -c["sin2"]
    t, s = np.arange(256)[:, None], np.arange(256)[None, :]
    m = []
    for win, dil in ((128, 1), (512, 4), (2048, 16)):
        ok = (t >= s) & ((t - s) % dil == 0) & ((t - s) <= win)
        m.append(np.where(ok, 0.0, NEG).astype(f32))
    c["mask1"] = np.stack([x[128:, :] for x in m], 1)
    e = np.zeros((128, 4), f32)
    e[:, 0], e[:, 1] = EPS, LN_EPS
    c["eps"] = e
    z = np.zeros((128, 2), f32)
    z[0, 0] = z[1, 1] = z[2, 0] = z[3, 1] = 1.0
    c["sel"] = z
    return c


def kernel(**inputs):
    import concourse.bacc as _bacc
    from concourse.bass_utils import run_bass_kernel_spmd as _run

    I = {k: np.asarray(v) for k, v in inputs.items()}
    f32 = np.float32

    nc = _bacc.Bacc("TRN2", target_bir_lowering=False, num_devices=1)
    ci = nc.dram_tensor("cpack", (P, C_N), F32, kind="ExternalInput").ap()
    xi = nc.dram_tensor("xin", (P, KD * TT), F32, kind="ExternalInput").ap()
    wi = nc.dram_tensor("wpack", (WTOTAL,), F32, kind="ExternalInput").ap()
    ui = nc.dram_tensor("wuq", (2, P, 1536), F32, kind="ExternalInput").ap()
    vi = nc.dram_tensor("wukv", (2, P, 1024), F32, kind="ExternalInput").ap()
    oo = nc.dram_tensor("out", (D, T), F32, kind="ExternalOutput").ap()
    plan = build(nc, ci, xi, wi, ui, vi, oo)

    def cols(v, n):
        return v.reshape(n, P).T

    def rows(v):
        return np.broadcast_to(v.reshape(1, -1), (P, v.size))

    c = tables()
    c["cvec"] = np.stack([cols(I["c_ctx"], 8), cols(I["c"][0], 8)], 2)
    c["bmod"] = np.concatenate([cols(I["b_mod"][l], 24) for l in range(2)], 1)
    c["ng"] = np.concatenate([cols(I["norm_g"][l], 8) for l in range(2)], 1)
    c["qag"] = np.concatenate([cols(I["q_a_g"][l], 2) for l in range(2)], 1)
    c["kvag"] = np.concatenate([cols(I["kv_a_g"][l], 1) for l in range(2)], 1)
    for nm, src in (("gq", "q_norm_g"), ("gk", "k_norm_g")):
        z = np.ones((P, 2), f32)
        z[:64, :] = I[src][:, :64].T
        c[nm] = z
        c[nm + "r"] = np.concatenate([rows(I[src][l, 64:]) for l in range(2)], 1)
    c["lng"] = np.concatenate([rows(I["g_ln_g"][l]) for l in range(2)], 1)
    c["bs"] = np.stack([np.repeat(I["g_bs"][l, 2 * m:2 * m + 2], 64, 0) for l in range(2) for m in range(2)], 1)
    c["convw"] = I["conv_w_2"][0].T.reshape(4, P, 31).transpose(1, 0, 2)
    c["convb"] = cols(I["conv_b_2"][0], 4)
    c["cg"], c["cb"] = cols(I["conv_ln_g_2"][0], 4), cols(I["conv_ln_b_2"][0], 4)
    c["l1g"], c["l1b"] = cols(I["ln1_g_2"][0], 8), cols(I["ln1_b_2"][0], 8)
    c["l2g"], c["l2b"] = cols(I["ln2_g_2"][0], 8), cols(I["ln2_b_2"][0], 8)
    cpack = np.zeros((P, C_N), f32)
    for nm, (off, n) in C_AT.items():
        cpack[:, off:off + n] = np.asarray(c[nm]).reshape(P, n)

    xin = np.concatenate([I["ctx"][0].T, I["x"][0].T], 1).reshape(KD, P, TT).transpose(1, 0, 2).reshape(P, KD * TT)

    kvc = np.concatenate([np.arange(h * 128, h * 128 + 64) for h in range(8)] + [np.arange(h * 128 + 64, h * 128 + 128) for h in range(8)])
    gvkr = np.concatenate([np.arange(768, 1024), np.arange(1664, 1696)])
    wpack = np.empty(WTOTAL, f32)
    at = 0
    for (name, l, ks, cc), n, _ in plan:
        if name == "g_ws":
            blk = I[name][l].transpose(2, 0, 1)
        else:
            w = I[name][l]
            blk = w.reshape(-1, P, w.shape[1])[ks[0]:ks[-1] + 1]
            if cc[0] == ("gvkr",):
                blk = blk[:, :, gvkr]
            else:
                blk = blk[:, :, cc[0]:cc[0] + cc[1]]
            blk = blk.transpose(1, 0, 2)
        wpack[at:at + P * n] = blk.reshape(-1)
        at += P * n
    assert at == WTOTAL

    r = _run(nc, [{"cpack": cpack, "xin": np.ascontiguousarray(xin), "wpack": wpack,
                    "wuq": np.ascontiguousarray(I["w_uq"].reshape(2, 2, P, 768).transpose(0, 2, 1, 3).reshape(2, P, 1536)),
                    "wukv": np.ascontiguousarray(I["w_ukv"][:, :, kvc])}], core_ids=[0])
    y = r.results[0]["out"]
    return np.ascontiguousarray(y.T).reshape(1, T, D)
```

```python
import math
from contextlib import ExitStack

import numpy as np
import concourse.bass as bass
from concourse import mybir

F32 = mybir.dt.float32
F32R = mybir.dt.float32r
I32 = mybir.dt.int32
ALU = mybir.AluOpType
ACT = mybir.ActivationFunctionType
AX = mybir.AxisListType

P = 128
D = 1024
T = 256
TT = 512
KD = D // P
FF = 2816
KF = FF // P
EPS = 1e-6
LN_EPS = 1e-5
ALPHA = 2.0 ** 0.25
NRAW = 4
NHL = 4
CH = 1024
NEG = -1.0e30
WTOTAL = 128 * 248320


def const_layout():
    items = [
        ("cvec", 8 * 2), ("bmod", 2 * 24), ("ng", 2 * 8), ("eps", 4), ("sel", 2),
        ("ones", 128), ("ident", 128),
        ("c64", 128), ("s64", 128), ("c256", 512), ("s256", 512),
        ("qag", 2 * 2), ("kvag", 2), ("gq", 2), ("gk", 2), ("gqr", 2 * 32), ("gkr", 2 * 32),
        ("cos1", 2 * 32), ("sin1", 2 * 32), ("lng", 2 * 64), ("bs", 2 * 2 * 128),
        ("cos2", 2 * 32), ("sin2", 2 * 32), ("nsin2", 2 * 32), ("convw", 4 * 31), ("convb", 4), ("cg", 4), ("cb", 4),
        ("l1g", 8), ("l1b", 8), ("l2g", 8), ("l2b", 8),
        ("mask1", 3 * 256),
    ]
    at, off = {}, 0
    for name, n in items:
        at[name] = (off, n)
        off += n
    return at, off


C_AT, C_N = const_layout()
C_EARLY = C_AT["c64"][0]
C2_FROM, C2_TO = C_AT["cos2"][0], C_AT["c64"][0]
C_SB = C_AT["cos2"][0]
assert C_N - C2_FROM <= C_AT["qag"][0] - C2_TO


class Lane:

    def __init__(self, sem):
        self.sem, self.n, self.q, self.seen = sem, 0, [], {}

    def wait(self, toks):
        for t in toks:
            if t is None:
                continue
            sem, v = t
            if self.seen.get(sem.name, 0) < v:
                self.seen[sem.name] = v
                self.q.append(("w", sem, v))

    def quiet(self, fn, after=()):
        self.wait(after)
        self.q.append(("i", fn, None, 0))

    def __call__(self, fn, after=()):
        self.wait(after)
        self.n += 1
        self.q.append(("i", fn, self.sem, 1))
        return (self.sem, self.n)

    def dma(self, fn, tok, after=()):
        self.wait(after)
        self.q.append(("i", fn, tok[0], 16))
        return tok

    def last(self):
        return (self.sem, self.n)

    def run(self, e):
        for x in self.q:
            if x[0] == "w":
                e.wait_ge(x[1], x[2])
            else:
                i = x[1](e)
                if x[2] is not None:
                    i.then_inc(x[2], x[3])


class Banks:

    def __init__(self, ps):
        self.ps, self.free, self.held, self.i = ps, [()] * 8, [False] * 8, 0

    def take(self, n=1):
        for _ in range(16):
            i = self.i % 8
            if i + n <= 8 and not any(self.held[i:i + n]):
                self.i = i + n
                for j in range(i, i + n):
                    self.held[j] = True
                return i, [t for j in range(i, i + n) for t in self.free[j]]
            self.i += 1
        raise RuntimeError("no PSUM bank is free")

    def give(self, i, toks, n=1):
        for j in range(i, i + n):
            self.held[j] = False
            self.free[j] = tuple(toks)

    def ap(self, i, n=512):
        return self.ps[:, i * 512:i * 512 + n]


class Stream:

    def __init__(self, S, plan):
        self.S, self.plan, self.seq = S, plan, []
        self.loaded = self.prepped = self.split = 0
        self.rel = {}
        self.relsplit = {}
        self.ready = {}
        self.off = 0
        self.low = []

    def advance(self):
        S = self.S
        if self.plan is None:
            return
        while self.loaded < len(self.plan):
            i = self.loaded
            if i >= NRAW and (i - NRAW) not in self.rel:
                break
            _, n, _ = self.plan[i]
            slot, off = i % NRAW, self.off
            dst, src = S.raw[:, slot * CH:slot * CH + n], S.wpack[off:off + P * n].rearrange("(p n) -> p n", n=n)
            tok = (S.s_raw[slot], 16 * (i // NRAW + 1))
            S.SP.dma(lambda e, d=dst, s=src: e.dma_start(d, s), tok, [self.rel.get(i - NRAW)])
            self.off += P * n
            self.loaded += 1
        while self.prepped < self.loaded:
            i = self.prepped
            _, n, sp = self.plan[i]
            slot = i % NRAW
            tok = (S.s_raw[slot], 16 * (i // NRAW + 1))
            if not sp:
                self.ready[i] = ([tok], None)
            else:
                j = self.split
                if j >= NHL and (j - NHL) not in self.relsplit:
                    break
                h = j % NHL
                raw = S.raw[:, slot * CH:slot * CH + n]
                hi, lo = S.whi[:, h * CH:h * CH + n], S.wlo[:, h * CH:h * CH + n]
                used = self.relsplit.get(j - NHL)
                t1 = S.ACT(lambda e, o=hi, x=raw: e.activation(o, x, ACT.Copy), [tok, used])
                self.low.append((i, j, lo, raw, hi, tok, t1))
                self.split += 1
            self.prepped += 1
            self.lows(1)

    def lows(self, keep, upto=-1):
        while len(self.low) > keep or (self.low and self.low[0][0] <= upto):
            i, j, lo, raw, hi, tok, t1 = self.low.pop(0)
            t2 = self.S.DVE(lambda e, o=lo, x=raw, y=hi: e.tensor_tensor(o, x, y, ALU.subtract), [tok, t1])
            self.rel[i] = t2
            self.ready[i] = ([t1, t2], j)

    def get(self, desc, n, split=True):
        i = len(self.seq)
        self.seq.append((desc, n, split))
        if self.plan is None:
            z = self.S.raw[:, 0:n]
            return (z, z if split else None), [], i
        self.advance()
        self.lows(len(self.low), i)
        toks, j = self.ready[i]
        if j is None:
            s = i % NRAW
            return (self.S.raw[:, s * CH:s * CH + n], None), toks, i
        h = j % NHL
        return (self.S.whi[:, h * CH:h * CH + n], self.S.wlo[:, h * CH:h * CH + n]), toks, i

    def done(self, i, tok):
        if self.plan is None:
            return
        j = self.ready[i][1]
        if j is None:
            self.rel[i] = tok
        else:
            self.relsplit[j] = tok




class State:
    pass


def emit(S, plan):
    PE, AC, DV, SP, GP = Lane(S.s_pe), Lane(S.s_act), Lane(S.s_dve), Lane(S.s_c0), Lane(S.s_uq)
    S.GP = GP
    S.PE, S.ACT, S.DVE, S.SP = PE, AC, DV, SP
    W = Stream(S, plan)
    B = Banks(S.ps)
    XT, hh, hl = S.XT, S.hh, S.hl
    AF = S.AF

    def C(name, a=0, n=None, parts=P):
        off, m = C_AT[name]
        if off >= C2_FROM:
            off += C2_TO - C2_FROM
        return S.cst[0:parts, off + a:off + a + (m - a if n is None else n)]

    def mm(out, lhsT, rhs, start, stop, after=(), inc=False):
        f = lambda e: e.matmul(out, lhsT, rhs, start=start, stop=stop, skip_group_check=True)
        if inc:
            return PE(f, after)
        PE.quiet(f, after)

    def act(out, in_, func=ACT.Copy, after=(), **kw):
        return AC(lambda e: e.activation(out, in_, func, **kw), after)

    def tt(out, a, b, op, after=()):
        return DV(lambda e: e.tensor_tensor(out, a, b, op), after)

    def stt(out, a, s, b, op0, op1, after=()):
        return DV(lambda e: e.scalar_tensor_tensor(out=out, in0=a, scalar=s, in1=b, op0=op0, op1=op1), after)

    def ts(out, a, s1, s2, op0, op1, after=()):
        return DV(lambda e: e.tensor_scalar(out, a, s1, s2, op0, op1), after)

    def rsum(out, in_, after=()):
        return DV(lambda e: e.tensor_reduce(out, in_, AX.X, ALU.add), after)

    def dcopy(out, in_, after=()):
        return DV(lambda e: e.tensor_copy(out, in_), after)

    def transpose(out, in_, after=()):
        return PE(lambda e: e.transpose(out, in_, C("ident")), after)

    def split_to(hi, lo, src, after=()):
        t = act(hi, src, after=after)
        u = tt(lo, src, hi, ALU.subtract, [*after, t])
        return [t, u]

    def both(*gs):
        for g in gs:
            yield from g

    def barrier():
        return [PE.last(), AC.last(), DV.last()]

    t_c0 = SP.dma(lambda e: e.dma_start(S.cst[:, 0:C_EARLY], S.cpack[:, 0:C_EARLY]), (S.s_c0, 16))
    t_x = AC.dma(lambda e: e.dma_start(XT[:, :, :], S.xin.rearrange("p (k n) -> p k n", k=KD)), (S.s_x, 16))
    W.advance()
    t_c1 = AC.dma(lambda e: e.dma_start(S.cst[:, C_EARLY:C_SB], S.cpack[:, C_EARLY:C_SB]), (S.s_c1, 16))

    def lin_fm(wname, l, cols, K, xh, xl, N, xtoks, ps=None, kk=None, start=True, stop=True, free=()):
        if ps is None:
            b, free = B.take()
            ps = B.ap(b, N)
        else:
            b = None
        kk = list(range(K)) if kk is None else kk
        tok = None
        groups = [kk[i:i + 8] for i in range(0, len(kk), 8)]
        for g in groups:
            (whi, wlo), toks, ci = W.get((wname, l, tuple(g), tuple(cols)), len(g) * P)
            for j, k in enumerate(g):
                wh, wl = whi[:, j * P:(j + 1) * P], wlo[:, j * P:(j + 1) * P]
                xt = list(xtoks(k)) if callable(xtoks) else list(xtoks)
                first, last = start and k == kk[0], stop and k == kk[-1]
                mm(ps, wh, xh(k), first, False, [*toks, *free, *xt])
                mm(ps, wh, xl(k), False, False)
                if k == g[-1]:
                    tok = mm(ps, wl, xh(k), False, last, inc=True)
                else:
                    mm(ps, wl, xh(k), False, last)
            W.done(ci, tok)
        return b, ps, tok

    def lin_many(specs, xtoks):
        out = []
        for wname, l, cols, xh, xl, N in specs:
            b, free = B.take()
            (whi, wlo), toks, ci = W.get((wname, l, tuple(range(KD)), tuple(cols)), KD * P)
            out.append([b, B.ap(b, N), free, whi, wlo, toks, ci])
        for k in range(KD):
            for (wname, l, cols, xh, xl, N), o in zip(specs, out):
                b, ps, free, whi, wlo, toks, ci = o
                wh, wl = whi[:, k * P:(k + 1) * P], wlo[:, k * P:(k + 1) * P]
                mm(ps, wh, xh(k), k == 0, False, [*toks, *free, *xtoks(k)])
                mm(ps, wh, xl(k), False, False)
                if k == KD - 1:
                    tok = mm(ps, wl, xh(k), False, True, inc=True)
                    W.done(ci, tok)
                    o.append(tok)
                else:
                    mm(ps, wl, xh(k), False, False)
        return [(o[0], o[1], o[7]) for o in out]

    def lin_tm(wname, l, c0, ncols, xh, xl, toks_of, tiles, per, xtoks, cut=None, beside=None):
        bs = {t: B.take() for t in tiles}
        k = 0
        while k < KD:
            g = list(range(k, min(k + per, KD)))
            (whi, wlo), toks, ci = W.get((wname, l, tuple(g), (c0, ncols)), len(g) * ncols)
            for j, kk in enumerate(g):
                xt = list(xtoks(kk)) if callable(xtoks) else list(xtoks)
                for t in tiles:
                    lo_c = cut(t) if cut else 0
                    wh, wl = (w[:, j * ncols + lo_c:(j + 1) * ncols] for w in (whi, wlo))
                    o = B.ps[:, bs[t][0] * 512 + lo_c:bs[t][0] * 512 + ncols]
                    ts_ = toks_of(t)
                    mm(o, xh(kk)[:, ts_], wh, kk == 0, False, [*toks, *bs[t][1], *xt])
                    mm(o, xh(kk)[:, ts_], wl, False, False)
                    tok = mm(o, xl(kk)[:, ts_], wh, False, kk == KD - 1, inc=True)
            W.done(ci, tok)
            if beside:
                beside()
            k += per
        return {t: bs[t][0] for t in tiles}, tok

    t = act(S.c32[:, 0:16], C("cvec"), ACT.Silu, [t_c0])
    c32 = S.c32[:, 0:16].rearrange("p (k s) -> p k s", s=2)
    c4 = S.c4[:, :].rearrange("p (k s) -> p k s", s=4)
    t1 = act(c4[:, :, 0:2], c32, after=[t])
    t_c4 = [t1, tt(c4[:, :, 2:4], c32, c4[:, :, 0:2], ALU.subtract, [t, t1])]
    modt = {}
    mod_rd = [None, None]
    modc = [0]

    def mod_steps(l, n, split=True):
        b, free = B.take()
        r = 4 if split else 2
        ps = B.ps[0:r, b * 512:b * 512 + 512]
        for g in range(4):
            (whi, wlo), toks, ci = W.get(("w_mod", l, (2 * g, 2 * g + 1), (512 * n, 512)), 1024, split)
            for j in range(2):
                k = 2 * g + j
                if not split:
                    tok = mm(ps, c32[:, k, :], whi[:, j * 512:(j + 1) * 512], k == 0, k == 7, [*toks, *free, *t_c4], inc=True)
                    continue
                mm(ps, c4[:, k, :], whi[:, j * 512:(j + 1) * 512], k == 0, False, [*toks, *free, *t_c4])
                tok = mm(ps, c4[:, k, :], wlo[:, j * 512:(j + 1) * 512], False, k == 7, inc=(j == 1))
            W.done(ci, tok)
            if g < 3:
                yield
        z = 0
        row = S.modrow[0:r, :]
        t = act(row, ps, after=[tok, mod_rd[z]])
        B.give(b, [t])
        yield
        b, free = B.take()
        for j in range(4):
            tok = mm(B.ps[:, b * 512 + 2 * j:b * 512 + 2 * j + 2], row[:, j * P:(j + 1) * P],
                     C("sel", parts=4) if split else C("ident", 0, 2, 2), True, True, [t, *free], inc=(j == 3))
        mod_rd[z] = tok
        o = S.mod[:, l * 48 + 8 * n:l * 48 + 8 * n + 8].rearrange("p (j s) -> p j s", s=2)
        bm = C("bmod", 24 * l + 4 * n, 4).unsqueeze(2).broadcast_to([P, 4, 2])
        t = tt(o, B.ap(b, 8).rearrange("p (j s) -> p j s", s=2), bm, ALU.add, [tok])
        B.give(b, [t])
        if n in (2, 3):
            ng = C("ng", 8 * l + 4 * (n - 2), 4).unsqueeze(2).broadcast_to([P, 4, 2])
            t = stt(o, o, 1.0, ng, ALU.add, ALU.mult, [t])
        modt[(l, n)] = t
        yield

    def modulation(l, n, split=True):
        for _ in mod_steps(l, n, split):
            pass

    def modv(l, what, k, s):
        n = what * 2 + k // 4
        c = l * 48 + 8 * n + 2 * (k % 4) + s
        return S.mod[:, c:c + 1], modt[(l, n)]

    def rsqrt(v, u, w, after):
        y = u
        t = ts(y.bitcast(I32), v.bitcast(I32), -0.5, 1597463007.0, ALU.mult, ALU.add, after)
        for i in range(3):
            t = tt(w, y, y, ALU.mult, [t])
            t = stt(w, w, -0.5, v, ALU.mult, ALU.mult, [t])
            t = stt(v if i == 2 else y, w, 1.5, y, ALU.add, ALU.mult, [t])
        return t

    def acc_add(src, first, after):
        n = src.free_size()
        a = S.acc[:, 0:n]
        if first:
            S.acc_t = dcopy(a, src, [*after, *S.acc_rd])
        else:
            S.acc_t = tt(a, a, src, ALU.add, [*after, S.acc_t])
        return S.acc_t

    def square_add(src, first, z, after):
        n = src.free_size()
        sq = S.sq[:, z * 512:z * 512 + n]
        t = act(sq, src, ACT.Square, [*after, S.sq_rd[z]])
        S.sq_rd[z] = acc_add(sq, first, [t])

    def rstd_wide(n, nfeat, eps):
        for _ in rstd_steps(n, nfeat, eps):
            pass
        return S.rstd

    def rstd_steps(n, nfeat, eps):
        nt = n // P
        b, free = B.take()
        for j in range(nt):
            tok = mm(B.ps[:, b * 512 + j:b * 512 + j + 1], S.acc[:, j * P:(j + 1) * P], C("ones", 0, 1), True, True,
                     [S.acc_t, *free], inc=(j == nt - 1))
        S.acc_rd = [tok]
        v, u, w = (S.nrm[:, 4 * i:4 * i + nt] for i in range(3))
        t = ts(v, B.ap(b, nt), 1.0 / nfeat, eps, ALU.mult, ALU.add, [tok])
        B.give(b, [t])
        t = rsqrt(v, u, w, [t])
        dg = S.rs[:, 0:n].rearrange("p (t n) -> p t n", n=P)
        t = tt(dg, C("ident").unsqueeze(1).broadcast_to([P, nt, P]), v.unsqueeze(2).broadcast_to([P, nt, P]),
               ALU.mult, [t, *S.rs_rd])
        yield
        b, free = B.take()
        tok = mm(B.ap(b, n), C("ones"), S.rs[:, 0:n], True, True, [t, *free], inc=True)
        S.rs_rd = [tok]
        S.rstd = b, tok
        yield

    t_h = []

    def make_h(l, b, tr):
        bar = barrier()
        late = []

        def low():
            out, last = late.pop(0)
            for tmp, sh, oh_, ol_, z, u in out:
                v = stt(ol_, tmp, sh, oh_, ALU.add, ALU.subtract, [u])
                S.tmp_rd[z] = v
            t_h.append([u, v])
            if last:
                B.give(b, [v])
                S.sq_rd = [v, v]

        for k in range(KD):
            out = []
            for s in range(2):
                c = slice(256 * s, 256 * s + 256)
                A, ta = modv(l, 1, k, s)
                sh, tb = modv(l, 0, k, s)
                z = (2 * k + s) % 4
                tmp = S.sq[:, z * 256:(z + 1) * 256]
                t = stt(tmp, XT[:, k, c], A, B.ap(b)[:, c], ALU.mult, ALU.mult, [tr, ta, *bar, S.tmp_rd[z]])
                u = act(hh[:, k, c], tmp, ACT.Identity, [t, tb], bias=sh)
                out.append((tmp, sh, hh[:, k, c], hl[:, k, c], z, u))
            late.append((out, k == KD - 1))
            if k % 4:
                low()
            if k % 4 == 3:
                low()
            yield

    S.mean_rd = []
    S.sq_rd, S.acc_rd, S.rs_rd, S.tmp_rd, S.acc_t = [None, None], [], [], [None] * 4, None

    S.x2 = [None] * KD
    for k in range(KD):
        square_add(XT[:, k, :], k == 0, k % 2, [t_x])
    modulation(0, 2)
    r_ = rstd_steps(TT, D, EPS)
    for i, _ in enumerate(mod_steps(0, 0)):
        if i in (0, 2):
            next(r_)
    br, tr = S.rstd
    t_h = []
    hs_ = make_h(0, br, tr)
    for n in (3, 1):
        for i, _ in enumerate(mod_steps(0, n)):
            if i in (1, 3):
                next(hs_)

    t_x2 = [None] * KD
    for l in range(2):
        ns = 2 if l == 0 else 1
        x0 = 0 if l == 0 else 256
        N = TT - x0
        cs = slice(x0, TT)
        tiles = list(range(x0 // P, 4))
        if l == 1:
            t_h = []
            hs_ = make_h(l, br, tr)
        W.advance()
        for _ in hs_:
            pass
        bar = barrier()
        t_uq = GP.dma(lambda e, l=l: e.dma_start(S.uq[:, :], S.wuq[l]), (S.s_uq, 16 * (2 * l + 1)), bar)
        uq = S.uq

        o = 0

        def area(n):
            nonlocal o
            a = AF[:, o:o + n]
            o += n
            return a

        fg = area(2 * N).rearrange("p (k n) -> p k n", k=2)
        ug = area(2 * N).rearrange("p (k n) -> p k n", k=2)
        ag = area(4 * N).rearrange("p (k n) -> p k n", k=4)
        go_ = o
        ckv = area(TT)
        gv = area(1024)
        Pb = area(3 * 512)
        kr = area(4 * 32)
        cq = area(2 * N).rearrange("p (k n) -> p k n", k=2)
        tq = area(2 * 768)
        stat = area(240)
        tq2 = area(1536) if l == 1 else None
        V = area(4 * 512).rearrange("p (t n) -> p t n", t=4)
        Q = area(2 * 1024)
        PT = area(2 * 512)
        ko = o
        K = area(8 * TT).rearrange("p (h n) -> p h n", h=8)
        end = o
        o = ko
        fi = area(2 * TT).rearrange("p (k n) -> p k n", k=2)
        W12 = area(1024).rearrange("p (c k n) -> p c k n", c=2, k=2)
        Vf = area(4 * 512).rearrange("p (t n) -> p t n", t=4)
        assert max(o, end) <= S.NAF, max(o, end)
        wkv = Pb[:, 512:1536]
        X3 = [tq, S.wk[:, 0:1536], tq2]
        scr = [AF[:, ko - 3072:ko - 1536], AF[:, ko - 1536:ko], AF[:, go_:go_ + 1536]]
        st_of = [(48, 96, 112), (144, 160, 176), (192, 208, 224)]
        gsq = V[:, 0:2, :].rearrange("p t n -> p (t n)")
        t_ukv = GP.dma(lambda e, l=l, w=wkv: e.dma_start(w, S.wukv[l]), (S.s_uq, 16 * (2 * l + 2)), bar)
        xh, xl = (lambda k: hh[:, k, cs]), (lambda k: hl[:, k, cs])
        XH, XL = (lambda k: hh[:, k, :]), (lambda k: hl[:, k, :])
        ht = lambda k: t_h[k]
        off = {}
        c0 = 0
        for nm, w in (("fin", 256), ("fgate", 256), ("gu", 256), ("gv", 256), ("ggate", 256), ("cq", 256), ("ckv", 128), ("kr", 32), ("agate", 512)):
            off[nm] = c0
            c0 += w

        def inp(nm, m, full=False):
            return lin_fm("w_in", l, (off[nm] + P * m, P), KD, XH if full else xh, XL if full else xl,
                          TT if full else N, ht)

        def spec(nm, m, full=False):
            return ("w_in", l, (off[nm] + P * m, P), XH if full else xh, XL if full else xl, TT if full else N)

        def ckv_take(res):
            b, ps, tok = res
            t = act(ckv, ps, after=[tok, t_c1, *bar], scale=C("kvag", l, 1))
            u = act(S.acc[:, :], ps, ACT.Square, [tok, *bar, *S.acc_rd])
            B.give(b, [t, u])
            return t, u

        t_fi = []
        first = lin_many([spec("fin", 0), spec("fin", 1) if l == 0 else spec("ckv", 0, True)], ht)
        if l == 1:
            ckv_res = ckv_take(first.pop())
            first.append(inp("fin", 1))
        for m in range(2):
            b, ps, tok = first[m]
            t = act(fi[:, m, cs], ps, after=[tok, *bar])
            B.give(b, [t])
            t_fi.append(t)
        (wf, _), toks, ci = W.get(("w_fmix", l, (0, 1), (0, 256)), 512, split=False)
        for c, nm in enumerate(("c64", "s64")):
            b, free = B.take()
            tok = mm(B.ap(b), C(nm), wf, True, True, [*toks, *free, t_c1], inc=True)
            t = act(W12[:, c, :, :], B.ap(b).rearrange("p (k n) -> p k n", k=2), after=[tok, *bar])
            B.give(b, [t])
        W.done(ci, tok)
        t_w12 = t
        t_fg, t_ug, t_ag = {}, {}, {}

        def f_gate(m, res=None):
            b, ps, tok = res or inp("fgate", m)
            t = act(fg[:, m, :], ps, ACT.Silu, [tok, *bar])
            B.give(b, [t])
            t_fg[m] = t

        def g_gate(m):
            b, ps, tok = inp("ggate", m)
            t = act(ug[:, m, :], ps, ACT.Silu, [tok, *bar])
            B.give(b, [t])
            t_ug[m] = t

        def g_u(m):
            b, ps, tok = inp("gu", m)
            u = tt(ug[:, m, :], ug[:, m, :], ps, ALU.mult, [tok, t_ug[m]])
            B.give(b, [u])
            t_ug[m] = u

        def a_gate(m):
            b, ps, tok = inp("agate", m)
            t = act(ag[:, m, :], ps, ACT.Silu, [tok, *bar])
            B.give(b, [t])
            t_ag[m] = t

        f_gate(0)
        t_vf = {}
        for t in tiles:
            b, free = B.take()
            for m in range(2):
                tok = mm(B.ap(b).rearrange("p (c n) -> p c n", c=2), fi[:, m, t * P:(t + 1) * P], W12[:, :, m, :],
                         m == 0, m == 1, [t_w12, *t_fi, *free], inc=(m == 1))
            t_vf[t] = dcopy(Vf[:, t, :], B.ap(b), [tok, *bar])
            B.give(b, [t_vf[t]])
        f_gate(1)
        for m in range(2):
            b, free = B.take()
            for s in range(2 if l == 0 else 1):
                q = s if l == 0 else 1
                for t in range(2):
                    tk = 2 * q + t
                    o_ = B.ps[:, b * 512 + 256 * s:b * 512 + 256 * s + 256]
                    mm(o_, Vf[:, tk, m * P:(m + 1) * P], C("c256", 256 * t, 256), t == 0, False, [t_vf[tk], *free])
                    tok = mm(o_, Vf[:, tk, 256 + m * P:256 + (m + 1) * P], C("s256", 256 * t, 256), False, t == 1, inc=True)
            t_fg[m] = tt(fg[:, m, :], B.ap(b, N), fg[:, m, :], ALU.mult, [tok, t_fg[m]])
            B.give(b, [t_fg[m]])
        kbar = [PE.last(), *t_vf.values()]

        sqb = S.sq
        b_st, free_st = B.take()
        t_sq = []
        for m in range(2):
            b, ps, tok = inp("cq", m)
            t = act(cq[:, m, :], ps, after=[tok, t_c1, *bar], scale=C("qag", 2 * l + m, 1))
            u = act(sqb[:, m * 512:m * 512 + N], ps, ACT.Square, [tok, *S.sq_rd])
            B.give(b, [t, u])
            t_sq.append(u)
        t_cq = [t]
        if l == 0:
            ckv_res = ckv_take(inp("ckv", 0, True))
        t_ck, u = ckv_res
        for t in tiles:
            for m in range(2):
                j = (t - tiles[0]) * P
                tok = mm(B.ps[:, b_st * 512 + t:b_st * 512 + t + 1], sqb[:, m * 512 + j:m * 512 + j + P],
                         C("ones", 0, 1), m == 0, m == 1, [*t_sq, *free_st], inc=(m == 1))

        gb, tok = lin_tm("w_in", l, ("gvkr",), 288, XH, XL, lambda t: slice(t * P, (t + 1) * P), list(range(4)), 3, ht,
                         cut=lambda t: 0 if t in tiles else 256)
        for t in range(4):
            tk = mm(B.ps[:, b_st * 512 + 4 + t:b_st * 512 + 5 + t], S.acc[:, t * P:(t + 1) * P],
                    C("ones", 0, 1), True, True, [u], inc=(t == 3))
        S.sq_rd = [tk, tk]
        S.acc_rd = [tk]
        S.tmp_rd = [tk] * 4
        st8, s8u, s8w = stat[:, tiles[0]:8], stat[:, 120 + tiles[0]:128], stat[:, 128 + tiles[0]:136]
        t = ts(stat[:, tiles[0]:4], B.ps[:, b_st * 512 + tiles[0]:b_st * 512 + 4], 1.0 / 256, EPS, ALU.mult, ALU.add, [tk, *bar])
        t = ts(stat[:, 4:8], B.ps[:, b_st * 512 + 4:b_st * 512 + 8], 1.0 / 128, EPS, ALU.mult, ALU.add, [tk, *bar])
        B.give(b_st, [t])
        t_stat = rsqrt(st8, s8u, s8w, [t])
        for t in range(4):
            pb = B.ap(gb[t])
            u = act(kr[:, t * 32:(t + 1) * 32], pb[:, 256:288], after=[tok, *bar])
            if t in tiles:
                u = act(gv[:, t * 256:(t + 1) * 256], pb[:, 0:256], after=[tok, *bar])
            B.give(gb[t], [u])
        t_gv = [u]

        rt = {}
        for i, nm in enumerate(("gqr", "gkr")):
            g32 = C(nm, 32 * l, 32)
            tab = S.rtab[:, i * 128:(i + 1) * 128]
            gc = tab[:, 0:64].rearrange("p (t n) -> p t n", t=2)
            gs = tab[:, 64:128].rearrange("p (t a b n) -> p t a b n", t=2, a=2, b=2)
            gr = g32.rearrange("p (a b n) -> p a b n", a=2, b=2)
            sn = C("sin1").rearrange("p (t a b n) -> p t a b n", t=2, a=2, b=2)
            a = tt(gc, C("cos1").rearrange("p (t n) -> p t n", t=2), g32.unsqueeze(1).broadcast_to([P, 2, 32]),
                   ALU.mult, [t_c1, *bar])
            for hf in range(2):
                for t_ in range(2):
                    a = tt(gs[:, t_, :, hf, :], sn[:, t_, :, hf, :], gr[:, :, 1 - hf, :], ALU.mult, [a])
            rt[i] = (tab, g32, a)

        def gv_norm():
            G = gv[:, tiles[0] * 256:1024].rearrange("p (g d) -> p g d", d=64)
            G2 = gsq[:, tiles[0] * 256:1024].rearrange("p (g d) -> p g d", d=64)
            n = 4 * len(tiles)
            mu, va, vu, vw = (stat[:, 16 * i:16 * i + n] for i in (1, 2, 4, 5))
            t = rsum(mu, G, [*t_gv, *bar])
            t = ts(mu, mu, -1.0 / 64, None, ALU.mult, ALU.bypass, [t])
            t = tt(G, G, mu.unsqueeze(2).broadcast_to([P, n, 64]), ALU.add, [t])
            u = act(G2, G, ACT.Square, [t, *bar])
            yield
            u = rsum(va, G2, [u])
            u = ts(va, va, 1.0 / 64, EPS, ALU.mult, ALU.add, [u])
            u = rsqrt(va, vu, vw, [u])
            t = tt(G, G, va.unsqueeze(2).broadcast_to([P, n, 64]), ALU.mult, [t, u])
            S.t_ln = tt(G, G, C("lng", 64 * l, 64).unsqueeze(1).broadcast_to([P, n, 64]), ALU.mult, [t, t_c1])

        gv_rd = [[]]

        def spatial():
            (ws, _), toks, ci = W.get(("g_ws", l, (0, 1, 2, 3), (0, 128)), 512, split=False)
            for m in range(2):
                b, free = B.take()
                for t in tiles:
                    j = t - tiles[0]
                    for h2 in range(2):
                        h = 2 * m + h2
                        tok = mm(B.ps[64 * h2:64 * h2 + 64, b * 512 + j * P:b * 512 + (j + 1) * P],
                                 gv[:, t * 256 + h * 64:t * 256 + h * 64 + 64], ws[:, h * P:(h + 1) * P],
                                 True, True, [S.t_ln, *toks, *free], inc=True)
                go = S.rs[:, 0:N]
                bs = C("bs", (2 * l + m) * P, P).unsqueeze(1).broadcast_to([P, len(tiles), P])
                t = tt(go.rearrange("p (t n) -> p t n", n=P), B.ap(b, N).rearrange("p (t n) -> p t n", n=P), bs, ALU.add,
                       [tok, *S.rs_rd])
                B.give(b, [t])
                t_ug[m] = tt(ug[:, m, :], go, ug[:, m, :], ALU.mult, [t, t_ug[m]])
                S.rs_rd = [t_ug[m]]
            W.done(ci, tok)
            gv_rd[0] = [tok]

        X_free = [[], [], []]
        Q_free = [[], []]
        t_K, t_V, qq, kn = {}, {}, {}, []

        def norm_rope(i, x, z, t0, ready, scaled):
            X, sqq = X3[x], scr[z]
            Xg = X.rearrange("p (g d) -> p g d", d=96)
            ss, su, sw = (stat[:, o_:o_ + 16] for o_ in st_of[x])
            a = act(sqq, X, ACT.Square, [*ready, *gv_rd[0]])
            yield
            a = rsum(ss, sqq.rearrange("p (g d) -> p g d", d=96), [a])
            k = 96.0 if scaled else 1.0
            a = ts(ss, ss, k / 96, EPS * k, ALU.mult, ALU.add, [a])
            a = rsqrt(ss, su, sw, [a])
            a = tt(Xg, Xg, ss.unsqueeze(2).broadcast_to([P, 16, 96]), ALU.mult, [a])
            yield
            tab, g32, tk = rt[i]
            R = Xg[:, :, 64:96]
            if t0 >= 2:
                for y in range(2):
                    Ry = R[:, 8 * y:8 * y + 8, :]
                    R1 = sqq[:, 512 * y:512 * y + 256].rearrange("p (h n) -> p h n", h=8)
                    R2 = sqq[:, 512 * y + 256:512 * y + 512].rearrange("p (h n) -> p h n", h=8)
                    gc = tab[:, 32 * y:32 * y + 32].unsqueeze(1).broadcast_to([P, 8, 32])
                    gs = tab[:, 64 + 32 * y:96 + 32 * y].rearrange("p (a b n) -> p a b n", a=2, b=2)
                    u = tt(R1, Ry, gc, ALU.mult, [a, tk])
                    for ax in range(2):
                        for hf in range(2):
                            v = tt(R2[:, :, 16 * ax + 8 * hf:16 * ax + 8 * hf + 8],
                                   Ry[:, :, 16 * ax + 8 * (1 - hf):16 * ax + 8 * (1 - hf) + 8],
                                   gs[:, ax, hf, :].unsqueeze(1).broadcast_to([P, 8, 8]), ALU.mult, [a, tk])
                    r = tt(Ry, R1, R2, ALU.add, [u, v])
                a = r
            else:
                a = tt(R, R, g32.unsqueeze(1).broadcast_to([P, 16, 32]), ALU.mult, [a])
            qq["r", x] = a

        def heads_T(x, dst, gcol, ready, after):
            for y in range(2):
                for h0 in (0, 4):
                    b, free = B.take()
                    for j in range(4):
                        tok = transpose(B.ps[0:96, b * 512 + j * P:b * 512 + (j + 1) * P],
                                        X3[x][:, y * 768 + (h0 + j) * 96:y * 768 + (h0 + j + 1) * 96], [*ready, *free])
                    src = B.ps[0:96, b * 512:b * 512 + 512].rearrange("p (h n) -> p h n", h=4)
                    if h0:
                        a = act(dst(y, h0), src, after=[tok, *after(y)], scale=gcol)
                    else:
                        d = ts(dst(y, h0), src, gcol, None, ALU.mult, ALU.bypass, [tok, *after(y)])
                    B.give(b, [a if h0 else d])
                yield
            qq["T", x] = [a, d]
            X_free[x] = [tok]
            if x == 1:
                S.sq_rd = [tok, tok]
                S.rs_rd = [tok]
                S.tmp_rd = [tok] * 4

        def kv_pair(p, x, z):
            c = []
            for y in range(2):
                t = 2 * p + y
                b0, f0 = B.take()
                b1, f1 = B.take()
                tk0 = mm(B.ap(b0), ckv[:, t * P:(t + 1) * P], wkv[:, 0:512], True, True, [t_ukv, *f0, t_ck], inc=True)
                tk1 = mm(B.ap(b1), ckv[:, t * P:(t + 1) * P], wkv[:, 512:1024], True, True, [*f1], inc=True)
                Xy = X3[x][:, y * 768:(y + 1) * 768].rearrange("p (h d) -> p h d", h=8)
                a = act(Xy[:, :, 0:64], B.ap(b0).rearrange("p (h d) -> p h d", h=8), after=[tk0, t_stat, *X_free[x], *bar],
                        scale=stat[:, 4 + t:5 + t])
                B.give(b0, [a])
                c += [a, dcopy(Xy[:, :, 64:96], kr[:, t * 32:(t + 1) * 32].unsqueeze(1).broadcast_to([P, 8, 32]),
                               [*t_gv, *X_free[x]])]
                v = ts(V[:, t, :], B.ap(b1), stat[:, 4 + t:5 + t], None, ALU.mult, ALU.bypass, [tk1, S.t_ln, *bar])
                B.give(b1, [v])
                t_V[t] = v
            yield
            yield from norm_rope(1, x, z, 2 * p, c, False)
            kn.append(qq["r", x])
            yield
            yield from heads_T(x, lambda y, h0: K[0:96, h0:h0 + 4, (2 * p + y) * P:(2 * p + y + 1) * P], C("gk", l, 1, 96),
                               [qq["r", x]], lambda y: kbar)
            t_K[2 * p] = t_K[2 * p + 1] = qq["T", x]


        def q_pair(p, x, z):
            c = []
            if x == 1:
                X_free[1] = [*S.sq_rd, *S.rs_rd]
            for y in range(2):
                t = 2 * p + y
                b0, f0 = B.take(2)
                for cc, w in ((0, 512), (512, 256)):
                    for m in range(2):
                        tok = mm(B.ps[:, b0 * 512 + cc:b0 * 512 + cc + w], cq[:, m, t * P - x0:(t + 1) * P - x0],
                                 uq[:, m * 768 + cc:m * 768 + cc + w], m == 0, m == 1, [*f0, t_uq, *t_cq], inc=(m == 1))
                a = act(X3[x][:, y * 768:(y + 1) * 768], B.ap(b0, 768), after=[tok, t_stat, *X_free[x], *bar], scale=stat[:, t:t + 1])
                B.give(b0, [a], 2)
                c.append(a)
            yield
            yield from norm_rope(0, x, z, 2 * p, c, True)
            yield
            Q4 = Q.rearrange("p (y h n) -> p y h n", y=2, h=8)
            yield from heads_T(x, lambda y, h0: Q4[0:96, y, h0:h0 + 4, :], C("gq", l, 1, 96), [qq["r", x]], lambda y: [*Q_free[y], *kn])
            for y in range(2):
                qq[2 * p + y] = (Q4[:, y, :, :], qq["T", x])

        def weave(gen, fill, every=1):
            i = 0
            for _ in gen:
                i += 1
                if i % every == 0 and fill:
                    fill.pop(0)()

        fill = [lambda: g_gate(0), lambda: g_u(0), lambda: g_gate(1), lambda: g_u(1)]
        fill += [lambda m=m: a_gate(m) for m in range(4)]
        weave(gv_norm(), fill)
        kv0 = kv_pair(0, 0, 0)
        next(kv0)
        while len(fill) > 4:
            fill.pop(0)()
        spatial()
        live = [kv0, q_pair(tiles[0] // 2, 1, 1)]
        kv1 = kv_pair(1, 0 if l == 0 else 2, 2)
        if l == 1:
            live.append(kv1)
        while live:
            for g in list(live):
                if next(g, 0) == 0:
                    live.remove(g)
                    if g is kv0 and l == 0:
                        next(kv1)
            if fill:
                fill.pop(0)()
        while fill:
            fill.pop(0)()

        hfree = [PE.last()]
        mixt = {}
        for m in range(2):
            mixt[m] = split_to(hh[:, m, cs], hl[:, m, cs], fg[:, m, :], [t_fg[m], *hfree])
            mixt[2 + m] = split_to(hh[:, 2 + m, cs], hl[:, 2 + m, cs], ug[:, m, :], [t_ug[m], *hfree])
        for k in range(4, 8):
            mixt[k] = []

        P_free = [[DV.last()], [DV.last()], [DV.last()]]
        PT_free = [[], []]
        items = [(t, h) for t in tiles for h in range(8)]
        ob, info = {}, {}

        def partA(i):
            t, h = items[i]
            Qt, tQ = qq[t]
            nk = 2 if t < 2 else 4
            b, free = B.take()
            n = nk * P
            tok = mm(B.ap(b, n), Qt[0:96, h, :], K[0:96, h, 0:n], True, True, [*tQ, *(x for j in range(nk) for x in t_K[j]), *free], inc=True)
            Q_free[t % 2] = [tok]
            z = i % 3
            mx, sm = stat[:, 64 + z:65 + z], stat[:, 68 + z:69 + z]
            a = DV(lambda e: e.tensor_reduce(mx, B.ap(b, n), AX.X, ALU.max, negate=True), [tok, *P_free[z]])
            pb = Pb[:, z * 512:z * 512 + n]
            c = AC(lambda e: e.activation(pb, B.ap(b, n), ACT.Exp, bias=mx, accum_out=sm), [a, *P_free[z]])
            B.give(b, [c])
            info[i] = [nk, z, pb, c, sm]

        def partA2(i):
            nk, z, pb, c, sm = info[i]
            a = DV(lambda e: e.reciprocal(sm, sm), [c])
            a = ts(pb, pb, sm, None, ALU.mult, ALU.bypass, [a])
            info[i].append(a)

        def partB(i):
            nk, z, pb, c, sm, a = info[i]
            b, free = B.take()
            for j in range(nk):
                tok = transpose(B.ps[:, b * 512 + j * P:b * 512 + (j + 1) * P], pb[:, j * P:(j + 1) * P], [a, *free])
            P_free[z] = [tok]
            y = i % 2
            pt = PT[:, y * 512:y * 512 + nk * P]
            u = act(pt, B.ap(b, nk * P), after=[tok, *PT_free[y], *bar])
            B.give(b, [u])
            info[i] += [pt, u]

        def partC(i):
            t, h = items[i]
            nk, z, pt, u = info[i][0], info[i][1], info[i][6], info[i][7]
            if h == 0:
                ob[t] = B.take()
            b, free = ob[t]
            o_ = B.ps[64 * (h % 2):64 * (h % 2) + 64, b * 512 + (h // 2) * P:b * 512 + (h // 2 + 1) * P]
            for j in range(nk):
                tok = mm(o_, V[:, j, h * 64:(h + 1) * 64], pt[:, j * P:(j + 1) * P], j == 0, j == nk - 1,
                         [u, t_V[j], *free], inc=(j == nk - 1))
            PT_free[i % 2] = [tok]
            if h == 7:
                z = t % 2
                oo = S.sq[:, z * 512:z * 512 + 512]
                o3 = oo.rearrange("p (k n) -> p k n", k=4)
                c = slice(t * P, (t + 1) * P)
                a = tt(o3, B.ap(b).rearrange("p (k n) -> p k n", k=4), ag[:, :, t * P - x0:(t + 1) * P - x0], ALU.mult,
                       [tok, *(t_ag[m] for m in range(4)), *AS(S.sq_rd[z])])
                B.give(b, [a])
                r = split_to(hh[:, 4:8, c], hl[:, 4:8, c], o3, [a, *hfree])
                for k in range(4, 8):
                    mixt[k] += r
                S.sq_rd[z] = r[1]

        def AS(t):
            return [t] if t is not None else []

        ni = len(items)
        mods = ((0, 4), (0, 5), (1, 2), (1, 3), (1, 0), (1, 1)) if l == 0 else ((1, 5),)
        fill = both(*(mod_steps(l_, n) for l_, n in mods))
        qx = both(kv1, q_pair(1, 0, 2)) if l == 0 else None
        for i in range(ni + 3):
            if i == 16 and qx is not None:
                for _ in qx:
                    pass
                qx = None
            if i < ni:
                partA(i)
            if 0 <= i - 1 < ni:
                partA2(i - 1)
            if qx is not None and i < 11 and i != 9:
                next(qx, None)
            next(fill, None)
            if 0 <= i - 2 < ni:
                partB(i - 2)
            if 0 <= i - 3 < ni:
                partC(i - 3)
        for _ in fill:
            pass

        mt = lambda k: mixt[k]
        for m in range(KD):
            b, ps, tok = lin_fm("w_out", l, (P * m, P), KD, xh, xl, N, mt)
            for s in range(2):
                if s == 0 and l == 1:
                    continue
                c = slice(256 * s, 256 * s + 256)
                gt, tg = modv(l, 2, m, s)
                pc = slice(256 * s - x0, 256 * s - x0 + 256)
                t = stt(XT[:, m, c], ps[:, pc], gt, XT[:, m, c], ALU.mult, ALU.add, [tok, tg])
            B.give(b, [t])
            if l == 0:
                square_add(XT[:, m, :], m == 0, m % 2, [t])
            else:
                t_x2[m] = split_to(hh[:, m, 0:256], hl[:, m, 0:256], XT[:, m, 256:512], [t, *hfree])
        if l == 0:
            r_ = rstd_steps(TT, D, EPS)
            next(r_)
            for i, _ in enumerate(mod_steps(1, 4)):
                if i == 2:
                    next(r_)
            br, tr = S.rstd

    xc = slice(256, 512)
    bar = barrier()
    t_c2 = AC.dma(lambda e: e.dma_start(S.cst[:, C2_TO:C2_TO + C_N - C2_FROM], S.cpack[:, C2_FROM:C_N]), (S.s_c2, 16), bar)
    X2h, X2l = (lambda k: hh[:, k, 0:256]), (lambda k: hl[:, k, 0:256])
    xt2 = lambda k: t_x2[k]
    o = 0

    def area(n):
        nonlocal o
        a = AF[:, o:o + n]
        o += n
        return a

    Q2 = area(3 * 1024).rearrange("p (g j n) -> p g j n", g=3, j=4)
    K2 = area(3 * 1024).rearrange("p (g j n) -> p g j n", g=3, j=4)
    V2 = area(2 * 1536).rearrange("p (t g n) -> p t g n", t=2, g=3)
    U = area(4 * 286).rearrange("p (m n) -> p m n", m=4)
    CV = area(4 * 256).rearrange("p (m n) -> p m n", m=4)
    Gt = area(16 * 256).rearrange("p (m n) -> p m n", m=16)
    P2 = area(3 * 768)
    rot = P2
    P2T = area(2 * 768)
    st2 = area(16)
    assert o <= S.NAF, o

    t_q2, t_v2 = [], []
    t_u = [None] * 4
    tz = DV(lambda e: e.memset(U[:, :, 0:30], 0.0), bar)
    t_cw = ts(C("convw"), C("convw"), 0.5, None, ALU.mult, ALU.bypass, [t_c2])
    t_cv = [None] * 4
    taps = [(j, 0) for j in range(8)]
    taps += [t for i in range(31) for t in (((i + 8, 0),) if i < 23 else ()) + ((i, 1),)]
    taps += [(j, m) for j in range(31) for m in (2, 3)]

    def conv_taps(n):
        for _ in range(min(n, len(taps))):
            j, m = taps.pop(0)
            w = C("convw", 31 * m + j, 1)
            if j == 0:
                t_cv[m] = ts(CV[:, m, :], U[:, m, 0:256], w, C("convb", m, 1), ALU.mult, ALU.add, [t_u[m], tz, t_cw, *bar])
            else:
                t_cv[m] = stt(CV[:, m, :], U[:, m, j:j + 256], w, CV[:, m, :], ALU.mult, ALU.add, [t_cv[m]])

    for m in range(4):
        b, ps, tok = lin_fm("w_in_2", 0, (4608 + 512 + P * m, P), KD, X2h, X2l, 256, xt2)
        sg = Gt[:, m, :]
        a = act(sg, ps, ACT.Tanh, [tok, *bar], scale=0.5)
        B.give(b, [a])
        b, ps, tok = lin_fm("w_in_2", 0, (4608 + P * m, P), KD, X2h, X2l, 256, xt2)
        u = stt(U[:, m, 30:286], sg, 1.0, ps, ALU.add, ALU.mult, [tok, a, tz])
        B.give(b, [u])
        t_u[m] = u
        if m:
            conv_taps(8)

    rfree = [[], []]
    late = []

    def turn(ps, give, w, g, t, tok):
        z = t
        r1 = rot[:, z * 1024:z * 1024 + 512]
        r2 = rot[:, z * 1024 + 512:z * 1024 + 1024]
        p4 = ps.rearrange("p (h a n) -> p h a n", h=8, a=2)
        q4 = r2.rearrange("p (h a n) -> p h a n", h=8, a=2)
        a = tt(r1.rearrange("p (h n) -> p h n", n=32), ps.rearrange("p (h n) -> p h n", n=32),
               C("cos2", 32 * t, 32).unsqueeze(1).broadcast_to([P, 16, 32]), ALU.mult, [tok, t_c2, *rfree[z], *bar])
        tt(q4[:, :, 0, :], p4[:, :, 1, :], C("nsin2", 32 * t, 32).unsqueeze(1).broadcast_to([P, 8, 32]), ALU.mult, [])
        u = tt(q4[:, :, 1, :], p4[:, :, 0, :], C("sin2", 32 * t, 32).unsqueeze(1).broadcast_to([P, 8, 32]), ALU.mult, [])
        B.give(give, [u])
        a = tt(r1, r1, r2, ALU.add, [a, u])

        def finish():
            b, free = B.take()
            for j in range(4):
                tk = transpose(B.ps[:, b * 512 + j * P:b * 512 + (j + 1) * P], r1[:, j * P:(j + 1) * P], [a, *free])
            rfree[z] = [tk]
            dst = (Q2, K2)[w][:, g, :, t * P:(t + 1) * P]
            c = act(dst, B.ap(b).rearrange("p (j n) -> p j n", j=4), after=[tk, *bar])
            B.give(b, [c])
            t_q2[:] = [c]
        late.append(finish)

    for g in range(3):
        for w in (0, 1, 2):
            bb, tok = lin_tm("w_in_2", 0, g * 1536 + w * 512, 512, X2h, X2l, lambda t: slice(t * P, (t + 1) * P), [0, 1], 2, xt2,
                             beside=lambda: conv_taps(2))
            while late:
                late.pop(0)()
            for t in range(2):
                ps = B.ap(bb[t])
                if w == 2:
                    a = act(V2[:, t, g, :], ps, after=[tok, *bar])
                    B.give(bb[t], [a])
                    t_v2 = [a]
                else:
                    turn(ps, bb[t], w, g, t, tok)
    while late:
        late.pop(0)()

    t_g = {}

    def gate(m):
        b, ps, tok = lin_fm("w_in_2", 0, (4608 + 1024 + P * m, P), KD, X2h, X2l, 256, xt2)
        a = act(Gt[:, m, :], ps, ACT.Tanh, [tok, *t_u], scale=0.5)
        B.give(b, [a])
        t_g[m] = a

    ch, cl = S.ch, S.cl

    def ln(src, nt, nfeat, toks, eps):
        b, free = B.take()
        tok = mm(B.ap(b, 256), C("ones"), S.acc[:, 0:256], True, True, [S.acc_t, *free], inc=True)
        S.acc_rd = [tok]
        a = act(S.mean[:, :], B.ap(b, 256), after=[tok, *S.mean_rd], scale=1.0 / nfeat)
        B.give(b, [a])
        yield
        u = []
        for k in range(nt):
            u.append(tt(src(k), src(k), S.mean[:, :], ALU.subtract, [a, *toks(k)]))
            if k >= 1:
                square_add(src(k - 1), k == 1, (k - 1) % 2, [u[k - 1]])
        S.mean_rd = [u[-1]]
        square_add(src(nt - 1), nt == 1, (nt - 1) % 2, [u[-1]])
        yield
        S.ln_out = rstd_wide(256, nfeat, eps)

    t_ch = []

    def conv_norm():
        for k in range(4):
            acc_add(CV[:, k, :], k == 0, [t_cv[k]])
        yield
        yield from ln(lambda k: CV[:, k, :], 4, 512, lambda k: [t_cv[k]], LN_EPS)
        b, tr = S.ln_out
        yield
        th = P2T[:, 1280:1536]
        for m in range(4):
            a = stt(CV[:, m, :], CV[:, m, :], C("cg", m, 1), B.ap(b, 256), ALU.mult, ALU.mult, [tr])
            if m == 3:
                B.give(b, [a])
            a = ts(CV[:, m, :], CV[:, m, :], C("cb", m, 1), None, ALU.add, ALU.bypass, [a])
            th = U[:, m, 0:256]
            c = act(th, CV[:, m, :], ACT.Tanh, [a, t_cv[m]], scale=0.5)
            a = stt(CV[:, m, :], th, 1.0, CV[:, m, :], ALU.add, ALU.mult, [a, c])
            t = act(ch[:, m, :], CV[:, m, :], after=[a, *bar], scale=0.5)
            u = stt(cl[:, m, :], CV[:, m, :], 0.5, ch[:, m, :], ALU.mult, ALU.subtract, [a, t])
            t_ch.append([t, u])
            yield

    oh, ol = S.oh, S.ol
    t_o = []
    items = [(qb, h) for qb in range(2) for h in range(8)]
    info = {}
    Pf, PTf = [[*rfree[0], *rfree[1]] for _ in range(3)], [[], []]
    ob = {}

    def A(i):
        qb, h = items[i]
        nb = qb + 1
        r = slice(64 * (h % 2), 64 * (h % 2) + 64)
        w = nb * P
        b, free = B.take(2)
        ps = B.ap(b, 3 * w)
        for g in range(3):
            tok = mm(ps[:, g * w:(g + 1) * w], Q2[r, g, h // 2, qb * P:(qb + 1) * P], K2[r, g, h // 2, 0:w],
                     True, True, [*t_q2, *free], inc=(g == 2))
        z = i % 3
        mx, sm = st2[:, z:z + 1], st2[:, 4 + z:5 + z]
        pb = P2[:, z * 768:z * 768 + 3 * w]
        mk = C("mask1").rearrange("p (g n) -> p g n", g=3)[:, :, (0 if qb else 128):256]
        p3, s3 = pb.rearrange("p (g n) -> p g n", g=3), ps.rearrange("p (g n) -> p g n", g=3)
        a = DV(lambda e: e.tensor_tensor_reduce(p3, s3, mk, 1.0, -3.0e38, ALU.add, ALU.max, mx), [tok, *Pf[z], *bar])
        B.give(b, [a], 2)
        a = ts(mx, mx, -0.125, None, ALU.mult, ALU.bypass, [a])
        c = AC(lambda e: e.activation(pb, pb, ACT.Exp, bias=mx, scale=0.125, accum_out=sm), [a])
        info[i] = [nb, z, pb, sm, c]

    def A2(i):
        nb, z, pb, sm, c = info[i]
        a = DV(lambda e: e.reciprocal(sm, sm), [c])
        info[i].append(ts(pb, pb, sm, None, ALU.mult, ALU.bypass, [a]))

    def Bp(i):
        nb, z, pb, sm, c, a = info[i]
        n = 3 * nb
        b, free = B.take(2)
        for j in range(n):
            tok = transpose(B.ps[:, b * 512 + j * P:b * 512 + (j + 1) * P], pb[:, j * P:(j + 1) * P], [a, *free])
        Pf[z] = [tok]
        y = i % 2
        pt = P2T[:, y * 768:y * 768 + n * P]
        u = act(pt, B.ap(b, n * P), after=[tok, *PTf[y], *bar])
        B.give(b, [u], 2)
        info[i] += [pt, u]

    def Cp(i):
        qb, h = items[i]
        nb, z, pt, u = info[i][0], info[i][1], info[i][6], info[i][7]
        if h == 0:
            ob[qb] = B.take()
        b, free = ob[qb]
        o_ = B.ps[64 * (h % 2):64 * (h % 2) + 64, b * 512 + (h // 2) * P:b * 512 + (h // 2 + 1) * P]
        n = 3 * nb
        for j in range(n):
            tok = mm(o_, V2[:, j % nb, j // nb, h * 64:(h + 1) * 64], pt[:, j * P:(j + 1) * P], j == 0, j == n - 1,
                     [u, *t_v2, *free], inc=(j == n - 1))
        PTf[i % 2] = [tok]
        if h == 7:
            o3 = B.ap(b).rearrange("p (k n) -> p k n", k=4)
            c = slice(qb * P, (qb + 1) * P)
            r = split_to(oh[:, :, c], ol[:, :, c], o3, [tok, *bar])
            B.give(b, r)
            t_o.extend(r)

    t_m = [None] * KD
    conv_gen = conv_norm()

    def conv_out(m):
        b, ps, tok = lin_fm("w_conv_out_2", 0, (P * m, P), 4, lambda k: ch[:, k, :], lambda k: cl[:, k, :], 256, lambda k: t_ch[k])
        t_m[m] = stt(Gt[:, 8 + m, :], Gt[:, 8 + m, :], 1.0, ps, ALU.add, ALU.mult, [tok, t_g[8 + m]])
        B.give(b, [t_m[m]])

    fill = [lambda m=m: gate(m) for m in (*range(8, 16), *range(8))] + [lambda m=m: conv_out(m) for m in range(8)]
    nf = len(fill)
    for i in range(16 + 3):
        conv_taps(7)
        if i < 16:
            A(i)
        if 0 <= i - 1 < 16:
            A2(i - 1)
        if not taps:
            next(conv_gen, None)
        for _ in range(1 if i % 3 or i < 3 else 2):
            if fill and not (i > 17):
                fill.pop(0)()
        if 0 <= i - 2 < 16:
            Bp(i - 2)
        if 0 <= i - 3 < 16:
            Cp(i - 3)
    for _ in conv_gen:
        pass
    while fill:
        fill.pop(0)()

    bar2 = barrier()
    t_h2 = []
    for m in range(KD):
        b, ps, tok = lin_fm("w_attn_out_2", 0, (P * m, P), 4, lambda k: oh[:, k, :], lambda k: ol[:, k, :], 256, lambda k: t_o)
        a = stt(Gt[:, m, :], Gt[:, m, :], 1.0, ps, ALU.add, ALU.mult, [tok, t_g[m]])
        B.give(b, [a])
        a = tt(Gt[:, m, :], Gt[:, m, :], Gt[:, 8 + m, :], ALU.add, [a, t_m[m]])
        t = act(hh[:, m, 0:256], Gt[:, m, :], after=[a, *bar2], scale=0.5)
        u = stt(hl[:, m, 0:256], Gt[:, m, :], 0.5, hh[:, m, 0:256], ALU.mult, ALU.subtract, [a, t])
        t_h2.append([t, u])

    t_r = []
    for m in range(KD):
        b, ps, tok = lin_fm("w_o_2", 0, (P * m, P), KD, X2h, X2l, 256, lambda k: t_h2[k])
        t_r.append(stt(XT[:, m, xc], XT[:, m, xc], ALPHA, ps, ALU.mult, ALU.add, [tok]))
        B.give(b, [t_r[-1]])
        acc_add(XT[:, m, xc], m == 0, [t_r[-1]])
    for _ in ln(lambda k: XT[:, k, xc], KD, D, lambda k: [t_r[k]], LN_EPS):
        pass
    b, tr = S.ln_out
    bar3 = barrier()
    t_x3, t_xt = [], []
    for k in range(KD):
        tmp = S.sq[:, (k % 4) * 256:(k % 4) * 256 + 256]
        a = stt(tmp, XT[:, k, xc], C("l1g", k, 1), B.ap(b, 256), ALU.mult, ALU.mult,
                [tr, *bar3, *([t_x3[k - 4][1], t_xt[k - 4]] if k >= 4 else [])])
        t = act(hh[:, k, 0:256], tmp, ACT.Identity, [a], bias=C("l1b", k, 1))
        if k:
            t_x3.append([tp, stt(hl[:, k - 1, 0:256], tmpp, C("l1b", k - 1, 1), hh[:, k - 1, 0:256], ALU.add, ALU.subtract, [tp])])
            t_xt.append(act(XT[:, k - 1, xc], tmpp, ACT.Identity, [ap], bias=C("l1b", k - 1, 1)))
        ap, tp, tmpp = a, t, tmp
    k = KD
    t_x3.append([tp, stt(hl[:, k - 1, 0:256], tmpp, C("l1b", k - 1, 1), hh[:, k - 1, 0:256], ALU.add, ALU.subtract, [tp])])
    t_xt.append(act(XT[:, k - 1, xc], tmpp, ACT.Identity, [ap], bias=C("l1b", k - 1, 1)))
    B.give(b, [ap])
    S.sq_rd = [t_x3[-1][1], t_xt[-1]]

    HK = KF // 2
    fh, fl = S.fh, S.fl
    toks_d = None
    sgs = [AF[:, 0:256], AF[:, 256:512]]
    hs = [AF[:, 512:768], AF[:, 768:1024]]
    s_rd = [list(bar3), list(bar3)]
    h_rd = [list(bar3), list(bar3)]
    t_d = [None] * KD
    t_r = list(t_xt)
    for half in range(2):
        t_f = {}
        for f in range(HK):
            m = half * HK + f
            z = f % 2
            b, ps, tok = lin_fm("w_ffn_gate_2", 0, (P * m, P), KD, X2h, X2l, 256, lambda k: t_x3[k])
            a = act(sgs[z], ps, ACT.Silu, [tok, *s_rd[z]])
            B.give(b, [a])
            b, ps, tok = lin_fm("w_ffn_up_2", 0, (P * m, P), KD, X2h, X2l, 256, lambda k: t_x3[k])
            u = tt(hs[z], sgs[z], ps, ALU.mult, [tok, a, *h_rd[z]])
            B.give(b, [u])
            s_rd[z] = [u]
            t_f[f] = split_to(fh[:, f, :], fl[:, f, :], hs[z], [u, toks_d])
            h_rd[z] = t_f[f]
        kk = list(range(half * HK, (half + 1) * HK))
        for m in range(KD):
            b, ps, t_d = lin_fm("w_ffn_down_2", 0, (P * m, P), None, lambda k: fh[:, k - half * HK, :],
                                lambda k: fl[:, k - half * HK, :], 256, lambda k: t_f[k - half * HK], kk=kk)
            t_r[m] = stt(XT[:, m, xc], XT[:, m, xc], 1.0 if half else ALPHA, ps, ALU.mult, ALU.add, [t_d, t_r[m]])
            B.give(b, [t_r[m]])
            if half:
                acc_add(XT[:, m, xc], m == 0, [t_r[m]])
        toks_d = t_d
    for _ in ln(lambda k: XT[:, k, xc], KD, D, lambda k: [t_r[k]], LN_EPS):
        pass
    b, tr = S.ln_out
    outs = S.out.rearrange("(k p) n -> p k n", p=P)
    for k in range(KD):
        a = stt(XT[:, k, xc], XT[:, k, xc], C("l2g", k, 1), B.ap(b, 256), ALU.mult, ALU.mult, [tr])
        a = act(XT[:, k, xc], XT[:, k, xc], ACT.Identity, [a], bias=C("l2b", k, 1))
        SP.dma(lambda e, k=k: e.dma_start(outs[:, k, :], XT[:, k, xc]), (S.s_out, 16 * (k + 1)), [a])
    SP.wait([(S.s_out, 16 * KD)])
    return W.seq


def build(nc, cpack, xin, wpack, wuq, wukv, out):
    with ExitStack() as ctx:
        S = State()

        def sb(name, shape, dt=F32):
            return ctx.enter_context(nc.sbuf_tensor(name, shape, dt))

        def sem(name):
            return ctx.enter_context(nc.semaphore(name))

        S.cpack, S.xin, S.wpack, S.wuq, S.wukv, S.out = cpack, xin, wpack, wuq, wukv, out
        S.NAF = 19400
        S.cst = sb("cst", [P, C_SB])
        S.XT = sb("XT", [P, KD, TT])
        S.hh = sb("hh", [P, KD, TT], F32R)
        S.hl = sb("hl", [P, KD, TT], F32R)
        S.raw = sb("raw", [P, NRAW * CH])
        S.whi = sb("whi", [P, NHL * CH], F32R)
        S.wlo = sb("wlo", [P, NHL * CH], F32R)
        HB = KF // 2
        S.fh = S.hh[:, :, 256:512]
        S.xr = sb("xr", [P, 2 * 3 * 256], F32R)
        S.AF = sb("AF", [P, S.NAF])
        S.wk = sb("wk", [P, 1536])
        S.sq, S.rs = S.wk[:, 0:1024], S.wk[:, 1024:1536]
        S.acc = sb("acc", [P, 512])
        S.mod = sb("mod", [P, 96])
        S.modrow = sb("modrow", [4, 512])
        S.nrm = sb("nrm", [P, 12])
        S.mean = sb("mean", [P, 256])
        S.uq = sb("uq", [P, 1536])
        S.c32 = sb("c32", [P, 16])
        S.c4 = sb("c4", [P, 32], F32R)
        S.rtab = sb("rtab", [P, 256])
        S.ps = ctx.enter_context(nc.psum_tensor("ps", [P, 8 * 512], F32))

        class Hidden:

            def __init__(self, h, off):
                self.h, self.off = h, off

            def __getitem__(self, key):
                _, k, _ = key
                if k < 8:
                    return self.h[:, k, 256:512]
                o = self.off + (k - 8) * 256
                return S.xr[:, o:o + 256]

        S.fh, S.fl = Hidden(S.hh, 0), Hidden(S.hl, 768)
        S.ch, S.cl = S.hh[:, 0:4, 256:512], S.hl[:, 0:4, 256:512]
        S.oh, S.ol = S.hh[:, 4:8, 256:512], S.hl[:, 4:8, 256:512]

        S.s_pe, S.s_act, S.s_dve = sem("s_pe"), sem("s_act"), sem("s_dve")
        S.s_raw = [sem(f"s_raw{i}") for i in range(NRAW)]
        S.s_uq, S.s_c0, S.s_c1, S.s_c2, S.s_x, S.s_out = sem("s_uq"), sem("s_c0"), sem("s_c1"), sem("s_c2"), sem("s_x"), sem("s_out")

        plan = emit(S, None)
        assert sum(P * n for _, n, _ in plan) == WTOTAL, sum(n for _, n, _ in plan)
        emit(S, plan)

        block = ctx.enter_context(nc.Block())

        @block.sync
        def _(e):
            S.SP.run(e)

        @block.gpsimd
        def _(e):
            S.GP.run(e)

        @block.scalar
        def _(e):
            S.ACT.run(e)

        @block.vector
        def _(e):
            S.DVE.run(e)

        @block.tensor
        def _(e):
            S.PE.run(e)
    return plan


def tables():
    f32 = np.float32
    c = {}
    i = np.arange(256)
    a = 2 * np.pi * np.outer(i, i) / 256
    c["c256"] = (np.cos(a) / 128).astype(f32).reshape(2, 128, 256).transpose(1, 0, 2)
    c["s256"] = (-np.sin(a) / 128).astype(f32).reshape(2, 128, 256).transpose(1, 0, 2)
    j = np.arange(64)
    b = 2 * np.pi * np.outer(j, j) / 64
    for nm, m in (("c64", np.cos(b)), ("s64", np.sin(b))):
        z = np.zeros((128, 128), f32)
        z[:64, :64] = m
        z[64:, 64:] = m
        c[nm] = z
    c["ones"] = np.ones((128, 128), f32)
    c["ident"] = np.eye(128, dtype=f32)
    half = 16
    inv = (f32(10000.0) ** (-np.arange(0, half, 2, dtype=f32) / f32(half))).astype(f32)
    row = np.repeat(np.arange(4, dtype=f32), 64)
    col = np.tile(np.arange(64, dtype=f32), 4)
    ar, ac = (row[:, None] * inv[None]).astype(f32), (col[:, None] * inv[None]).astype(f32)
    ang = np.concatenate([ar, ar, ac, ac], -1)
    sgn = np.tile(np.repeat(np.array([-1, 1], f32), 8), 2)
    c["cos1"] = np.cos(ang).astype(f32).reshape(2, 128, 32).transpose(1, 0, 2)
    c["sin1"] = (np.sin(ang).astype(f32) * sgn).reshape(2, 128, 32).transpose(1, 0, 2)
    inv2 = (1.0 / (f32(10000.0) ** (np.arange(0, 64, 2, dtype=f32) / f32(64)))).astype(f32)
    ang2 = (np.arange(256, dtype=f32)[:, None] * inv2[None]).astype(f32)
    c["cos2"] = np.cos(ang2).astype(f32).reshape(2, 128, 32).transpose(1, 0, 2)
    c["sin2"] = np.sin(ang2).astype(f32).reshape(2, 128, 32).transpose(1, 0, 2)
    c["nsin2"] = -c["sin2"]
    t, s = np.arange(256)[:, None], np.arange(256)[None, :]
    m = []
    for win, dil in ((128, 1), (512, 4), (2048, 16)):
        ok = (t >= s) & ((t - s) % dil == 0) & ((t - s) <= win)
        m.append(np.where(ok, 0.0, NEG).astype(f32))
    c["mask1"] = np.stack([x[128:, :] for x in m], 1)
    e = np.zeros((128, 4), f32)
    e[:, 0], e[:, 1] = EPS, LN_EPS
    c["eps"] = e
    z = np.zeros((128, 2), f32)
    z[0, 0] = z[1, 1] = z[2, 0] = z[3, 1] = 1.0
    c["sel"] = z
    return c


def kernel(**inputs):
    import concourse.bacc as _bacc
    from concourse.bass_utils import run_bass_kernel_spmd as _run

    I = {k: np.asarray(v) for k, v in inputs.items()}
    f32 = np.float32

    nc = _bacc.Bacc("TRN2", target_bir_lowering=False, num_devices=1)
    ci = nc.dram_tensor("cpack", (P, C_N), F32, kind="ExternalInput").ap()
    xi = nc.dram_tensor("xin", (P, KD * TT), F32, kind="ExternalInput").ap()
    wi = nc.dram_tensor("wpack", (WTOTAL,), F32, kind="ExternalInput").ap()
    ui = nc.dram_tensor("wuq", (2, P, 1536), F32, kind="ExternalInput").ap()
    vi = nc.dram_tensor("wukv", (2, P, 1024), F32, kind="ExternalInput").ap()
    oo = nc.dram_tensor("out", (D, T), F32, kind="ExternalOutput").ap()
    plan = build(nc, ci, xi, wi, ui, vi, oo)

    def cols(v, n):
        return v.reshape(n, P).T

    def rows(v):
        return np.broadcast_to(v.reshape(1, -1), (P, v.size))

    c = tables()
    c["cvec"] = np.stack([cols(I["c_ctx"], 8), cols(I["c"][0], 8)], 2)
    c["bmod"] = np.concatenate([cols(I["b_mod"][l], 24) for l in range(2)], 1)
    c["ng"] = np.concatenate([cols(I["norm_g"][l], 8) for l in range(2)], 1)
    c["qag"] = np.concatenate([cols(I["q_a_g"][l], 2) for l in range(2)], 1)
    c["kvag"] = np.concatenate([cols(I["kv_a_g"][l], 1) for l in range(2)], 1)
    for nm, src in (("gq", "q_norm_g"), ("gk", "k_norm_g")):
        z = np.ones((P, 2), f32)
        z[:64, :] = I[src][:, :64].T
        c[nm] = z
        c[nm + "r"] = np.concatenate([rows(I[src][l, 64:]) for l in range(2)], 1)
    c["lng"] = np.concatenate([rows(I["g_ln_g"][l]) for l in range(2)], 1)
    c["bs"] = np.stack([np.repeat(I["g_bs"][l, 2 * m:2 * m + 2], 64, 0) for l in range(2) for m in range(2)], 1)
    c["convw"] = I["conv_w_2"][0].T.reshape(4, P, 31).transpose(1, 0, 2)
    c["convb"] = cols(I["conv_b_2"][0], 4)
    c["cg"], c["cb"] = cols(I["conv_ln_g_2"][0], 4), cols(I["conv_ln_b_2"][0], 4)
    c["l1g"], c["l1b"] = cols(I["ln1_g_2"][0], 8), cols(I["ln1_b_2"][0], 8)
    c["l2g"], c["l2b"] = cols(I["ln2_g_2"][0], 8), cols(I["ln2_b_2"][0], 8)
    cpack = np.zeros((P, C_N), f32)
    for nm, (off, n) in C_AT.items():
        cpack[:, off:off + n] = np.asarray(c[nm]).reshape(P, n)

    xin = np.concatenate([I["ctx"][0].T, I["x"][0].T], 1).reshape(KD, P, TT).transpose(1, 0, 2).reshape(P, KD * TT)

    kvc = np.concatenate([np.arange(h * 128, h * 128 + 64) for h in range(8)] + [np.arange(h * 128 + 64, h * 128 + 128) for h in range(8)])
    gvkr = np.concatenate([np.arange(768, 1024), np.arange(1664, 1696)])
    wpack = np.empty(WTOTAL, f32)
    at = 0
    for (name, l, ks, cc), n, _ in plan:
        if name == "g_ws":
            blk = I[name][l].transpose(2, 0, 1)
        else:
            w = I[name][l]
            blk = w.reshape(-1, P, w.shape[1])[ks[0]:ks[-1] + 1]
            if cc[0] == ("gvkr",):
                blk = blk[:, :, gvkr]
            else:
                blk = blk[:, :, cc[0]:cc[0] + cc[1]]
            blk = blk.transpose(1, 0, 2)
        wpack[at:at + P * n] = blk.reshape(-1)
        at += P * n
    assert at == WTOTAL

    r = _run(nc, [{"cpack": cpack, "xin": np.ascontiguousarray(xin), "wpack": wpack,
                    "wuq": np.ascontiguousarray(I["w_uq"].reshape(2, 2, P, 768).transpose(0, 2, 1, 3).reshape(2, P, 1536)),
                    "wukv": np.ascontiguousarray(I["w_ukv"][:, :, kvc])}], core_ids=[0])
    y = r.results[0]["out"]
    return np.ascontiguousarray(y.T).reshape(1, T, D)
```
